# Optimizing a Trainium2 kernel written in Bass

```python
import math
import jax, jax.numpy as jnp
from jax import lax
import numpy as np

D_MODEL = 1024
BATCH = 1
SEQ = 512
DEPTH = 4

N_MIXERS = 4
EPS = 1e-6
CONV_WIDTH = 1024
CONV_K = 3
FOX_HEADS = 8
FOX_HEAD_DIM = 128
FOX_WIDTH = FOX_HEADS * FOX_HEAD_DIM
Q_BLOCK = 128
GDN_HEADS = 8
GDN_HEAD_DIM = 128
GDN_WIDTH = GDN_HEADS * GDN_HEAD_DIM
GDN_CONV_K = 4
GDN_CHUNK = 64
SWA_HEADS = 16
SWA_KV_HEADS = 4
SWA_GROUP = SWA_HEADS // SWA_KV_HEADS
SWA_HEAD_DIM = 64
SWA_WIDTH = SWA_HEADS * SWA_HEAD_DIM
SWA_KV_WIDTH = SWA_KV_HEADS * SWA_HEAD_DIM
WINDOW = 128
ROPE_THETA = 10000.0

N_CONV_LAYERS = (DEPTH + 3) // 4
N_FOX_LAYERS = (DEPTH + 2) // 4
N_GDN_LAYERS = (DEPTH + 1) // 4
N_SWA_LAYERS = DEPTH // 4


def rms_norm(x, w):
    x32 = x.astype(jnp.float32)
    y = x32 * lax.rsqrt(jnp.mean(x32 * x32, axis=-1, keepdims=True) + EPS)
    return (y * w.astype(jnp.float32)).astype(x.dtype)

def causal_conv(u, w):
    K = w.shape[0]
    S = u.shape[1]
    up = jnp.pad(u, ((0, 0), (K - 1, 0), (0, 0)))
    out = up[:, 0:S] * w[0]
    for k in range(1, K):
        out = out + up[:, k:k + S] * w[k]
    return out

def rope(x, positions):
    d = x.shape[-1]
    half = d // 2
    inv_freq = ROPE_THETA ** (-jnp.arange(half, dtype=jnp.float32) / half)
    ang = positions.astype(jnp.float32)[..., None] * inv_freq
    cos = jnp.cos(ang)[:, :, None, :]
    sin = jnp.sin(ang)[:, :, None, :]
    x32 = x.astype(jnp.float32)
    x1, x2 = x32[..., :half], x32[..., half:]
    return jnp.concatenate([x1 * cos - x2 * sin, x2 * cos + x1 * sin], axis=-1).astype(x.dtype)

def conv_mixer(h, w_in, w_conv, w_out):
    proj = h @ w_in
    b_gate, c_gate, v, z = jnp.split(proj, 4, axis=-1)
    y = b_gate * causal_conv(c_gate * v, w_conv)
    return (y * jax.nn.silu(z)) @ w_out

def fox_mixer(h, w_in, b_f, w_out):
    B_, S, _ = h.shape
    H, d = FOX_HEADS, FOX_HEAD_DIM
    proj = h @ w_in
    q, k, v, z, f_logit = jnp.split(proj, [FOX_WIDTH, 2 * FOX_WIDTH, 3 * FOX_WIDTH, 4 * FOX_WIDTH], axis=-1)
    q = q.reshape(B_, S, H, d)
    k = k.reshape(B_, S, H, d)
    v = v.reshape(B_, S, H, d)
    log_f = jax.nn.log_sigmoid((f_logit + b_f).astype(jnp.float32))
    c = jnp.cumsum(log_f, axis=1)
    c_keys = c.transpose(0, 2, 1)
    nblk = S // Q_BLOCK
    q_blocks = q.reshape(B_, nblk, Q_BLOCK, H, d).transpose(1, 0, 2, 3, 4)
    c_blocks = c.reshape(B_, nblk, Q_BLOCK, H).transpose(1, 0, 3, 2)
    scale = 1.0 / math.sqrt(d)
    k_pos = jnp.arange(S)

    def block(args):
        i, q_i, c_i = args
        s = jnp.einsum('bqhd,bkhd->bhqk', q_i, k).astype(jnp.float32) * scale
        decay = c_i[..., :, None] - c_keys[:, :, None, :]
        q_pos = i * Q_BLOCK + jnp.arange(Q_BLOCK)
        mask = k_pos[None, :] <= q_pos[:, None]
        logits = jnp.where(mask, s + decay, -jnp.inf)
        p = jax.nn.softmax(logits, axis=-1)
        return jnp.einsum('bhqk,bkhd->bqhd', p.astype(v.dtype), v)

    o = lax.map(block, (jnp.arange(nblk), q_blocks, c_blocks))
    o = o.transpose(1, 0, 2, 3, 4).reshape(B_, S, FOX_WIDTH)
    return (o * jax.nn.silu(z)) @ w_out

def chunk_gated_delta(q, k, v, g, beta):
    B_, S, H, dk = q.shape
    dv = v.shape[-1]
    C = GDN_CHUNK
    n = S // C
    f32 = jnp.float32

    def chunks(t):
        return t.astype(f32).reshape(B_, n, C, H, -1).transpose(0, 3, 1, 2, 4)

    q, k, v = chunks(q), chunks(k), chunks(v)
    beta = beta.astype(f32).reshape(B_, n, C, H).transpose(0, 3, 1, 2)
    g_cum = jnp.cumsum(g.astype(f32).reshape(B_, n, C, H).transpose(0, 3, 1, 2), axis=-1)
    k_beta = k * beta[..., None]
    v_beta = v * beta[..., None]
    idx = jnp.arange(C)
    causal = idx[:, None] >= idx[None, :]
    strict = idx[:, None] > idx[None, :]
    diff = g_cum[..., :, None] - g_cum[..., None, :]
    decay = jnp.where(causal, jnp.exp(jnp.where(causal, diff, 0.0)), 0.0)
    L = jnp.where(strict, jnp.einsum('bhnid,bhnjd->bhnij', k_beta, k) * decay, 0.0)
    eye = jnp.eye(C, dtype=f32)
    T = lax.linalg.triangular_solve(eye + L, jnp.broadcast_to(eye, L.shape), left_side=True, lower=True, unit_diagonal=True)
    u = T @ v_beta
    w = T @ (k_beta * jnp.exp(g_cum)[..., None])
    qk = jnp.where(causal, jnp.einsum('bhnid,bhnjd->bhnij', q, k) * decay, 0.0)
    g_last = g_cum[..., -1]
    k_dec = k * jnp.exp(g_last[..., None] - g_cum)[..., None]
    q_dec = q * jnp.exp(g_cum)[..., None]

    def to_scan(t):
        return jnp.moveaxis(t, 2, 0)

    def step(state, xs):
        qd, kd, u_c, w_c, qk_c, gl = xs
        v_new = u_c - w_c @ state
        o = qd @ state + qk_c @ v_new
        state = state * jnp.exp(gl)[..., None, None] + jnp.einsum('bhck,bhcv->bhkv', kd, v_new)
        return state, o

    state0 = jnp.zeros((B_, H, dk, dv), f32)
    xs = (to_scan(q_dec), to_scan(k_dec), to_scan(u), to_scan(w), to_scan(qk), to_scan(g_last))
    _, o = lax.scan(step, state0, xs)
    return o.transpose(1, 0, 3, 2, 4).reshape(B_, S, H, dv)

def gdn_mixer(h, w_in, w_conv, a_log, dt_bias, w_onorm, w_out):
    B_, S, _ = h.shape
    H, d = GDN_HEADS, GDN_HEAD_DIM
    proj = h @ w_in
    qkv, z, beta_logit, a_logit = jnp.split(proj, [3 * GDN_WIDTH, 4 * GDN_WIDTH, 4 * GDN_WIDTH + H], axis=-1)
    qkv = jax.nn.silu(causal_conv(qkv, w_conv))
    q, k, v = jnp.split(qkv, 3, axis=-1)
    q = q.reshape(B_, S, H, d).astype(jnp.float32)
    k = k.reshape(B_, S, H, d).astype(jnp.float32)
    v = v.reshape(B_, S, H, d)
    q = q * lax.rsqrt(jnp.sum(q * q, axis=-1, keepdims=True) + EPS) * (1.0 / math.sqrt(d))
    k = k * lax.rsqrt(jnp.sum(k * k, axis=-1, keepdims=True) + EPS)
    beta = jax.nn.sigmoid(beta_logit.astype(jnp.float32))
    g = -jnp.exp(a_log.astype(jnp.float32)) * jax.nn.softplus(a_logit.astype(jnp.float32) + dt_bias.astype(jnp.float32))
    o = chunk_gated_delta(q, k, v, g, beta)
    o = o * lax.rsqrt(jnp.mean(o * o, axis=-1, keepdims=True) + EPS) * w_onorm.astype(jnp.float32)
    o = o.reshape(B_, S, GDN_WIDTH).astype(h.dtype)
    return (o * jax.nn.silu(z)) @ w_out

def swa_mixer(h, positions, w_in, sinks, w_out):
    B_, S, _ = h.shape
    Hk, G, d = SWA_KV_HEADS, SWA_GROUP, SWA_HEAD_DIM
    proj = h @ w_in
    q, k, v, z = jnp.split(proj, [SWA_WIDTH, SWA_WIDTH + SWA_KV_WIDTH, SWA_WIDTH + 2 * SWA_KV_WIDTH], axis=-1)
    q = rope(q.reshape(B_, S, SWA_HEADS, d), positions)
    k = rope(k.reshape(B_, S, Hk, d), positions)
    v = v.reshape(B_, S, Hk, d)
    W = WINDOW
    nblk = S // W
    qb = q.reshape(B_, nblk, W, Hk, G, d)

    def band(t):
        tb = t.reshape(B_, nblk, W, Hk, d)
        prev = jnp.pad(tb, ((0, 0), (1, 0), (0, 0), (0, 0), (0, 0)))[:, :-1]
        return jnp.concatenate([prev, tb], axis=2)

    kk, vv = band(k), band(v)
    s = jnp.einsum('bnqhgd,bnkhd->bnhgqk', qb, kk).astype(jnp.float32) * (1.0 / math.sqrt(d))
    q_idx = jnp.arange(W)[:, None] + W
    k_idx = jnp.arange(2 * W)[None, :]
    rel = q_idx - k_idx
    blk = jnp.arange(nblk)[:, None, None]
    mask = (rel >= 0) & (rel < WINDOW) & (blk * W + k_idx - W >= 0)
    logits = jnp.where(mask[None, :, None, None, :, :], s, -jnp.inf)
    sink = sinks.astype(jnp.float32).reshape(1, 1, Hk, G, 1, 1)
    m = jnp.maximum(jnp.max(logits, axis=-1, keepdims=True), sink)
    e = jnp.exp(logits - m)
    p = e / (jnp.sum(e, axis=-1, keepdims=True) + jnp.exp(sink - m))
    o = jnp.einsum('bnhgqk,bnkhd->bnqhgd', p.astype(vv.dtype), vv).reshape(B_, S, SWA_WIDTH)
    return (o * jax.nn.silu(z)) @ w_out

def first_inputs(seed: int = 0) -> dict:
    key = jax.random.key(seed)
    ks = jax.random.split(key, 24)
    f32 = jnp.float32
    D = D_MODEL

    def lin(k, shape):
        return jax.random.normal(k, shape, f32) * (shape[-2] ** -0.5)

    x = jax.random.normal(ks[0], (BATCH, SEQ, D), f32)
    offset = jax.random.randint(ks[1], (BATCH, 1), 0, 1024, dtype=jnp.int32)
    positions = offset + jnp.arange(SEQ, dtype=jnp.int32)[None, :]
    norm_w = 1.0 + 0.1 * jax.random.normal(ks[2], (DEPTH, D), f32)
    final_norm_w = 1.0 + 0.1 * jax.random.normal(ks[3], (D,), f32)
    conv_w_in = lin(ks[4], (N_CONV_LAYERS, D, 4 * CONV_WIDTH))
    conv_w_conv = jax.random.normal(ks[5], (N_CONV_LAYERS, CONV_K, CONV_WIDTH), f32) * (CONV_K ** -0.5)
    conv_w_out = lin(ks[6], (N_CONV_LAYERS, CONV_WIDTH, D))
    fox_w_in = lin(ks[7], (N_FOX_LAYERS, D, 4 * FOX_WIDTH + FOX_HEADS))
    fox_b_f = jax.random.uniform(ks[8], (N_FOX_LAYERS, FOX_HEADS), f32, 1.0, 5.0)
    fox_w_out = lin(ks[9], (N_FOX_LAYERS, FOX_WIDTH, D))
    gdn_w_in = lin(ks[10], (N_GDN_LAYERS, D, 4 * GDN_WIDTH + 2 * GDN_HEADS))
    gdn_w_conv = jax.random.normal(ks[11], (N_GDN_LAYERS, GDN_CONV_K, 3 * GDN_WIDTH), f32) * (GDN_CONV_K ** -0.5)
    gdn_a_log = jnp.log(jax.random.uniform(ks[12], (N_GDN_LAYERS, GDN_HEADS), f32, 1.0, 16.0))
    dt = jnp.exp(jax.random.uniform(ks[13], (N_GDN_LAYERS, GDN_HEADS), f32, math.log(1e-3), math.log(1e-1)))
    gdn_dt_bias = dt + jnp.log(-jnp.expm1(-dt))
    gdn_norm_w = 1.0 + 0.1 * jax.random.normal(ks[14], (N_GDN_LAYERS, GDN_HEAD_DIM), f32)
    gdn_w_out = lin(ks[15], (N_GDN_LAYERS, GDN_WIDTH, D))
    swa_w_in = lin(ks[16], (N_SWA_LAYERS, D, 2 * SWA_WIDTH + 2 * SWA_KV_WIDTH))
    swa_sinks = 0.5 * jax.random.normal(ks[17], (N_SWA_LAYERS, SWA_HEADS), f32)
    swa_w_out = lin(ks[18], (N_SWA_LAYERS, SWA_WIDTH, D))
    return {"x": x, "positions": positions, "norm_w": norm_w, "final_norm_w": final_norm_w,
            "conv_w_in": conv_w_in, "conv_w_conv": conv_w_conv, "conv_w_out": conv_w_out,
            "fox_w_in": fox_w_in, "fox_b_f": fox_b_f, "fox_w_out": fox_w_out,
            "gdn_w_in": gdn_w_in, "gdn_w_conv": gdn_w_conv, "gdn_a_log": gdn_a_log, "gdn_dt_bias": gdn_dt_bias,
            "gdn_norm_w": gdn_norm_w, "gdn_w_out": gdn_w_out,
            "swa_w_in": swa_w_in, "swa_sinks": swa_sinks, "swa_w_out": swa_w_out}

def first_block(x, positions, norm_w, final_norm_w, conv_w_in, conv_w_conv, conv_w_out,
              fox_w_in, fox_b_f, fox_w_out, gdn_w_in, gdn_w_conv, gdn_a_log, gdn_dt_bias,
              gdn_norm_w, gdn_w_out, swa_w_in, swa_sinks, swa_w_out):
    for i in range(DEPTH):
        h = rms_norm(x, norm_w[i])
        kind, j = i % N_MIXERS, i // N_MIXERS
        if kind == 0:
            y = conv_mixer(h, conv_w_in[j], conv_w_conv[j], conv_w_out[j])
        elif kind == 1:
            y = fox_mixer(h, fox_w_in[j], fox_b_f[j], fox_w_out[j])
        elif kind == 2:
            y = gdn_mixer(h, gdn_w_in[j], gdn_w_conv[j], gdn_a_log[j], gdn_dt_bias[j], gdn_norm_w[j], gdn_w_out[j])
        else:
            y = swa_mixer(h, positions, swa_w_in[j], swa_sinks[j], swa_w_out[j])
        x = x + y.astype(x.dtype)
    return rms_norm(x, final_norm_w)


DEPTH_2 = 2

N_MIXERS_2 = 2
PLE_DIM = 256
D_FF = 4 * D_MODEL

HG_KDIM = 128
HG_HEADS = D_MODEL // HG_KDIM
HG_VDIM = D_MODEL // HG_HEADS
HG_QK = HG_HEADS * HG_KDIM
HG_V = HG_HEADS * HG_VDIM
HG_CHUNK = 64
N_HGRN = (DEPTH_2 + 1) // 2

MLA_HEADS = 16
MLA_Q_RANK = 384
MLA_KV_RANK = 256
MLA_NOPE = 128
MLA_ROPE = 64
MLA_V = 128
ROPE_BASE = 10000.0
N_MLA = DEPTH_2 // 2


def rms_norm_2(x, gain):
    xf = x.astype(jnp.float32)
    y = xf * lax.rsqrt(jnp.mean(xf * xf, axis=-1, keepdims=True) + EPS)
    return (y * gain.astype(jnp.float32)).astype(x.dtype)

def gla_chunk_scan(q, k, v, g):
    b, h, s, dk = q.shape
    dv = v.shape[-1]
    nc = s // HG_CHUNK

    def to_chunks(t):
        return jnp.moveaxis(t.reshape(b, h, nc, HG_CHUNK, t.shape[-1]), 2, 0)

    qc, kc, vc, gc = to_chunks(q), to_chunks(k), to_chunks(v), to_chunks(g)
    mask = jnp.tril(jnp.ones((HG_CHUNK, HG_CHUNK), dtype=bool))

    def step(state, inp):
        qi, ki, vi, gi = inp
        G = jnp.cumsum(gi.astype(jnp.float32), axis=-2)
        G_last = G[..., -1:, :]
        q_dec = qi * jnp.exp(G)
        k_inv = ki * jnp.exp(-G)
        k_end = ki * jnp.exp(G_last - G)
        attn = jnp.where(mask, jnp.einsum('bhik,bhjk->bhij', q_dec, k_inv), 0.0)
        o = (jnp.einsum('bhij,bhjv->bhiv', attn, vi)
             + jnp.einsum('bhik,bhkv->bhiv', q_dec, state))
        new_state = (jnp.exp(G_last[..., 0, :])[..., None] * state
                     + jnp.einsum('bhjk,bhjv->bhkv', k_end, vi))
        return new_state, o

    state0 = jnp.zeros((b, h, dk, dv), jnp.float32)
    _, o = lax.scan(step, state0, (qc, kc, vc, gc))
    return jnp.moveaxis(o, 0, 2).reshape(b, h, s, dv).astype(v.dtype)

def hgrn2_mixer(x, w_in, o_norm, w_out, lb):
    b, s, _ = x.shape
    proj = x @ w_in
    q, f_fw, f_bw, inp, gate = jnp.split(
        proj, [HG_QK, 2 * HG_QK, 3 * HG_QK, 3 * HG_QK + HG_V], axis=-1)

    def heads(t):
        return jnp.transpose(t.reshape(b, s, HG_HEADS, -1), (0, 2, 1, 3))

    q = heads(q) * (HG_KDIM ** -0.5)
    v = heads(inp)
    lbh = lb.astype(jnp.float32).reshape(HG_HEADS, 1, HG_KDIM)

    def gates(f_logit):
        f = lbh + (1.0 - lbh) * jax.nn.sigmoid(heads(f_logit).astype(jnp.float32))
        return 1.0 - f, jnp.log(f)

    k_f, g_f = gates(f_fw)
    k_b, g_b = gates(f_bw)
    flip = lambda t: jnp.flip(t, axis=2)
    o_f = gla_chunk_scan(q, k_f, v, g_f)
    o_b = flip(gla_chunk_scan(flip(q), flip(k_b), flip(v), flip(g_b)))
    o = rms_norm_2(o_f + o_b, o_norm[:, None, :])
    o = jnp.transpose(o, (0, 2, 1, 3)).reshape(b, s, HG_V)
    return (o * jax.nn.silu(gate)) @ w_out

def rope_angles(positions, dim):
    inv = 1.0 / (ROPE_BASE ** (jnp.arange(0, dim, 2, dtype=jnp.float32) / dim))
    ang = positions.astype(jnp.float32)[..., None] * inv
    return jnp.cos(ang), jnp.sin(ang)

def apply_rope(t, cos, sin):
    t1, t2 = jnp.split(t, 2, axis=-1)
    cos = cos.astype(t.dtype)
    sin = sin.astype(t.dtype)
    return jnp.concatenate([t1 * cos - t2 * sin, t1 * sin + t2 * cos], axis=-1)

def mla_mixer(x, positions, w_in, q_norm, w_uq, kv_norm, w_ukv, w_o):
    b, s, _ = x.shape
    proj = x @ w_in
    cq, ckv, k_rope = jnp.split(proj, [MLA_Q_RANK, MLA_Q_RANK + MLA_KV_RANK], axis=-1)
    cq = rms_norm_2(cq, q_norm)
    ckv = rms_norm_2(ckv, kv_norm)
    q = (cq @ w_uq).reshape(b, s, MLA_HEADS, MLA_NOPE + MLA_ROPE)
    q_nope, q_rope = q[..., :MLA_NOPE], q[..., MLA_NOPE:]
    cos, sin = rope_angles(positions, MLA_ROPE)
    q_rope = apply_rope(q_rope, cos[:, :, None, :], sin[:, :, None, :])
    k_rope = apply_rope(k_rope, cos, sin)
    w_ukv_h = w_ukv.reshape(MLA_KV_RANK, MLA_HEADS, MLA_NOPE + MLA_V)
    w_uk, w_uv = w_ukv_h[..., :MLA_NOPE], w_ukv_h[..., MLA_NOPE:]
    q_lat = jnp.einsum('bshn,chn->bshc', q_nope, w_uk)
    scale = (MLA_NOPE + MLA_ROPE) ** -0.5
    nb = s // Q_BLOCK

    def blockify(t):
        return jnp.moveaxis(t.reshape(b, nb, Q_BLOCK, *t.shape[2:]), 1, 0)

    def attend(blk):
        ql, qr = blk
        scores = (jnp.einsum('bqhc,bkc->bhqk', ql, ckv)
                  + jnp.einsum('bqhr,bkr->bhqk', qr, k_rope)) * scale
        probs = jax.nn.softmax(scores.astype(jnp.float32), axis=-1).astype(ckv.dtype)
        return jnp.einsum('bhqk,bkc->bqhc', probs, ckv)

    o_lat = lax.map(attend, (blockify(q_lat), blockify(q_rope)))
    o_lat = jnp.moveaxis(o_lat, 0, 1).reshape(b, s, MLA_HEADS, MLA_KV_RANK)
    o = jnp.einsum('bshc,chv->bshv', o_lat, w_uv).reshape(b, s, MLA_HEADS * MLA_V)
    return o @ w_o

def squared_relu_mlp(x, w1, w2):
    return jnp.square(jax.nn.relu(x @ w1)) @ w2

def second_inputs(seed: int = 0) -> dict:
    key = jax.random.key(seed)
    ks = jax.random.split(key, 32)
    f32 = jnp.float32

    def nrm(k, shape, fan_in):
        return jax.random.normal(k, shape, f32) * (fan_in ** -0.5)

    def gain(k, shape):
        return 1.0 + 0.05 * jax.random.normal(k, shape, f32)

    x = jax.random.normal(ks[0], (BATCH, SEQ, D_MODEL), f32)
    p = jax.random.normal(ks[1], (DEPTH_2, BATCH, SEQ, PLE_DIM), f32)
    positions = (jnp.arange(SEQ, dtype=jnp.int32)[None, :]
                 + jax.random.randint(ks[2], (BATCH, 1), 0, SEQ, dtype=jnp.int32))
    return {
        "x": x,
        "p": p,
        "positions": positions,
        "pre_mix_norm": gain(ks[3], (DEPTH_2, D_MODEL)),
        "post_mix_norm": gain(ks[4], (DEPTH_2, D_MODEL)),
        "pre_mlp_norm": gain(ks[5], (DEPTH_2, D_MODEL)),
        "post_mlp_norm": gain(ks[6], (DEPTH_2, D_MODEL)),
        "w_mlp_in": nrm(ks[7], (DEPTH_2, D_MODEL, D_FF), D_MODEL),
        "w_mlp_out": nrm(ks[8], (DEPTH_2, D_FF, D_MODEL), D_FF),
        "w_ple_proj": nrm(ks[9], (DEPTH_2, PLE_DIM, D_MODEL), PLE_DIM),
        "w_ple_gate": nrm(ks[10], (DEPTH_2, D_MODEL, D_MODEL), D_MODEL),
        "ple_norm": gain(ks[11], (DEPTH_2, D_MODEL)),
        "hg_lb_logits": 0.1 * jax.random.normal(ks[12], (DEPTH_2 + 1, HG_QK), f32),
        "hg_w_in": nrm(ks[13], (N_HGRN, D_MODEL, 3 * HG_QK + 2 * HG_V), D_MODEL),
        "hg_o_norm": gain(ks[14], (N_HGRN, HG_HEADS, HG_VDIM)),
        "hg_w_out": nrm(ks[15], (N_HGRN, HG_V, D_MODEL), HG_V),
        "mla_w_in": nrm(ks[16], (N_MLA, D_MODEL, MLA_Q_RANK + MLA_KV_RANK + MLA_ROPE), D_MODEL),
        "mla_q_norm": gain(ks[17], (N_MLA, MLA_Q_RANK)),
        "mla_w_uq": nrm(ks[18], (N_MLA, MLA_Q_RANK, MLA_HEADS * (MLA_NOPE + MLA_ROPE)), MLA_Q_RANK),
        "mla_kv_norm": gain(ks[19], (N_MLA, MLA_KV_RANK)),
        "mla_w_ukv": nrm(ks[20], (N_MLA, MLA_KV_RANK, MLA_HEADS * (MLA_NOPE + MLA_V)), MLA_KV_RANK),
        "mla_w_o": nrm(ks[21], (N_MLA, MLA_HEADS * MLA_V, D_MODEL), MLA_HEADS * MLA_V),
    }

def second_block(x, p, positions, pre_mix_norm, post_mix_norm, pre_mlp_norm, post_mlp_norm,
              w_mlp_in, w_mlp_out, w_ple_proj, w_ple_gate, ple_norm,
              hg_lb_logits, hg_w_in, hg_o_norm, hg_w_out,
              mla_w_in, mla_q_norm, mla_w_uq, mla_kv_norm, mla_w_ukv, mla_w_o):
    lb_all = jnp.cumsum(jax.nn.softmax(hg_lb_logits.astype(jnp.float32), axis=0), axis=0)
    h = x
    for i in range(DEPTH_2):
        a = rms_norm_2(h, pre_mix_norm[i])
        j = i // N_MIXERS_2
        if i % N_MIXERS_2 == 0:
            m = hgrn2_mixer(a, hg_w_in[j], hg_o_norm[j], hg_w_out[j], lb_all[i])
        else:
            m = mla_mixer(a, positions, mla_w_in[j], mla_q_norm[j], mla_w_uq[j],
                          mla_kv_norm[j], mla_w_ukv[j], mla_w_o[j])
        h = h + rms_norm_2(m, post_mix_norm[i])
        f = squared_relu_mlp(rms_norm_2(h, pre_mlp_norm[i]), w_mlp_in[i], w_mlp_out[i])
        h = h + rms_norm_2(f, post_mlp_norm[i])
        e = p[i].astype(h.dtype) @ w_ple_proj[i]
        g = jax.nn.sigmoid(h @ w_ple_gate[i])
        h = h + rms_norm_2(g * e, ple_norm[i])
    return h


def setup_inputs(seed=0):
    out = dict(first_inputs(seed))
    for name, value in second_inputs(seed + 1).items():
        if name != "x":
            out[name + "_2"] = value
    return out


def reference(
    x, positions, norm_w, final_norm_w, conv_w_in, conv_w_conv, conv_w_out, fox_w_in, fox_b_f,
    fox_w_out, gdn_w_in, gdn_w_conv, gdn_a_log, gdn_dt_bias, gdn_norm_w, gdn_w_out, swa_w_in,
    swa_sinks, swa_w_out, p_2, positions_2, pre_mix_norm_2, post_mix_norm_2, pre_mlp_norm_2,
    post_mlp_norm_2, w_mlp_in_2, w_mlp_out_2, w_ple_proj_2, w_ple_gate_2, ple_norm_2,
    hg_lb_logits_2, hg_w_in_2, hg_o_norm_2, hg_w_out_2, mla_w_in_2, mla_q_norm_2, mla_w_uq_2,
    mla_kv_norm_2, mla_w_ukv_2, mla_w_o_2,
):
    x = first_block(
        x, positions, norm_w, final_norm_w, conv_w_in, conv_w_conv, conv_w_out, fox_w_in,
        fox_b_f, fox_w_out, gdn_w_in, gdn_w_conv, gdn_a_log, gdn_dt_bias, gdn_norm_w, gdn_w_out,
        swa_w_in, swa_sinks, swa_w_out,
    )
    return second_block(
        x, p_2, positions_2, pre_mix_norm_2, post_mix_norm_2, pre_mlp_norm_2, post_mlp_norm_2,
        w_mlp_in_2, w_mlp_out_2, w_ple_proj_2, w_ple_gate_2, ple_norm_2, hg_lb_logits_2,
        hg_w_in_2, hg_o_norm_2, hg_w_out_2, mla_w_in_2, mla_q_norm_2, mla_w_uq_2, mla_kv_norm_2,
        mla_w_ukv_2, mla_w_o_2,
    )


_drawn_inputs = setup_inputs


def setup_inputs(seed=0):
    import zlib

    import numpy as np

    out = dict(_drawn_inputs(seed))
    spreads = {}
    factors = {'swa_sinks': 8.0, 'mla_q_norm_2': 5.824}
    for name, (base, spread) in spreads.items():
        noise = np.random.default_rng([zlib.crc32(name.encode()), seed]).standard_normal(out[name].shape)
        drawn = base * np.exp(spread * noise) if base else spread * noise
        out[name] = __import__('jax').numpy.asarray(drawn.astype(out[name].dtype))
    for name, factor in factors.items():
        out[name] = (out[name] * factor).astype(out[name].dtype)
    return out
```

```python
import math
from contextlib import ExitStack

import concourse.bass as bass
import numpy as np
from concourse import mybir

F32 = mybir.dt.float32
F32R = mybir.dt.float32r
I32 = mybir.dt.int32
ALU = mybir.AluOpType
ACT = mybir.ActivationFunctionType
AX = mybir.AxisListType

P = 128
S = 512
D = 1024
DT = D // P
EPS = 1e-6
NEG = -1.0e30
SLOTS = 4
AHEAD = SLOTS - 1
CH = 64
NCH = S // CH
H8 = 8
QT = S // P


def const_layout():
    i = np.arange(P)
    c = {}
    c["ident"] = np.eye(P)
    c["ones"] = np.ones((P, S))
    c["eps"] = np.full((P, 1), EPS)
    c["causal"] = np.where(i[None, :] <= i[:, None], 0.0, NEG)
    c["before"] = np.where(i[None, :] > i[:, None], 0.0, NEG)
    rot = np.zeros((P, P))
    for g in range(0, P, 64):
        for j in range(32):
            rot[g + j + 32, g + j] = -1.0
            rot[g + j, g + j + 32] = 1.0
    c["rotate"] = rot
    k = np.arange(CH)
    m = np.zeros((P, CH)); m[:CH] = np.where(k[:, None] <= k[None, :], 1.0, 0.0)
    c["upto"] = m
    m = np.zeros((P, CH)); m[:CH] = np.where(k[:, None] >= k[None, :], 1.0, 0.0)
    c["from"] = m
    m = np.zeros((P, CH)); m[:CH] = np.where(k[:, None] <= k[None, :], 0.0, NEG)
    c["upto_neg"] = m
    for lvl in range(6):
        b = 1 << lvl
        up = (k[:, None] // (2 * b) == k[None, :] // (2 * b)) & (k[:, None] // b % 2 == 0) & (k[None, :] // b % 2 == 1)
        m = np.zeros((P, CH)); m[:CH] = up
        c[f"level{lvl}"] = m
    c["restart"] = np.tile(np.where(np.arange(S) % CH == 0, 0.0, 1.0), (P, 1))
    half = 32
    f = (10000.0 ** (-np.arange(half, dtype=np.float32) / np.float32(half))).astype(np.float32)
    c["swa_freq"] = np.tile(f, 4)[:, None]
    f = (1.0 / (10000.0 ** (np.arange(0, 64, 2, dtype=np.float32) / np.float32(64)))).astype(np.float32)
    c["mla_freq"] = np.tile(f, 4)[:, None]
    return {k: np.asarray(v, np.float32) for k, v in c.items()}


PARAMS = [("norm_w", 4 * DT), ("final_norm_w", DT), ("conv_w_conv", 3 * DT), ("gdn_w_conv", 4 * 3 * DT),
          ("gdn_norm_w", 1), ("pre_mix_norm_2", 2 * DT), ("post_mix_norm_2", 2 * DT),
          ("pre_mlp_norm_2", 2 * DT), ("post_mlp_norm_2", 2 * DT), ("ple_norm_2", 2 * DT),
          ("hg_lb_logits_2", 3 * DT), ("hg_o_norm_2", DT), ("mla_q_norm_2", 3), ("mla_kv_norm_2", 2)]
HEAD_COLS = ["fox_b_f", "gdn_dt_bias", "gdn_a_log"]


def param_columns():
    at, cols = 0, {}
    for name, n in PARAMS:
        cols[name] = at
        at += n
    for name in HEAD_COLS:
        cols[name] = at
        at += 1
    return cols, at


JOBS = [("conv", 4 * DT), ("conv_out", DT),
        ("fox_f", 1), ("fox", 4 * H8), ("fox_out", DT),
        ("gdn_ba", 1), ("gdn", 4 * H8), ("gdn_out", DT),
        ("swa0", 10), ("swa1", 10), ("swa_out", DT),
        ("hg", 4 * H8), ("hg_gate", DT), ("hg_out", DT),
        ("mlp0", 64), ("ple0_gate", DT), ("ple0_proj", 2),
        ("mla_in", 6), ("mla_rope", 4), ("mla_a", 8), ("mla_outa", DT), ("mla_b", 8), ("mla_outb", DT),
        ("mlp1", 64), ("ple1_gate", DT), ("ple1_proj", 2)]
FIRST_JOB = {}
N_JOBS = 0
for _name, _n in JOBS:
    FIRST_JOB[_name] = N_JOBS
    N_JOBS += _n
PADDED_JOBS = N_JOBS + AHEAD

SPLITS = [("conv_h", DT), ("conv_y", DT), ("fox_h", DT), ("fox_y", DT), ("gdn_h", DT), ("gdn_y", DT),
          ("swa_h", DT), ("swa_y", DT), ("hg_h", DT), ("hg_y", DT),
          ("mlp0_h", DT), ("mlp0_y", 4 * DT), ("ple0_h", DT), ("ple0_p", 2),
          ("mla_h", DT), ("mla_cq", 3), ("mla_ckv", 2), ("mla_y", 2 * DT),
          ("mlp1_h", DT), ("mlp1_y", 4 * DT), ("ple1_h", DT), ("ple1_p", 2)]
FIRST_SPLIT, _t = {}, 0
for _name, _n in SPLITS:
    FIRST_SPLIT[_name] = _t
    _t += _n

STATS = [("conv", DT, D), ("fox", DT, D), ("gdn", DT, D), ("swa", DT, D), ("final", DT, D),
         ("hg", DT, D), ("hg_post", DT, D), ("mlp0", DT, D), ("mlp0_post", DT, D), ("ple0_post", DT, D),
         ("mla", DT, D), ("mla_q", 3, 384), ("mla_kv", 2, 256),
         ("mla_post", DT, D), ("mlp1", DT, D), ("mlp1_post", DT, D), ("ple1_post", DT, D)]
FIRST_SQUARE, STAT_NO, STAT_SIZE, _t = {}, {}, {}, 0
for _k, (_name, _n, _f) in enumerate(STATS):
    FIRST_SQUARE[_name], STAT_NO[_name], STAT_SIZE[_name] = _t, _k, (_n, _f)
    _t += _n

MSTEPS = [("hg", DT), ("mlp0", 4 * DT), ("ple0", DT), ("mla", 2 * DT), ("mlp1", 4 * DT), ("ple1", DT)]
M_DONE = {name: sum(n for _, n in MSTEPS[:k + 1]) for k, (name, _) in enumerate(MSTEPS)}
NTH_PLE = {name: k for k, name in enumerate(name for name, _ in MSTEPS if name.startswith("ple"))}

XSTEPS = ["load", "conv", "fox", "gdn", "swa", "final", "hg", "mlp0", "ple0", "mla", "mlp1", "ple1"]
X_DONE = {name: (k + 1) * DT for k, name in enumerate(XSTEPS)}


def settle(e):
    e.eng.sem_inc(e.K.sem("waits_ended"), 1)


class Names:
    pass


class Chain:

    def __init__(self, eng, sem):
        self.eng, self.sem, self.base, self.k = eng, sem, 0, 0

    def step(self, ins):
        ins.then_inc(self.sem, 1)
        self.k += 1

    def wait(self):
        self.eng.wait_ge(self.sem, self.base + self.k)

    def enter(self, i, per):
        self.entry = self.base + self.k
        self.base, self.k, self.per = self.entry + i * per, 0, per

    def leave(self, trips):
        assert self.k == self.per, (self.k, self.per)
        self.base, self.k = self.entry + trips * self.per, 0


def at(buf, i, n=None):
    return buf[:, bass.ds(i, 1), :].rearrange("p a n -> p (a n)")


def hybrid_stack(nc, weights, x_t, p_t, consts, params, positions, positions_2, sinks, out):
    const_cols = {}
    n = 0
    for name, a in const_layout().items():
        const_cols[name] = (n, a.shape[1])
        n += a.shape[1]
    n_const = n
    cols, n_params = param_columns()

    ctx = ExitStack()
    with ctx:
        def sb(name, shape, dt=F32):
            return ctx.enter_context(nc.sbuf_tensor(name, shape, dt))

        sems = {}

        def sem(name):
            if name not in sems:
                sems[name] = ctx.enter_context(nc.semaphore(name))
            return sems[name]

        K = Names()
        K.nc, K.sem, K.cols, K.out, K.weights, K.x_t, K.p_t = nc, sem, cols, out, weights, x_t, p_t
        K.consts_in, K.params_in, K.positions, K.positions_2, K.sinks_in = consts, params, positions, positions_2, sinks
        K.const = sb("const", [P, n_const])
        K.param = sb("param", [P, n_params])
        K.sinks = sb("sink_rows", [P, 16])
        K.raw = sb("weights_raw", [P, SLOTS, D])
        K.w_hi = sb("weights_high", [P, SLOTS, D], F32R)
        K.w_lo = sb("weights_low", [P, SLOTS, D], F32R)
        K.X = sb("residual", [P, DT, S])
        K.M = sb("mixed", [P, DT, S])
        K.act_hi = sb("activations_high", [P, 2 * DT, S], F32R)
        K.act_lo = sb("activations_low", [P, 2 * DT, S], F32R)
        K.ident_r = sb("ident_r", [P, P], F32R)
        K.mask_r = sb("mask_r", [P, 2 * P], F32R)
        K.sq = sb("squares", [P, 2, S])
        K.rstd = sb("rstd", [P, S])
        K.root = sb("root", [P, S])
        K.y = sb("to_split", [P, 2, S])
        K.work = sb("work", [P, 10240])
        K.ps = [ctx.enter_context(nc.psum_tensor(f"bank{k}", [P, S], F32)) for k in range(8)]
        K.job_sems = dict(raw=[sem(f"raw_full{k}") for k in range(SLOTS)], high=sem("weights_high_ready"),
                          low=sem("weights_low_ready"), done=sem("jobs_done"),
                          bank=[sem(f"bank_free{k}") for k in range(SLOTS)])

        def c(name, parts=P):
            a, w = const_cols[name]
            return K.const[0:parts, a:a + w]
        K.c = c
        K.col = lambda name, j: K.param[:, cols[name] + j:cols[name] + j + 1]
        for name in ("constants_in", "x_in", "x_ready", "y_done", "split_high_done", "split_done",
                     "square_ready", "square_used", "rstd_ready", "vector_steps", "scalar_steps", "stored", "finished", "masks_ready", "position", "waits_ended"):
            sem(name)

        block = ctx.enter_context(nc.Block())
        stages = STAGES

        @block.sync
        def _(sync):
            sync.dma_start(K.const[:, :], consts).then_inc(sem("constants_in"), 16)
            sync.dma_start(K.param[:, :], params).then_inc(sem("constants_in"), 16)
            sync.dma_start(K.sinks[:, :], sinks[None, :].broadcast_to([P, 16])).then_inc(sem("constants_in"), 16)
            def fill(r, j):
                sync.wait_ge(K.job_sems["low"], j + 1)
                sync.dma_start(K.raw[:, r, :], weights[bass.ds(j, 1)].rearrange("a p n -> p (a n)")) \
                    .then_inc(K.job_sems["raw"][r], 16)

            with sync.Fori(0, PADDED_JOBS // SLOTS) as i:
                for r in range(SLOTS):
                    fill(r, i * SLOTS + r)
            for r in range(PADDED_JOBS % SLOTS):
                fill(r, PADDED_JOBS // SLOTS * SLOTS + r)
            sync.wait_ge(sem("finished"), 1)
            sync.dma_start(out.rearrange("(t p) s -> p t s", p=P), K.X[:, :, :]).then_inc(sem("stored"), 16)
            sync.wait_ge(sem("stored"), 16)

        @block.gpsimd
        def _(pool):
            pool.sem_inc(K.job_sems["low"], SLOTS)
            pool.dma_start(K.X[:, :, :], x_t.rearrange("(t p) s -> p t s", p=P)).then_inc(sem("x_in"), 16)

            def low(r, j):
                pool.wait_ge(K.job_sems["high"], j + 1)
                nc.gpsimd.tensor_tensor(K.w_lo[:, r, :], K.raw[:, r, :], K.w_hi[:, r, :].bitcast(F32),
                                        ALU.subtract).then_inc(K.job_sems["low"], 1)

            with pool.Fori(0, PADDED_JOBS // SLOTS) as i:
                for r in range(SLOTS):
                    low(r, i * SLOTS + r)
            for r in range(PADDED_JOBS % SLOTS):
                low(r, PADDED_JOBS // SLOTS * SLOTS + r)

        @block.scalar
        def _(act):
            e = Names()
            e.eng, e.K, e.steps = act, K, Chain(act, sem("scalar_steps"))
            act.wait_ge(sem("constants_in"), 48)
            for j in range(AHEAD):
                weight_high(e, j)
            for name in stages:
                PROGRAM[name][1](e)

        @block.tensor
        def _(pe):
            e = Names()
            e.eng, e.K = pe, K
            pe.wait_ge(sem("constants_in"), 48)
            pe.wait_ge(sem("masks_ready"), 1)
            for name in stages:
                PROGRAM[name][0](e)

        @block.vector
        def _(dve):
            e = Names()
            e.eng, e.K, e.steps = dve, K, Chain(dve, sem("vector_steps"))
            for k in range(SLOTS):
                dve.sem_inc(K.job_sems["bank"][k], 1)
            dve.wait_ge(sem("constants_in"), 48)
            e.steps.step(nc.vector.tensor_copy(K.ident_r[:, :], K.c("ident")))
            e.steps.step(nc.vector.tensor_copy(K.mask_r[:, 0:P], K.c("before")))
            nc.vector.tensor_copy(K.mask_r[:, P:2 * P], K.c("causal")).then_inc(sem("masks_ready"), 1)
            dve.wait_ge(sem("x_in"), 16)
            dve.sem_inc(sem("x_ready"), DT)
            for name in stages:
                PROGRAM[name][2](e)
            dve.wait_ge(sem("x_ready"), X_DONE[stages[-1]])
            dve.sem_inc(sem("finished"), 1)



def weight_high(e, c, i=None):
    js, s, off = e.K.job_sems, c % SLOTS, 0 if i is None else i
    e.eng.wait_ge(js["raw"][s], off * 16 + 16 * (c // SLOTS + 1))
    if c >= SLOTS:
        e.eng.wait_ge(js["done"], off * SLOTS + c - SLOTS + 1)
    e.K.nc.scalar.activation(e.K.w_hi[:, s, :], e.K.raw[:, s, :], ACT.Copy).then_inc(js["high"], 1)


def job_wait(e, c, i=None):
    off = 0 if i is None else i
    e.eng.wait_ge(e.K.job_sems["done"], off * SLOTS + c + 1)


def bank_of(e, c):
    return e.K.ps[c % SLOTS]


def release(e, c):
    e.eng.sem_inc(e.K.job_sems["bank"][c % SLOTS], 1)


def job_start(e, c, i=None):
    off = 0 if i is None else i
    js = e.K.job_sems
    e.eng.wait_ge(js["low"], off * SLOTS + c + 1 + SLOTS)
    e.eng.wait_ge(js["bank"][c % SLOTS], off + c // SLOTS + 1)


def product(e, c, dst, tiles, chunk0=0, start=True, stop=True):
    K, s = e.K, c % SLOTS
    for n, t in enumerate(tiles):
        k = chunk0 + n
        wh, wl = K.w_hi[:, s, k * P:(k + 1) * P], K.w_lo[:, s, k * P:(k + 1) * P]
        first, last = start and n == 0, stop and n == len(tiles) - 1
        K.nc.tensor.matmul(dst, wh, K.act_hi[:, t, :], start=first, stop=False)
        K.nc.tensor.matmul(dst, wh, K.act_lo[:, t, :], start=False, stop=False)
        ins = K.nc.tensor.matmul(dst, wl, K.act_hi[:, t, :], start=False, stop=last)
    return ins


A_TILES = list(range(DT))
B_TILES = list(range(DT, 2 * DT))


def job(e, c, i=None, tiles=A_TILES):
    job_start(e, c, i)
    product(e, c, bank_of(e, c)[:, :], tiles).then_inc(e.K.job_sems["done"], 1)


def split_wait(e, stage, n):
    e.eng.wait_ge(e.K.sem("split_done"), FIRST_SPLIT[stage] + n)


def split_high(e, stage, k, tile, src):
    e.eng.wait_ge(e.K.sem("y_done"), FIRST_SPLIT[stage] + k + 1)
    e.K.nc.scalar.activation(at(e.K.act_hi, tile), src, ACT.Copy).then_inc(e.K.sem("split_high_done"), 1)


def split_low(e, stage, k, tile, src):
    e.eng.wait_ge(e.K.sem("split_high_done"), FIRST_SPLIT[stage] + k + 1)
    e.K.nc.vector.tensor_tensor(at(e.K.act_lo, tile), src, at(e.K.act_hi, tile).bitcast(F32),
                                ALU.subtract).then_inc(e.K.sem("split_done"), 1)


STAT_BANK = 7


def stat_scalar(e, stage, source, ready):
    K, (n, feats) = e.K, STAT_SIZE[stage]
    for k in range(n):
        t = FIRST_SQUARE[stage] + k
        ready(k)
        if t >= 2:
            e.eng.wait_ge(K.sem("square_used"), t - 1)
        K.nc.scalar.activation(K.sq[:, t % 2, :], source[:, k, :], ACT.Square, scale=feats ** -0.5) \
            .then_inc(K.sem("square_ready"), 1)
    root_scalar(e, stage)


def stat_tensor(e, stage):
    K, (n, _) = e.K, STAT_SIZE[stage]
    if STAT_NO[stage]:
        e.eng.wait_ge(K.sem("rstd_ready"), STAT_NO[stage])
    for k in range(n):
        t = FIRST_SQUARE[stage] + k
        e.eng.wait_ge(K.sem("square_ready"), t + 1)
        K.nc.tensor.matmul(K.ps[STAT_BANK][:, :], K.c("ones")[:, 0:P], K.sq[:, t % 2, :],
                           start=k == 0, stop=k == n - 1).then_inc(K.sem("square_used"), 1)


def inverse_root(e, out, tmp, src):
    e.steps.step(e.K.nc.scalar.activation(tmp, src, ACT.Ln, bias=e.K.c("eps")))
    e.steps.wait()
    return e.K.nc.scalar.activation(out, tmp, ACT.Exp, scale=-0.5)


def root_scalar(e, stage):
    K, (n, _) = e.K, STAT_SIZE[stage]
    e.eng.wait_ge(K.sem("square_used"), FIRST_SQUARE[stage] + n)
    inverse_root(e, K.rstd[:, :], K.root[:, :], K.ps[STAT_BANK][:, :]).then_inc(K.sem("rstd_ready"), 1)


def stat_vector(e, stage):
    e.eng.wait_ge(e.K.sem("rstd_ready"), STAT_NO[stage] + 1)


def norm_split_vector(e, stage, split, source, weight, col0, n, tile0=0, free_after=None):
    K = e.K
    if free_after is not None:
        e.eng.wait_ge(K.job_sems["done"], free_after)
    for k in range(n + 1):
        if k < n:
            if FIRST_SPLIT[split] + k >= 2:
                e.eng.wait_ge(K.sem("split_done"), FIRST_SPLIT[split] + max(k - 1, 0))
            K.nc.vector.scalar_tensor_tensor(K.y[:, k % 2, :], source[:, k, :], K.col(weight, col0 + k), K.rstd[:, :],
                                             ALU.mult, ALU.mult).then_inc(K.sem("y_done"), 1)
        if k:
            split_low(e, split, k - 1, tile0 + k - 1, K.y[:, (k - 1) % 2, :])


def norm_split_scalar(e, split, n, tile0=0):
    for k in range(n):
        split_high(e, split, k, tile0 + k, e.K.y[:, k % 2, :])


def x_wait(e, stage, k):
    e.eng.wait_ge(e.K.sem("x_ready"), X_DONE[XSTEPS[XSTEPS.index(stage) - 1]] - DT + k + 1)


def prenorm_pe(e, stage):
    stat_tensor(e, stage)
    split_wait(e, stage + "_h", DT)


def prenorm_act(e, stage):
    stat_scalar(e, stage, e.K.X, lambda k: x_wait(e, stage, k))
    norm_split_scalar(e, stage + "_h", DT)


def prenorm_dve(e, stage, weight, col0, free_after=None):
    stat_vector(e, stage)
    norm_split_vector(e, stage, stage + "_h", e.K.X, weight, col0, DT, 0, free_after)


def out_pe(e, phase, split, tiles=B_TILES, skip=0):
    c0 = FIRST_JOB[phase]
    with e.eng.Fori(0, DT // SLOTS) as i:
        for r in range(SLOTS):
            if r == 0:
                job_with_waits(e, c0, i, tiles, split, skip)
            else:
                job(e, c0 + r, i, tiles)


def ahead_act(e, phase):
    c0 = FIRST_JOB[phase]
    with e.eng.Fori(0, DT // SLOTS) as i:
        for r in range(SLOTS):
            weight_high(e, c0 + r + AHEAD, i)


def out_residual_dve(e, phase):
    K, c0 = e.K, FIRST_JOB[phase]
    e.steps.wait() if e.steps.k else None
    with e.eng.Fori(0, DT // SLOTS) as i:
        e.steps.enter(i, SLOTS)
        for r in range(SLOTS):
            job_wait(e, c0 + r, i)
            x = at(K.X, i * SLOTS + r)
            e.steps.step(K.nc.vector.tensor_tensor(x, bank_of(e, c0 + r)[:, :], x, ALU.add))
            e.steps.wait()
            release(e, c0 + r)
            e.eng.sem_inc(K.sem("x_ready"), 1)
        e.steps.leave(DT // SLOTS)


def conv_pe(e):
    prenorm_pe(e, "conv")
    c0 = FIRST_JOB["conv"]
    with e.eng.Fori(0, DT) as i:
        for r in range(4):
            job(e, c0 + r, i)
    out_pe(e, "conv_out", "conv_y")


def conv_buffers(K):
    w = K.work
    b = Names()
    b.c, b.z, b.u, b.t, b.taps = w[:, 0:512], w[:, 512:1024], w[:, 1024:1538], w[:, 1540:2052], w[:, 2052:2055]
    return b


def conv_act(e):
    K, b, c0 = e.K, conv_buffers(e.K), FIRST_JOB["conv"]
    prenorm_act(e, "conv")
    with e.eng.Fori(0, DT) as i:
        for r in range(4):
            weight_high(e, c0 + r + AHEAD, i)
            if r == 1:
                e.eng.wait_ge(K.sem("conv_u"), i + 1)
                job_wait(e, c0 + 1, i)
                K.nc.scalar.activation(b.c, bank_of(e, c0 + 1)[:, :], ACT.Copy).then_inc(K.sem("conv_c"), 1)
                e.eng.wait_ge(K.sem("conv_c"), i + 1)
                release(e, c0 + 1)
        job_wait(e, c0 + 3, i)
        K.nc.scalar.activation(b.z, bank_of(e, c0 + 3)[:, :], ACT.Silu).then_inc(K.sem("conv_z"), 1)
        e.eng.wait_ge(K.sem("conv_z"), i + 1)
        release(e, c0 + 3)
        e.eng.wait_ge(K.sem("y_done"), i + FIRST_SPLIT["conv_y"] + 1)
        K.nc.scalar.activation(at(K.act_hi, i + DT), K.y[:, 0, :], ACT.Copy).then_inc(K.sem("split_high_done"), 1)
    ahead_act(e, "conv_out")


def conv_dve(e):
    K, b, c0, v = e.K, conv_buffers(e.K), FIRST_JOB["conv"], e.K.nc.vector
    prenorm_dve(e, "conv", "norm_w", 0)
    e.steps.step(v.memset(b.u[:, 0:2], 0.0))
    e.steps.wait()
    e.eng.sem_inc(K.sem("conv_u"), 1)
    with e.eng.Fori(0, DT) as i:
        e.steps.enter(i, 6)
        e.steps.wait()
        e.eng.wait_ge(K.sem("split_done"), i + FIRST_SPLIT["conv_y"])
        e.steps.step(v.tensor_copy(b.taps, K.param[:, bass.ds(i * 3 + K.cols["conv_w_conv"], 3)]))
        job_wait(e, c0 + 2, i)
        e.eng.wait_ge(K.sem("conv_c"), i + 1)
        e.steps.step(v.tensor_tensor(b.u[:, 2:514], bank_of(e, c0 + 2)[:, :], b.c, ALU.mult))
        e.steps.wait()
        release(e, c0 + 2)
        e.eng.sem_inc(K.sem("conv_u"), 1)
        e.steps.step(v.tensor_scalar(b.t, b.u[:, 0:512], b.taps[:, 0:1], None, ALU.mult))
        e.steps.wait()
        e.steps.step(v.scalar_tensor_tensor(b.t, b.u[:, 1:513], b.taps[:, 1:2], b.t, ALU.mult, ALU.add))
        e.steps.wait()
        e.steps.step(v.scalar_tensor_tensor(b.t, b.u[:, 2:514], b.taps[:, 2:3], b.t, ALU.mult, ALU.add))
        e.steps.wait()
        e.steps.step(v.tensor_tensor(b.t, bank_of(e, c0)[:, :], b.t, ALU.mult))
        e.steps.wait()
        release(e, c0)
        e.eng.wait_ge(K.sem("conv_z"), i + 1)
        v.tensor_tensor(K.y[:, 0, :], b.t, b.z, ALU.mult).then_inc(K.sem("y_done"), 1)
        split = FIRST_SPLIT["conv_y"]
        e.eng.wait_ge(K.sem("split_high_done"), i + split + 1)
        v.tensor_tensor(at(K.act_lo, i + DT), K.y[:, 0, :], at(K.act_hi, i + DT).bitcast(F32),
                        ALU.subtract).then_inc(K.sem("split_done"), 1)
        e.steps.leave(DT)
    out_residual_dve(e, "conv_out")


def evacuated(e, c, i=None):
    off = 0 if i is None else i
    e.eng.wait_ge(e.K.job_sems["bank"][c % SLOTS], off + c // SLOTS + 2)


def carve(K, *shapes):
    views, a = [], 0
    for shape in shapes:
        n = math.prod(shape)
        v = K.work[:, a:a + n]
        views.append(v if len(shape) == 1 else v.rearrange("p (a b) -> p a b", a=shape[0]))
        a += n + (n & 1)
    assert a <= 10240, a
    return views


def y_pair_scalar(e, split, i):
    e.eng.wait_ge(e.K.sem("y_done"), i + FIRST_SPLIT[split] + 1)
    e.K.nc.scalar.activation(at(e.K.act_hi, i + DT), e.K.y[:, 0, :], ACT.Copy).then_inc(e.K.sem("split_high_done"), 1)


def y_pair_vector(e, split, i):
    e.eng.wait_ge(e.K.sem("split_high_done"), i + FIRST_SPLIT[split] + 1)
    e.K.nc.vector.tensor_tensor(at(e.K.act_lo, i + DT), e.K.y[:, 0, :], at(e.K.act_hi, i + DT).bitcast(F32),
                                ALU.subtract).then_inc(e.K.sem("split_done"), 1)


def fox_buffers(K):
    b = Names()
    (b.q, b.k, b.v, b.z, b.neg_c, b.x, b.e, b.sel, b.v_tok, b.p, b.pt, b.mx, b.nmax, b.sum, b.rec) = carve(
        K, (S,), (S,), (S,), (S,), (S,), (S,), (S,), (P,), (QT, P), (2, S), (QT, S), (QT,), (QT,), (QT,), (QT,))
    return b


TRANSPOSE_BANK = 6
OUT_BANK = 7


def fox_pe(e):
    K, b, nc, c0 = e.K, fox_buffers(e.K), e.K.nc, FIRST_JOB["fox"]
    prenorm_pe(e, "fox")
    job(e, FIRST_JOB["fox_f"])
    e.eng.wait_ge(K.sem("fox_c"), 1)
    tb = K.ps[TRANSPOSE_BANK]
    with e.eng.Fori(0, H8) as i:
        for r in range(3):
            job(e, c0 + r, i)
        evacuated(e, c0 + 2, i)
        e.eng.wait_ge(K.sem("fox_t_used"), i * 5 + 1)
        for t in range(QT):
            ins = nc.tensor.transpose(tb[:, t * P:(t + 1) * P], b.v[:, t * P:(t + 1) * P], K.c("ident"))
        ins.then_inc(K.sem("fox_t_ready"), 1)
        evacuated(e, c0, i)
        evacuated(e, c0 + 1, i)
        e.eng.wait_ge(K.sem("fox_sel"), i + 1)

        def scores(q):
            bank, n = K.ps[4 + q % 2], (q + 1) * P
            e.eng.wait_ge(K.sem("fox_s_used"), i * QT + q + 1)
            nc.tensor.matmul(bank[:, 0:n], b.q[:, q * P:n], b.k[:, 0:n], start=True, stop=False)
            nc.tensor.matmul(bank[:, 0:n], b.sel[0:H8, :], b.neg_c[0:H8, 0:n], start=False, stop=False)
            nc.tensor.matmul(bank[:, q * P:n], K.ident_r[:, :], K.mask_r[:, P:2 * P], start=False, stop=True) \
                .then_inc(K.sem("fox_s_ready"), 1)

        def transposed(q):
            e.eng.wait_ge(K.sem("fox_p_ready"), i * QT + q + 1)
            e.eng.wait_ge(K.sem("fox_t_used"), i * 5 + q + 2)
            for t in range(q + 1):
                ins = nc.tensor.transpose(tb[:, t * P:(t + 1) * P], b.p[:, q % 2, t * P:(t + 1) * P], K.c("ident"))
            ins.then_inc(K.sem("fox_t_ready"), 1)

        scores(0)
        scores(1)
        job(e, c0 + 3, i)
        transposed(0)
        scores(2)
        transposed(1)
        scores(3)
        transposed(2)
        transposed(3)
        e.eng.wait_ge(K.sem("fox_t_used"), i * 5 + 6)
        e.eng.wait_ge(K.sem("fox_o_used"), i + 1)
        for t in range(QT):
            ins = nc.tensor.matmul(K.ps[OUT_BANK][:, t * P:S], b.v_tok[:, t, :], b.pt[:, t, t * P:S],
                                   start=t == 0, stop=t == QT - 1)
        ins.then_inc(K.sem("fox_o_ready"), 1)
    out_pe(e, "fox_out", "fox_y")


def fox_act(e):
    K, b, nc, c0, cf = e.K, fox_buffers(e.K), e.K.nc, FIRST_JOB["fox"], FIRST_JOB["fox_f"]
    prenorm_act(e, "fox")
    weight_high(e, cf + AHEAD)
    st = e.steps
    e.eng.wait_ge(K.sem("fox_x"), 1)
    st.step(nc.scalar.activation(b.e[0:H8, :], b.e[0:H8, :], ACT.Exp))
    st.wait()
    nc.scalar.activation(b.e[0:H8, :], b.e[0:H8, :], ACT.Ln, bias=K.c("ones")[0:H8, 0:1]).then_inc(K.sem("fox_ln"), 1)
    with e.eng.Fori(0, H8) as i:
        for r in range(4):
            weight_high(e, c0 + r + AHEAD, i)
            if r < 3:
                job_wait(e, c0 + r, i)
                nc.scalar.activation((b.q, b.k, b.v)[r], bank_of(e, c0 + r)[:, :], ACT.Copy,
                                     scale=P ** -0.5 if r == 0 else 1.0).then_inc(K.job_sems["bank"][(c0 + r) % SLOTS], 1)
        for q in range(QT):
            e.eng.wait_ge(K.sem("fox_nmax"), i * QT + q + 1)
            if q >= 2:
                e.eng.wait_ge(K.sem("fox_t_ready"), i * 5 + q)
            nc.scalar.activation(b.p[:, q % 2, 0:(q + 1) * P], K.ps[4 + q % 2][:, 0:(q + 1) * P], ACT.Exp,
                                 bias=b.nmax[:, q:q + 1], accum_out=b.sum[:, q:q + 1]).then_inc(K.sem("fox_e"), 1)
        job_wait(e, c0 + 3, i)
        nc.scalar.activation(b.z, bank_of(e, c0 + 3)[:, :], ACT.Silu).then_inc(K.job_sems["bank"][(c0 + 3) % SLOTS], 1)
        y_pair_scalar(e, "fox_y", i)
    ahead_act(e, "fox_out")


def fox_dve(e):
    K, b, nc, c0, cf, st = e.K, fox_buffers(e.K), e.K.nc, FIRST_JOB["fox"], FIRST_JOB["fox_f"], e.steps
    v = nc.vector
    prenorm_dve(e, "fox", "norm_w", DT, FIRST_JOB["fox_f"])
    job_wait(e, cf)
    x, ee, ncum = b.x[0:H8, :], b.e[0:H8, :], b.neg_c[0:H8, :]
    st.step(v.tensor_scalar(x, bank_of(e, cf)[0:H8, :], K.col("fox_b_f", 0)[0:H8, :], None, ALU.add))
    st.wait()
    release(e, cf)
    v.scalar_tensor_tensor(ee, x, -1.0, x, ALU.mult, ALU.min).then_inc(K.sem("fox_x"), 1)
    e.eng.wait_ge(K.sem("fox_x"), 1)
    st.step(v.tensor_scalar(x, x, 0.0, None, ALU.min))
    st.wait()
    e.eng.wait_ge(K.sem("fox_ln"), 1)
    st.step(v.tensor_tensor(x, ee, x, ALU.subtract))
    st.wait()
    v.tensor_tensor_scan(ncum, K.c("ones")[0:H8, :], x, 0.0, ALU.mult, ALU.add).then_inc(K.sem("fox_c"), 1)
    e.eng.wait_ge(K.sem("fox_c"), 1)
    e.eng.sem_inc(K.sem("fox_t_used"), 1)
    e.eng.sem_inc(K.sem("fox_s_used"), 2)
    e.eng.sem_inc(K.sem("fox_o_used"), 1)
    ident = K.c("ident")
    a0 = const_at("ident")
    tb = K.ps[TRANSPOSE_BANK]
    with e.eng.Fori(0, H8) as i:
        st.enter(i, 8)
        v.tensor_copy(b.sel[0:H8, :], K.const[0:H8, bass.ds(i + a0, 1)].broadcast_to([H8, P])).then_inc(K.sem("fox_sel"), 1)
        e.eng.wait_ge(K.sem("fox_t_ready"), i * 5 + 1)
        v.tensor_copy(b.v_tok, tb[:, :].rearrange("p (a b) -> p a b", a=QT)).then_inc(K.sem("fox_t_used"), 1)

        def top(q):
            e.eng.wait_ge(K.sem("fox_s_ready"), i * QT + q + 1)
            st.step(v.tensor_reduce(b.mx[:, q:q + 1], K.ps[4 + q % 2][:, 0:(q + 1) * P], AX.X, ALU.max))
            st.wait()
            v.tensor_scalar(b.nmax[:, q:q + 1], b.mx[:, q:q + 1], -1.0, None, ALU.mult).then_inc(K.sem("fox_nmax"), 1)

        def share(q):
            e.eng.wait_ge(K.sem("fox_e"), i * QT + q + 1)
            e.eng.sem_inc(K.sem("fox_s_used"), 1)
            st.step(v.reciprocal(b.rec[:, q:q + 1], b.sum[:, q:q + 1]))
            st.wait()
            p = b.p[:, q % 2, 0:(q + 1) * P]
            v.tensor_scalar(p, p, b.rec[:, q:q + 1], None, ALU.mult).then_inc(K.sem("fox_p_ready"), 1)

        def evacuate(q):
            e.eng.wait_ge(K.sem("fox_t_ready"), i * 5 + q + 2)
            v.tensor_copy(b.pt[:, 0:q + 1, q * P:(q + 1) * P],
                          tb[:, 0:(q + 1) * P].rearrange("p (a b) -> p a b", b=P)).then_inc(K.sem("fox_t_used"), 1)

        for step, q in ((top, 0), (top, 1), (share, 0), (evacuate, 0), (top, 2), (share, 1), (evacuate, 1),
                        (top, 3), (share, 2), (evacuate, 2), (share, 3), (evacuate, 3)):
            step(q)
        e.eng.wait_ge(K.sem("fox_o_ready"), i + 1)
        evacuated(e, c0 + 3, i)
        e.eng.wait_ge(K.sem("split_done"), i + FIRST_SPLIT["fox_y"])
        v.tensor_tensor(K.y[:, 0, :], K.ps[OUT_BANK][:, :], b.z, ALU.mult).then_inc(K.sem("y_done"), 1)
        y_pair_vector(e, "fox_y", i)
        e.eng.sem_inc(K.sem("fox_o_used"), 1)
        st.leave(H8)
    out_residual_dve(e, "fox_out")


def const_at(name):
    n = 0
    for k, a in const_layout().items():
        if k == name:
            return n
        n += a.shape[1]


class Ring:

    def __init__(self, e, name, banks, uses):
        self.e, self.banks, self.uses = e, banks, list(uses)
        self.ready = e.K.sem(name + "_ready")
        self.free = [e.K.sem(f"{name}_free{b}") for b in banks]

    def find(self, use):
        u = self.uses.index(use)
        b = u % len(self.banks)
        per_trip = len(range(b, len(self.uses), len(self.banks)))
        return u, b, u // len(self.banks), per_trip

    def bank(self, use):
        return self.e.K.ps[self.banks[self.find(use)[1]]]

    def begin(self):
        for f in self.free:
            self.e.eng.sem_inc(f, 1)

    def claim(self, use, i):
        _, b, k, per = self.find(use)
        self.e.eng.wait_ge(self.free[b], i * per + k + 1)

    def written(self, ins):
        ins.then_inc(self.ready, 1)

    def wait(self, use, i):
        self.e.eng.wait_ge(self.ready, i * len(self.uses) + self.find(use)[0] + 1)

    def read(self, use, ins):
        ins.then_inc(self.free[self.find(use)[1]], 1)

    def wait_read(self, use, i):
        _, b, k, per = self.find(use)
        self.e.eng.wait_ge(self.free[b], i * per + k + 2)


def job_with_waits(e, c, i, tiles, split, skip=0):
    parts = job_parts(e, c, i, tiles)
    for k in range(len(tiles)):
        split_wait(e, split, k + 1 + skip)
        next(parts)


def job_parts(e, c, i=None, tiles=A_TILES):
    K, s, dst = e.K, c % SLOTS, bank_of(e, c)[:, :]
    job_start(e, c, i)
    for k, t in enumerate(tiles):
        wh, wl = K.w_hi[:, s, k * P:(k + 1) * P], K.w_lo[:, s, k * P:(k + 1) * P]
        K.nc.tensor.matmul(dst, wh, K.act_hi[:, t, :], start=k == 0, stop=False)
        K.nc.tensor.matmul(dst, wh, K.act_lo[:, t, :], start=False, stop=False)
        ins = K.nc.tensor.matmul(dst, wl, K.act_hi[:, t, :], start=False, stop=k == len(tiles) - 1)
        if k == len(tiles) - 1:
            ins.then_inc(K.job_sems["done"], 1)
        yield


def take(parts, n):
    for _ in range(n):
        next(parts, None)


def all_parts(*gens):
    for g in gens:
        yield from g


GDN_LEVELS = range(1, 6)
GDN_USES = (["q_norm", "k_norm", "beta", "grow", "gi", "gram", "qk", "kt0", "kt1", "vt0", "vt1", "t1"]
            + [f"{w}{l}" for l in GDN_LEVELS for w in ("w", "ds", "dt") if (w, l) != ("dt", 5)]
            + ["wt"] + [f"{w}{c}" for c in range(NCH) for w in ("v", "k") if (w, c) != ("k", NCH - 1)] + ["o_norm"])


def gdn_buffers(K):
    b = Names()
    (b.u, b.t, b.x, b.taps, b.sel, b.bg, b.eg, b.tok, b.f1, b.hb, b.hg, b.hf, b.egl, b.ea, b.umat, b.um1, b.s, b.tt,
     b.qkt, b.nwt, b.vn, b.st) = carve(
        K, (3, 516), (3, S), (3, S), (12,), (P,), (S,), (S,), (NCH, 64), (NCH, H8), (NCH,), (NCH,), (NCH,), (NCH,),
        (2,), (S,), (S,), (S,), (S,), (S,), (S,), (2, P), (2, P))
    b.um = [K.root, b.um1]
    b.w, b.z, b.dt = K.rstd, K.sq[:, 0, :], K.sq[:, 1, :]
    m = K.M[:, :, :].rearrange("p a b -> p (a b)")
    b.kbe, b.kd, b.vb = (m[0:CH, k * 1024:(k + 1) * 1024].rearrange("p (a b) -> p a b", b=P) for k in range(3))
    b.qd, b.o = m[:, 3072:3584], m[:, 3584:4096]
    return b


def by_chunk(a):
    return a.rearrange("p (c j) -> p c j", j=CH)


def chunk(a, c):
    return a[:, c * CH:(c + 1) * CH]


def gdn_pe(e):
    K, b, nc, c0, mm = e.K, gdn_buffers(e.K), e.K.nc, FIRST_JOB["gdn"], e.K.nc.tensor.matmul
    ring = Ring(e, "gdn_aux", (4, 5, 6), GDN_USES)
    ident, ones = K.c("ident"), K.c("ones")[:, 0:P]
    prenorm_pe(e, "gdn")
    job(e, FIRST_JOB["gdn_ba"])
    e.eng.wait_ge(K.sem("gdn_gates"), 1)
    for c in range(NCH):
        ins = nc.tensor.transpose(K.ps[4][0:CH, c * CH:(c + 1) * CH], chunk(b.bg, c)[0:CH, :], ident[0:CH, 0:CH])
    ins.then_inc(K.sem("gdn_gates_t"), 1)
    e.eng.wait_ge(K.sem("gdn_begin"), 1)
    for r in range(3):
        job(e, c0 + r)

    def head(i, more):
        S_, T_, U_ = b.s[0:CH, :], b.tt[0:CH, :], [u[0:CH, :] for u in b.um]

        def bank64(use):
            return ring.bank(use)[0:CH, :]

        zjob = job_parts(e, c0 + 3, i)
        take(zjob, 3)
        e.eng.wait_ge(K.sem("gdn_head"), i + 1)
        ring_order = []
        for part, use in ((0, "q_norm"), (1, "k_norm")):
            e.eng.wait_ge(K.sem("gdn_square"), i * 2 + part + 1)
            ring.claim(use, i)
            ring.written(mm(ring.bank(use)[:, :], ones, b.t[:, part, :], start=True, stop=True))
        ring.claim("beta", i)
        settle(e)
        ring.written(mm(bank64("beta"), b.sel[0:H8, 0:CH], b.bg[0:H8, :], start=True, stop=True))
        ring.claim("grow", i)
        ring.written(mm(ring.bank("grow")[:, :], b.sel[32:40, :], b.eg[32:40, :], start=True, stop=True))
        ring.claim("gi", i)
        settle(e)
        ring.written(mm(bank64("gi"), b.sel[32:40, 0:CH], b.bg[32:40, :], start=True, stop=True))
        e.eng.wait_ge(K.sem("gdn_normed"), i * 2 + 2)
        for use, rhs in (("gram", 1), ("qk", 0)):
            ring.claim(use, i)
            settle(e)
            for c in range(NCH):
                ins = mm(chunk(bank64(use), c), chunk(b.x[:, 1, :], c), chunk(b.x[:, rhs, :], c), start=True, stop=True)
            ring.written(ins)
        for use, part in (("kt0", 1), ("kt1", 1), ("vt0", 2), ("vt1", 2)):
            ring.claim(use, i)
            settle(e)
            for c in range(4):
                cc = c + (4 if use[-1] == "1" else 0)
                ins = nc.tensor.transpose(ring.bank(use)[0:CH, c * P:(c + 1) * P], chunk(b.x[:, part, :], cc), ident)
            ring.written(ins)
        e.eng.wait_ge(K.sem("gdn_s"), i * 6 + 1)
        ring.claim("t1", i)
        settle(e)
        for c in range(NCH):
            ins = nc.tensor.transpose(chunk(bank64("t1"), c), chunk(S_, c), ident[0:CH, 0:CH])
        ring.written(ins)
        for l in GDN_LEVELS:
            e.eng.wait_ge(K.sem("gdn_um"), i * 5 + l)
            if l == 1:
                ring.wait_read("t1", i)
            else:
                e.eng.wait_ge(K.sem("gdn_s"), i * 6 + l)
            ring.claim(f"w{l}", i)
            settle(e)
            for c in range(NCH):
                ins = mm(chunk(bank64(f"w{l}"), c), chunk(U_[l % 2], c), chunk(T_, c), start=True, stop=True)
            ring.written(ins)
            take(zjob, 1)
            ring.wait_read(f"w{l}", i)
            W = b.w[0:CH, :]
            for use, lhs, rhs in ((f"ds{l}", W, S_), (f"dt{l}", S_, W)):
                if use in GDN_USES:
                    ring.claim(use, i)
                    settle(e)
                    for c in range(NCH):
                        ins = mm(chunk(bank64(use), c), chunk(lhs, c), chunk(rhs, c), start=True, stop=True)
                    ring.written(ins)
        take(zjob, 8)
        e.eng.wait_ge(K.sem("gdn_s"), i * 6 + 6)
        ring.claim("wt", i)
        e.eng.wait_ge(K.sem("gdn_tok"), i + 1)
        settle(e)
        for c in range(NCH):
            ins = mm(chunk(ring.bank("wt"), c), b.kbe[:, c, :], chunk(S_, c), start=True, stop=True)
        ring.written(ins)
        nxt = all_parts(*[job_parts(e, c0 + 4 + r, i) for r in range(3)]) if more else iter(())
        take(nxt, 1)
        e.eng.wait_ge(K.sem("gdn_o_free"), i + 1)
        O = K.ps[7]
        for c in range(NCH):
            st = b.st[:, c % 2, :]
            ring.claim(f"v{c}", i)
            vb = ring.bank(f"v{c}")[0:CH, 0:P]
            settle(e)
            ins = mm(vb, chunk(S_, c), b.vb[:, c, :], start=True, stop=c == 0)
            if c == 0:
                ring.wait_read("wt", i)
            else:
                ring.wait_read(f"k{c - 1}", i)
                settle(e)
                ins = mm(vb, chunk(b.nwt, c), st, start=False, stop=True)
            ring.written(ins)
            take(nxt, 1 + c % 2)
            if c:
                mm(chunk(O, c), st, chunk(b.qd, c), start=True, stop=False)
            ring.wait_read(f"v{c}", i)
            vn = b.vn[0:CH, c % 2, :]
            settle(e)
            if c < NCH - 1:
                ring.claim(f"k{c}", i)
                settle(e)
                ring.written(mm(ring.bank(f"k{c}")[:, 0:P], b.kd[:, c, :], vn, start=True, stop=True))
            ins = mm(chunk(O, c), vn, chunk(b.qkt[0:CH, :], c), start=c == 0, stop=True)
            take(nxt, 1 + c % 2)
        ins.then_inc(K.sem("gdn_o"), 1)
        take(nxt, 24)
        e.eng.wait_ge(K.sem("gdn_o_square"), i + 1)
        ring.claim("o_norm", i)
        ring.written(mm(ring.bank("o_norm")[:, :], ones, b.o, start=True, stop=True))

    with e.eng.Fori(0, H8 - 1) as i:
        head(i, True)
    head(H8 - 1, False)
    out_pe(e, "gdn_out", "gdn_y")


def gdn_act(e):
    K, b, nc, c0, st = e.K, gdn_buffers(e.K), e.K.nc, FIRST_JOB["gdn"], e.steps
    act = nc.scalar.activation
    ring = Ring(e, "gdn_aux", (4, 5, 6), GDN_USES)
    prenorm_act(e, "gdn")
    cb = FIRST_JOB["gdn_ba"]
    weight_high(e, cb + AHEAD)
    job_wait(e, cb)
    one = K.c("ones")[:, 0:1]
    act(b.bg[0:H8, :], bank_of(e, cb)[0:H8, :], ACT.Exp, scale=-1.0).then_inc(K.sem("gdn_beta_e"), 1)
    st.step(act(b.ea[32:40, 0:1], K.col("gdn_a_log", 0)[32:40, :], ACT.Exp))
    e.eng.wait_ge(K.sem("gdn_dt"), 1)
    st.step(act(b.eg[32:40, :], b.eg[32:40, :], ACT.Exp))
    st.wait()
    act(b.eg[32:40, :], b.eg[32:40, :], ACT.Ln, bias=one[32:40, :]).then_inc(K.sem("gdn_ln"), 1)
    e.eng.wait_ge(K.sem("gdn_gates"), 1)
    st.step(act(b.eg[32:40, :], b.bg[32:40, :], ACT.Exp))
    e.eng.wait_ge(K.sem("gdn_tok_in"), 1)
    st.wait()
    act(b.f1[0:CH], b.tok[0:CH, :, 32:40], ACT.Exp).then_inc(K.sem("gdn_f1_e"), 1)

    def fetch(r, i=None):
        c = c0 + r
        weight_high(e, c + AHEAD, i)
        job_wait(e, c, i)
        act(b.u[:, r % 4, 3:515], bank_of(e, c)[:, :], ACT.Copy).then_inc(K.job_sems["bank"][c % SLOTS], 1)

    for r in range(3):
        fetch(r)

    def head(i, more):
        weight_high(e, c0 + 3 + AHEAD, i)
        for part in range(3):
            e.eng.wait_ge(K.sem("gdn_conv"), i * 3 + part + 1)
            act(b.x[:, part, :], b.t[:, part, :], ACT.Silu).then_inc(K.sem("gdn_silu"), 1)
        for part in range(2):
            e.eng.wait_ge(K.sem("gdn_silu"), i * 3 + 3)
            act(b.t[:, part, :], b.x[:, part, :], ACT.Square).then_inc(K.sem("gdn_square"), 1)
        for part, use in ((0, "q_norm"), (1, "k_norm")):
            ring.wait(use, i)
            ring.read(use, act(b.t[:, part, :], ring.bank(use)[:, :], ACT.Ln, bias=K.c("eps")))
        for part, use in ((0, "q_norm"), (1, "k_norm")):
            ring.wait_read(use, i)
            act(b.t[:, part, :], b.t[:, part, :], ACT.Exp, scale=-0.5).then_inc(K.sem("gdn_rstd"), 1)
        e.eng.wait_ge(K.sem("gdn_decay_in"), i + 1)
        act(b.dt[0:CH, :], b.dt[0:CH, :], ACT.Exp).then_inc(K.sem("gdn_decay"), 1)
        ring.wait("t1", i)
        ring.read("t1", act(b.tt[0:CH, :], ring.bank("t1")[0:CH, :], ACT.Copy))
        for l in GDN_LEVELS:
            ring.wait(f"w{l}", i)
            ring.read(f"w{l}", act(b.w[0:CH, :], ring.bank(f"w{l}")[0:CH, :], ACT.Copy))
        ring.wait("wt", i)
        ring.read("wt", act(b.nwt, ring.bank("wt")[:, :], ACT.Copy, scale=-1.0))
        job_wait(e, c0 + 3, i)
        act(b.z, bank_of(e, c0 + 3)[:, :], ACT.Silu).then_inc(K.job_sems["bank"][(c0 + 3) % SLOTS], 1)
        if more:
            for r in range(3):
                weight_high(e, c0 + 4 + r + AHEAD, i)
                job_wait(e, c0 + 4 + r, i)
                act(b.u[:, r, 3:515], bank_of(e, c0 + 4 + r)[:, :], ACT.Copy) \
                    .then_inc(K.job_sems["bank"][(c0 + 4 + r) % SLOTS], 1)
        e.eng.wait_ge(K.sem("gdn_o"), i + 1)
        act(b.o, K.ps[7][:, :], ACT.Square, scale=P ** -0.5).then_inc(K.sem("gdn_o_square"), 1)
        ring.wait("o_norm", i)
        ring.read("o_norm", act(b.o, ring.bank("o_norm")[:, :], ACT.Ln, bias=K.c("eps")))
        ring.wait_read("o_norm", i)
        act(b.o, b.o, ACT.Exp, scale=-0.5).then_inc(K.sem("gdn_o_rstd"), 1)
        y_pair_scalar(e, "gdn_y", i)

    with e.eng.Fori(0, H8 - 1) as i:
        head(i, True)
    head(H8 - 1, False)
    ahead_act(e, "gdn_out")


def gdn_dve(e):
    K, b, nc, c0, st, v = e.K, gdn_buffers(e.K), e.K.nc, FIRST_JOB["gdn"], e.steps, e.K.nc.vector
    ring = Ring(e, "gdn_aux", (4, 5, 6), GDN_USES)
    cb = FIRST_JOB["gdn_ba"]
    prenorm_dve(e, "gdn", "norm_w", 2 * DT, cb)
    st.step(v.memset(b.u[:, :, 0:3], 0.0))
    st.wait()
    e.eng.wait_ge(K.sem("gdn_beta_e"), 1)
    st.step(v.tensor_scalar(b.bg[0:H8, :], b.bg[0:H8, :], 1.0, None, ALU.add))
    st.step(v.memset(b.umat[0:CH, :], 0.0))
    st.wait()
    st.step(v.reciprocal(b.umat[0:H8, :], b.bg[0:H8, :]))
    x, eg, g = b.s[32:40, :], b.eg[32:40, :], b.umat[32:40, :]
    st.step(v.tensor_scalar(x, bank_of(e, cb)[32:40, :], K.col("gdn_dt_bias", 0)[32:40, :], None, ALU.add))
    st.wait()
    release(e, cb)
    v.scalar_tensor_tensor(eg, x, -1.0, x, ALU.mult, ALU.min).then_inc(K.sem("gdn_dt"), 1)
    e.eng.wait_ge(K.sem("gdn_dt"), 1)
    st.step(v.tensor_scalar(x, x, 0.0, None, ALU.max))
    st.wait()
    e.eng.wait_ge(K.sem("gdn_ln"), 1)
    st.step(v.tensor_tensor(x, x, eg, ALU.add))
    st.wait()
    st.step(v.tensor_scalar(x, x, b.ea[32:40, 0:1], -1.0, ALU.mult, ALU.mult))
    st.wait()
    st.step(v.tensor_tensor_scan(g, K.c("restart")[32:40, :], x, 0.0, ALU.mult, ALU.add))
    st.wait()
    v.tensor_copy(b.bg[0:CH, :], b.umat[0:CH, :]).then_inc(K.sem("gdn_gates"), 1)
    e.eng.wait_ge(K.sem("gdn_gates_t"), 1)
    tok = b.tok[0:CH]
    v.tensor_copy(tok, by_chunk(K.ps[4][0:CH, :])).then_inc(K.sem("gdn_tok_in"), 1)
    e.eng.wait_ge(K.sem("gdn_f1_e"), 1)
    v.tensor_tensor(b.f1[0:CH], b.f1[0:CH], tok[:, :, 0:H8], ALU.mult).then_inc(K.sem("gdn_begin"), 1)
    e.eng.wait_ge(K.sem("gdn_begin"), 1)
    ring.begin()
    e.eng.sem_inc(K.sem("gdn_o_free"), 1)
    n_ident = const_at("ident")

    def bc(a, n=CH):
        return a.unsqueeze(2).broadcast_to([CH, a.shape[1], n])

    def each(name):
        return K.c(name)[0:CH, 0:CH].unsqueeze(1).broadcast_to([CH, NCH, CH])

    def head(i, more):
        def step(ins):
            st.step(ins)
            st.wait()

        step(v.tensor_copy(b.taps, K.param[:, bass.ds(i * 12 + K.cols["gdn_w_conv"], 12)]))
        st.step(v.tensor_copy(b.sel[0:H8, :], K.const[0:H8, bass.ds(i + n_ident, 1)].broadcast_to([H8, P])))
        st.step(v.tensor_copy(b.sel[32:40, :], K.const[32:40, bass.ds(i + n_ident + 32, 1)].broadcast_to([H8, P])))
        st.step(v.tensor_copy(b.hb[0:CH, :].unsqueeze(2), tok[:, :, bass.ds(i, 1)]))
        st.step(v.tensor_copy(b.hg[0:CH, :].unsqueeze(2), tok[:, :, bass.ds(i + 32, 1)]))
        step(v.tensor_copy(b.hf[0:CH, :].unsqueeze(2), b.f1[0:CH, :, bass.ds(i, 1)]))
        e.eng.sem_inc(K.sem("gdn_head"), 1)
        for part in range(3):
            evacuated(e, c0 + part, i)
            u, t = b.u[:, part, :], b.t[:, part, :]
            step(v.tensor_scalar(t, u[:, 0:S], b.taps[:, 4 * part:4 * part + 1], None, ALU.mult))
            for n in range(1, 4):
                ins = v.scalar_tensor_tensor(t, u[:, n:n + S], b.taps[:, 4 * part + n:4 * part + n + 1], t,
                                             ALU.mult, ALU.add)
                if n < 3:
                    step(ins)
            ins.then_inc(K.sem("gdn_conv"), 1)
        for part, use in ((0, "q_norm"), (1, "k_norm")):
            e.eng.wait_ge(K.sem("gdn_rstd"), i * 2 + part + 1)
            v.scalar_tensor_tensor(b.x[:, part, :], b.x[:, part, :], P ** -0.5 if part == 0 else 1.0, b.t[:, part, :],
                                   ALU.mult, ALU.mult).then_inc(K.sem("gdn_normed"), 1)
        dt = by_chunk(b.dt[0:CH, :])
        ring.wait("grow", i)
        e.eng.wait_ge(K.sem("gdn_normed"), i * 2 + 2)
        step(v.tensor_copy(b.egl[:, :].unsqueeze(2), by_chunk(ring.bank("grow")[:, :])[:, :, CH - 1:CH]))
        ring.wait("gi", i)
        ring.read("gi", v.tensor_tensor(dt, by_chunk(ring.bank("gi")[0:CH, :]), bc(b.hg[0:CH, :]), ALU.subtract))
        ring.wait_read("gi", i)
        v.tensor_tensor(dt, dt, each("upto_neg"), ALU.add).then_inc(K.sem("gdn_decay_in"), 1)
        ring.read("grow", v.tensor_tensor(b.qd, b.x[:, 0, :], ring.bank("grow")[:, :], ALU.mult))
        e.eng.wait_ge(K.sem("gdn_decay"), i + 1)
        um = by_chunk(b.umat[0:CH, :])
        ring.read("beta", v.tensor_tensor(um, dt, by_chunk(ring.bank("beta")[0:CH, :]), ALU.mult))
        ring.wait_read("beta", i)
        ring.wait("gram", i)
        ring.read("gram", v.tensor_tensor(um, um, by_chunk(ring.bank("gram")[0:CH, :]), ALU.mult))
        ring.wait_read("gram", i)
        ring.wait("qk", i)
        ring.read("qk", v.tensor_tensor(by_chunk(b.qkt[0:CH, :]), by_chunk(ring.bank("qk")[0:CH, :]), dt, ALU.mult))
        S_, T_ = by_chunk(b.s[0:CH, :]), by_chunk(b.tt[0:CH, :])
        U_ = [by_chunk(u[0:CH, :]) for u in b.um]
        step(v.tensor_tensor(U_[0], um, each("level0"), ALU.mult))
        v.tensor_tensor(S_, each("ident"), U_[0], ALU.subtract).then_inc(K.sem("gdn_s"), 1)
        e.eng.wait_ge(K.sem("gdn_s"), i * 6 + 1)
        v.tensor_tensor(U_[1], um, each("level1"), ALU.mult).then_inc(K.sem("gdn_um"), 1)
        for half in range(2):
            cs = slice(4 * half, 4 * half + 4)
            use = f"kt{half}"
            ring.wait(use, i)
            src = ring.bank(use)[0:CH, :].rearrange("p (c d) -> p c d", d=P)
            step(v.tensor_tensor(b.kbe[:, cs, :], src, bc(b.hf[0:CH, cs], P), ALU.mult))
            last = dt[:, cs, CH - 1:CH].broadcast_to([CH, 4, P])
            ring.read(use, v.tensor_tensor(b.kd[:, cs, :], src, last, ALU.mult))
            ring.wait_read(use, i)
        for half in range(2):
            cs = slice(4 * half, 4 * half + 4)
            use = f"vt{half}"
            ring.wait(use, i)
            src = ring.bank(use)[0:CH, :].rearrange("p (c d) -> p c d", d=P)
            ring.read(use, v.tensor_tensor(b.vb[:, cs, :], src, bc(b.hb[0:CH, cs], P), ALU.mult))
            ring.wait_read(use, i)
        ring.wait_read("grow", i)
        ring.wait_read("qk", i)
        e.eng.sem_inc(K.sem("gdn_tok"), 1)
        for l in GDN_LEVELS:
            if l < 5:
                if l >= 2:
                    ring.wait(f"w{l - 1}", i)
                v.tensor_tensor(U_[(l + 1) % 2], um, each(f"level{l + 1}"), ALU.mult).then_inc(K.sem("gdn_um"), 1)
                ring.wait(f"dt{l}", i)
                ring.wait_read(f"w{l}", i)
                ring.read(f"ds{l}", v.tensor_tensor(b.s[0:CH, :], b.s[0:CH, :], ring.bank(f"ds{l}")[0:CH, :], ALU.subtract))
                ring.read(f"dt{l}", v.tensor_tensor(b.tt[0:CH, :], b.tt[0:CH, :], ring.bank(f"dt{l}")[0:CH, :],
                                                    ALU.subtract))
                ring.wait_read(f"ds{l}", i)
                ring.wait_read(f"dt{l}", i)
            else:
                ring.wait(f"ds{l}", i)
                ring.read(f"ds{l}", v.tensor_tensor(b.s[0:CH, :], b.s[0:CH, :], ring.bank(f"ds{l}")[0:CH, :], ALU.subtract))
                ring.wait_read(f"ds{l}", i)
            e.eng.sem_inc(K.sem("gdn_s"), 1)
        for c in range(NCH):
            ring.wait(f"v{c}", i)
            ring.read(f"v{c}", v.tensor_copy(b.vn[0:CH, c % 2, :], ring.bank(f"v{c}")[0:CH, 0:P]))
            if c < NCH - 1:
                ring.wait(f"k{c}", i)
                src, new = ring.bank(f"k{c}")[:, 0:P], b.st[:, (c + 1) % 2, :]
                if c == 0:
                    ins = v.tensor_copy(new, src)
                else:
                    ring.wait_read(f"k{c - 1}", i)
                    ins = v.scalar_tensor_tensor(new, b.st[:, c % 2, :], b.egl[:, c:c + 1], src, ALU.mult, ALU.add)
                ring.read(f"k{c}", ins)
        e.eng.wait_ge(K.sem("gdn_o_rstd"), i + 1)
        step(v.scalar_tensor_tensor(b.o, K.ps[7][:, :], K.col("gdn_norm_w", 0), b.o, ALU.mult, ALU.mult))
        e.eng.sem_inc(K.sem("gdn_o_free"), 1)
        evacuated(e, c0 + 3, i)
        e.eng.wait_ge(K.sem("split_done"), i + FIRST_SPLIT["gdn_y"])
        v.tensor_tensor(K.y[:, 0, :], b.o, b.z, ALU.mult).then_inc(K.sem("y_done"), 1)
        y_pair_vector(e, "gdn_y", i)

    with e.eng.Fori(0, H8 - 1) as i:
        st.enter(i, GDN_STEPS)
        head(i, True)
        st.leave(H8 - 1)
    head(H8 - 1, False)
    out_residual_dve(e, "gdn_out")


GDN_STEPS = 20


TWO_PI_HI = 6.28125
TWO_PI_LO = 2.0 * math.pi - TWO_PI_HI
PI_BELOW = 3.1415925


def rope_angles(e, freq, cos, sin, n_before):
    K, v = e.K, e.K.nc.vector
    e.eng.wait_ge(K.sem("position"), 16 * (n_before + 1))
    ints = K.root[:, :].bitcast(I32)

    def step(ins):
        e.steps.step(ins)
        e.steps.wait()

    ang, turns = K.sq[:, 0, :], K.sq[:, 1, :]
    step(v.tensor_copy(ang, ints))
    step(v.tensor_scalar(ang, ang, K.c(freq), None, ALU.mult))
    for out, quarter in ((sin, 0.0), (cos, 0.25)):
        step(v.tensor_scalar(turns, ang, 1.0 / (2.0 * math.pi), quarter, ALU.mult, ALU.add))
        step(v.tensor_copy(ints, turns))
        step(v.tensor_copy(turns, ints))
        step(v.scalar_tensor_tensor(out, turns, -TWO_PI_HI, ang, ALU.mult, ALU.add))
        step(v.scalar_tensor_tensor(out, turns, -TWO_PI_LO, out, ALU.mult, ALU.add))
        if quarter:
            step(v.tensor_scalar(out, out, math.pi / 2, None, ALU.add))
        step(v.tensor_scalar(out, out, PI_BELOW, -PI_BELOW, ALU.min, ALU.max))
    e.eng.sem_inc(K.sem("angles"), 1)


def fetch_positions(e, source, n_before):
    e.eng.wait_ge(e.K.sem("position_room"), n_before + 1)
    e.eng.dma_start(e.K.root[:, :].bitcast(I32), source.broadcast_to([P, S])).then_inc(e.K.sem("position"), 16)


def rope_sines(e, cos, sin, n_before):
    e.eng.wait_ge(e.K.sem("angles"), n_before + 1)
    e.K.nc.scalar.activation(sin, sin, ACT.Sin).then_inc(e.K.sem("tables"), 1)
    e.K.nc.scalar.activation(cos, cos, ACT.Sin).then_inc(e.K.sem("tables"), 1)


SWA_G = [f"{w}_{s}" for s in range(2) for w in ("rot", "s00", "s01", "s10", "s11", "t00", "t01", "t10", "t11", "o")]
BLOCKS = [(0, 1), (1, 0), (1, 1), (2, 0), (2, 1), (3, 0), (3, 1)]


def swa_buffers(K):
    b = Names()
    (b.cos, b.sin, b.k, b.kr, b.v, b.q, b.qr, b.rot, b.z, b.v_tok, b.p0, b.p1, b.pt0, b.pt1, b.mx, b.es, b.sum, b.rec) = carve(
        K, (S,), (S,), (S,), (S,), (S,), (S,), (S,), (S,), (S,), (QT, P), (QT, 256), (QT, 256), (7, P), (7, P), (8,),
        (8,), (8,), (8,))
    return b


def swa_pe(e):
    K, b, nc, mm = e.K, swa_buffers(e.K), e.K.nc, e.K.nc.tensor.matmul
    ring, kv = Ring(e, "swa_aux", (4, 5, 6, 7), SWA_G), Ring(e, "swa_kv", (4, 5), ["rot", "v"])
    ident = K.c("ident")
    prenorm_pe(e, "swa")
    for p in range(2):
        c0 = FIRST_JOB[f"swa{p}"]
        job(e, c0)
        job(e, c0 + 1)
        if p:
            for use in SWA_G[-4:]:
                ring.wait_read(use, 2 * p - 1)
        evacuated(e, c0)
        kv.claim("rot", p)
        kv.written(mm(kv.bank("rot")[:, :], K.c("rotate"), b.k, start=True, stop=True))
        evacuated(e, c0 + 1)
        kv.claim("v", p)
        for t in range(QT):
            ins = nc.tensor.transpose(kv.bank("v")[:, t * P:(t + 1) * P], b.v[:, t * P:(t + 1) * P], ident)
        kv.written(ins)
        kv.wait_read("rot", p)
        kv.wait_read("v", p)
        with e.eng.Fori(0, 2) as i:
            for s in range(2):
                trip, c, use = i + 2 * p, c0 + 2 + 2 * s, lambda name: f"{name}_{s}"
                job(e, c, i)
                evacuated(e, c, i)
                ring.claim(use("rot"), trip)
                ring.written(mm(ring.bank(use("rot"))[:, :], K.c("rotate"), b.q, start=True, stop=True))
                job(e, c + 1, i)
                e.eng.wait_ge(K.sem("swa_q"), trip * 2 + s + 1)
                settle(e)
                for half in range(2):
                    rows = slice(64 * half, 64 * half + 64)
                    for pair in range(2):
                        u = use(f"s{half}{pair}")
                        ring.claim(u, trip)
                        settle(e)
                        for q in (2 * pair, 2 * pair + 1):
                            first = P if q == 0 else 0
                            dst = ring.bank(u)[:, (q % 2) * 256 + first:(q % 2) * 256 + 256]
                            mm(dst, b.qr[rows, q * P:(q + 1) * P], b.kr[rows, (q - 1) * P + first:(q + 1) * P],
                               start=True, stop=False)
                            ins = mm(dst, K.ident_r[:, :], K.mask_r[:, first:2 * P], start=False, stop=True)
                        ring.written(ins)
                for half in range(2):
                    e.eng.wait_ge(K.sem("swa_p"), trip * 4 + 2 * s + half + 1)
                    for n, (q, own) in enumerate(BLOCKS):
                        u = use(f"t{half}{n // 4}")
                        if n % 4 == 0:
                            ring.claim(u, trip)
                        ins = nc.tensor.transpose(ring.bank(u)[:, (n % 4) * P:(n % 4 + 1) * P],
                                                  (b.p0, b.p1)[half][:, q, own * P:(own + 1) * P], ident)
                        if n in (3, 6):
                            ring.written(ins)
                ring.claim(use("o"), trip)
                for half in range(2):
                    ring.wait_read(use(f"t{half}0"), trip)
                    ring.wait_read(use(f"t{half}1"), trip)
                    rows = slice(64 * half, 64 * half + 64)
                    settle(e)
                    for n, (q, own) in enumerate(BLOCKS):
                        ins = mm(ring.bank(use("o"))[rows, q * P:(q + 1) * P], b.v_tok[:, q - 1 + own, rows],
                                 (b.pt0, b.pt1)[half][:, n, :], start=own == 0 or q == 0, stop=own == 1)
                ring.written(ins)
    out_pe(e, "swa_out", "swa_y")


def swa_act(e):
    K, b, act = e.K, swa_buffers(e.K), e.K.nc.scalar.activation
    ring = Ring(e, "swa_aux", (4, 5, 6, 7), SWA_G)
    prenorm_act(e, "swa")
    fetch_positions(e, K.positions, 0)
    rope_sines(e, b.cos, b.sin, 0)

    def evacuate(c, dst, i=None, func=ACT.Copy, scale=1.0):
        job_wait(e, c, i)
        act(dst, bank_of(e, c)[:, :], func, scale=scale).then_inc(K.job_sems["bank"][c % SLOTS], 1)

    for p in range(2):
        c0 = FIRST_JOB[f"swa{p}"]
        weight_high(e, c0 + AHEAD)
        weight_high(e, c0 + 1 + AHEAD)
        evacuate(c0, b.k)
        evacuate(c0 + 1, b.v)
        with e.eng.Fori(0, 2) as i:
            for s in range(2):
                trip, c, use = i + 2 * p, c0 + 2 + 2 * s, lambda name: f"{name}_{s}"
                weight_high(e, c + AHEAD, i)
                evacuate(c, b.q, i, scale=64 ** -0.5)
                weight_high(e, c + 1 + AHEAD, i)
                for half in range(2):
                    ph = (b.p0, b.p1)[half]
                    e.eng.wait_ge(K.sem("swa_max"), trip * 4 + 2 * s + half + 1)
                    for q in range(QT):
                        first = P if q == 0 else 0
                        j = 4 * half + q
                        act(ph[:, q, first:256], ring.bank(use(f"s{half}{q // 2}"))[:, (q % 2) * 256 + first:(q % 2) * 256 + 256],
                            ACT.Exp, bias=b.mx[:, j:j + 1], accum_out=b.sum[:, j:j + 1]).then_inc(K.sem("swa_e"), 1)
                    act(b.es[:, 4 * half:4 * half + 4], b.es[:, 4 * half:4 * half + 4], ACT.Exp).then_inc(K.sem("swa_e"), 1)
                evacuate(c + 1, b.z, i, ACT.Silu)
                t = i * 2 + s + 4 * p
                y_pair_scalar(e, "swa_y", t)
    ahead_act(e, "swa_out")


def swa_dve(e):
    K, b, nc, st, v = e.K, swa_buffers(e.K), e.K.nc, e.steps, e.K.nc.vector
    ring, kv = Ring(e, "swa_aux", (4, 5, 6, 7), SWA_G), Ring(e, "swa_kv", (4, 5), ["rot", "v"])
    prenorm_dve(e, "swa", "norm_w", 3 * DT, FIRST_JOB["swa0"])
    e.eng.sem_inc(K.sem("position_room"), 1)
    rope_angles(e, "swa_freq", b.cos, b.sin, 0)
    ring.begin()
    kv.begin()
    e.eng.wait_ge(K.sem("tables"), 2)

    def step(ins):
        st.step(ins)
        st.wait()

    for p in range(2):
        c0 = FIRST_JOB[f"swa{p}"]
        evacuated(e, c0)
        step(v.tensor_tensor(b.kr, b.k, b.cos, ALU.mult))
        kv.wait("rot", p)
        kv.read("rot", v.tensor_tensor(b.rot, kv.bank("rot")[:, :], b.sin, ALU.mult))
        kv.wait_read("rot", p)
        step(v.tensor_tensor(b.kr, b.kr, b.rot, ALU.add))
        kv.wait("v", p)
        kv.read("v", v.tensor_copy(b.v_tok, kv.bank("v")[:, :].rearrange("p (a d) -> p a d", d=P)))
        with e.eng.Fori(0, 2) as i:
            st.enter(i, 2 * 22)
            for s in range(2):
                trip, c, use = i + 2 * p, c0 + 2 + 2 * s, lambda name: f"{name}_{s}"
                evacuated(e, c, i)
                step(v.tensor_tensor(b.qr, b.q, b.cos, ALU.mult))
                ring.wait(use("rot"), trip)
                ring.read(use("rot"), v.tensor_tensor(b.rot, ring.bank(use("rot"))[:, :], b.sin, ALU.mult))
                ring.wait_read(use("rot"), trip)
                step(v.tensor_tensor(b.qr, b.qr, b.rot, ALU.add))
                e.eng.sem_inc(K.sem("swa_q"), 1)

                def top(half):
                    j = 4 * half
                    for q in range(QT):
                        first = P if q == 0 else 0
                        u = use(f"s{half}{q // 2}")
                        ring.wait(u, trip)
                        st.step(v.tensor_reduce(b.mx[:, j + q:j + q + 1],
                                                ring.bank(u)[:, (q % 2) * 256 + first:(q % 2) * 256 + 256], AX.X, ALU.max))
                    st.wait()
                    sink = K.sinks[:, bass.ds(i * 2 + s + 4 * (2 * p + half), 1)].broadcast_to([P, QT])
                    mx, es = b.mx[:, j:j + 4], b.es[:, j:j + 4]
                    step(v.tensor_tensor(mx, mx, sink, ALU.max))
                    step(v.tensor_tensor(es, sink, mx, ALU.subtract))
                    step(v.tensor_scalar(mx, mx, -1.0, None, ALU.mult))
                    e.eng.sem_inc(K.sem("swa_max"), 1)

                def share(half):
                    j = 4 * half
                    ph, su, es, rec = (b.p0, b.p1)[half], b.sum[:, j:j + 4], b.es[:, j:j + 4], b.rec[:, j:j + 4]
                    e.eng.wait_ge(K.sem("swa_e"), trip * 20 + 10 * s + 5 * half + 5)
                    for pair in range(2):
                        e.eng.sem_inc(ring.free[ring.find(use(f"s{half}{pair}"))[1]], 1)
                    step(v.tensor_tensor(su, su, es, ALU.add))
                    step(v.reciprocal(rec, su))
                    st.step(v.tensor_scalar(ph[:, 0, P:256], ph[:, 0, P:256], rec[:, 0:1], None, ALU.mult))
                    v.tensor_tensor(ph[:, 1:4, :], ph[:, 1:4, :], rec[:, 1:4].unsqueeze(2).broadcast_to([P, 3, 256]),
                                    ALU.mult).then_inc(K.sem("swa_scaled"), 1)
                    st.wait()
                    e.eng.wait_ge(K.sem("swa_scaled"), trip * 4 + 2 * s + half + 1)
                    e.eng.sem_inc(K.sem("swa_p"), 1)

                def moved(half):
                    for n in range(2):
                        u, w = use(f"t{half}{n}"), (4, 3)[n]
                        ring.wait(u, trip)
                        ring.read(u, v.tensor_copy((b.pt0, b.pt1)[half][:, 4 * n:4 * n + w, :],
                                                   ring.bank(u)[:, 0:w * P].rearrange("p (a d) -> p a d", d=P)))

                top(0)
                top(1)
                share(0)
                share(1)
                moved(0)
                moved(1)
                ring.wait(use("o"), trip)
                evacuated(e, c + 1, i)
                t = i * 2 + s + 4 * p
                e.eng.wait_ge(K.sem("split_done"), t + FIRST_SPLIT["swa_y"])
                ring.read(use("o"), v.tensor_tensor(b.rot, ring.bank(use("o"))[:, :], b.z, ALU.mult))
                ring.wait_read(use("o"), trip)
                v.tensor_copy(K.y[:, 0, :], b.rot).then_inc(K.sem("y_done"), 1)
                y_pair_vector(e, "swa_y", t)
            st.leave(2)
    out_residual_dve(e, "swa_out")


def final_pe(e):
    stat_tensor(e, "final")


def final_act(e):
    stat_scalar(e, "final", e.K.X, lambda k: x_wait(e, "final", k))


def final_dve(e):
    K = e.K
    stat_vector(e, "final")
    for k in range(DT):
        K.nc.vector.scalar_tensor_tensor(K.X[:, k, :], K.X[:, k, :], K.col("final_norm_w", k), K.rstd[:, :],
                                         ALU.mult, ALU.mult).then_inc(K.sem("x_ready"), 1)
    e.eng.wait_ge(K.sem("x_ready"), X_DONE["final"])


def out_m_dve(e, phase, step, add=False, before_end=DT):
    K, c0 = e.K, FIRST_JOB[phase]
    count, base = K.sem("m_ready"), M_DONE[step] - before_end
    with e.eng.Fori(0, DT // SLOTS) as i:
        for r in range(SLOTS):
            job_wait(e, c0 + r, i)
            m = at(K.M, i * SLOTS + r)
            src = bank_of(e, c0 + r)[:, :]
            ins = K.nc.vector.tensor_tensor(m, src, m, ALU.add) if add else K.nc.vector.tensor_copy(m, src)
            ins.then_inc(count, 1)
            e.eng.wait_ge(count, i * SLOTS + r + base + 1)
            release(e, c0 + r)


def post_pe(e, step):
    stat_tensor(e, step + "_post")


def post_act(e, step):
    K = e.K
    stat_scalar(e, step + "_post", K.M, lambda k: e.eng.wait_ge(K.sem("m_ready"), M_DONE[step] - DT + k + 1))


def post_dve(e, step, weight, col0):
    K, v = e.K, e.K.nc.vector
    stat_vector(e, step + "_post")
    for k in range(DT + 1):
        if k < DT:
            e.steps.step(v.scalar_tensor_tensor(K.M[:, k, :], K.M[:, k, :], K.col(weight, col0 + k), K.rstd[:, :],
                                                ALU.mult, ALU.mult))
        if k:
            e.eng.wait_ge(e.steps.sem, e.steps.base + e.steps.k - (1 if k < DT else 0))
            v.tensor_tensor(K.X[:, k - 1, :], K.X[:, k - 1, :], K.M[:, k - 1, :], ALU.add).then_inc(K.sem("x_ready"), 1)
    e.eng.wait_ge(K.sem("x_ready"), X_DONE[step])


HG_USES = ["vt0", "vt1", "at0", "at1", "ke0a", "ke0b", "ke1a", "ke1b", "ks0a", "ks0b", "ks1a", "ks1b", "o_norm"]
HG_ORDER = [list(range(NCH)), list(range(NCH))[::-1]]


def hg_buffers(K):
    b = Names()
    (b.f, b.g, b.k, b.eg, b.v_tok, b.ke0, b.ke1, b.st0, b.st1, b.gl, b.hp, b.mx, b.lb, b.one_lb, b.e3, b.t8) = carve(
        K, (2, S), (2, S), (2, S), (2, S), (NCH, P), (NCH, P), (NCH, P), (NCH, P), (NCH, P), (2, NCH), (4,), (DT,),
        (DT,), (DT,), (3, DT), (DT,))
    b.q, b.v, b.ki = K.root[:, :], K.rstd[:, :], K.sq
    return b


def hg_pe(e):
    K, b, nc, c0, mm = e.K, hg_buffers(e.K), e.K.nc, FIRST_JOB["hg"], e.K.nc.tensor.matmul
    ring = Ring(e, "hg_aux", (4, 5, 6), HG_USES)
    ident = K.c("ident")
    prenorm_pe(e, "hg")
    e.eng.wait_ge(K.sem("hg_begin"), 1)
    for r in range(4):
        job(e, c0 + r)

    def head(i, more):
        nxt = all_parts(*[job_parts(e, c0 + 4 + r, i) for r in range(4)]) if more else iter(())
        evacuated(e, c0 + 3, i)
        for n in range(2):
            use = f"vt{n}"
            ring.claim(use, i)
            settle(e)
            for c in range(4):
                ins = nc.tensor.transpose(ring.bank(use)[0:CH, c * P:(c + 1) * P], chunk(b.v, 4 * n + c), ident)
            ring.written(ins)
        take(nxt, 12)
        for d in range(2):
            e.eng.wait_ge(K.sem("hg_decayed"), i * 2 + d + 1)
            use = f"at{d}"
            ring.claim(use, i)
            settle(e)
            for c in range(NCH):
                ins = mm(chunk(ring.bank(use)[0:CH, :], c), chunk(b.ki[:, d, :], c), chunk(b.f[:, d, :], c),
                         start=True, stop=True)
            ring.written(ins)
            take(nxt, 3)
        for d in range(2):
            e.eng.wait_ge(K.sem("hg_k_end"), i * 2 + d + 1)
            for n in range(2):
                use = f"ke{d}{'ab'[n]}"
                ring.claim(use, i)
                settle(e)
                for c in range(4):
                    ins = nc.tensor.transpose(ring.bank(use)[0:CH, c * P:(c + 1) * P], chunk(b.k[:, d, :], 4 * n + c), ident)
                ring.written(ins)
            take(nxt, 3)
        for d in range(2):
            ke = (b.ke0, b.ke1)[d]
            ring.wait_read(f"ke{d}a", i)
            ring.wait_read(f"ke{d}b", i)
            for n in range(2):
                use = f"ks{d}{'ab'[n]}"
                ring.claim(use, i)
                settle(e)
                for m, c in enumerate(HG_ORDER[d][4 * n:4 * n + 4 - n]):
                    ins = mm(ring.bank(use)[:, m * P:(m + 1) * P], ke[0:CH, c, :], b.v_tok[0:CH, c, :], start=True, stop=True)
                ring.written(ins)
            take(nxt, 4)
        e.eng.wait_ge(K.sem("hg_states"), i + 1)
        O = K.ps[7]
        settle(e)
        for c in range(NCH):
            dst = chunk(O, c)
            mm(dst, b.v_tok[0:CH, c, :], chunk(b.g[0:CH, 0, :], c), start=True, stop=False)
            ins = mm(dst, b.v_tok[0:CH, c, :], chunk(b.g[0:CH, 1, :], c), start=False, stop=False)
            for d in range(2):
                first = c == HG_ORDER[d][0]
                if not first:
                    last = d == 1 or c == HG_ORDER[1][0]
                    ins = mm(dst, (b.st0, b.st1)[d][:, c, :], chunk(b.f[:, d, :], c), start=False, stop=last)
        ins.then_inc(K.sem("hg_o"), 1)
        take(nxt, 32)
        e.eng.wait_ge(K.sem("hg_o_square"), i + 1)
        ring.claim("o_norm", i)
        ring.written(mm(ring.bank("o_norm")[:, :], K.c("ones")[:, 0:P], b.g[:, 0, :], start=True, stop=True))

    with e.eng.Fori(0, H8 - 1) as i:
        head(i, True)
    head(H8 - 1, False)
    c0 = FIRST_JOB["hg_gate"]
    with e.eng.Fori(0, DT // SLOTS) as i:
        for r in range(SLOTS):
            job(e, c0 + r, i)
    out_pe(e, "hg_out", "hg_y")
    post_pe(e, "hg")


def hg_act(e):
    K, b, nc, c0, act, st = e.K, hg_buffers(e.K), e.K.nc, FIRST_JOB["hg"], e.K.nc.scalar.activation, e.steps
    ring = Ring(e, "hg_aux", (4, 5, 6), HG_USES)
    e.eng.wait_ge(K.sem("hg_lb_in"), 1)
    act(b.e3, b.e3, ACT.Exp).then_inc(K.sem("hg_lb_e"), 1)
    prenorm_act(e, "hg")
    for r in range(4):
        weight_high(e, c0 + r + AHEAD)

    def head(i, more):
        for r, dst, func, scale in ((3, b.v, ACT.Copy, 1.0), (0, b.q, ACT.Copy, P ** -0.5),
                                    (1, b.f[:, 0, :], ACT.Sigmoid, 1.0), (2, b.f[:, 1, :], ACT.Sigmoid, 1.0)):
            job_wait(e, c0 + r, i)
            act(dst, bank_of(e, c0 + r)[:, :], func, scale=scale).then_inc(K.job_sems["bank"][(c0 + r) % SLOTS], 1)
        if more:
            weight_high(e, c0 + 4 + AHEAD, i)
        for d in range(2):
            e.eng.wait_ge(K.sem("hg_f"), i * 2 + d + 1)
            act(b.eg[:, d, :], b.f[:, d, :], ACT.Ln).then_inc(K.sem("hg_log"), 1)
        for d in range(2):
            e.eng.wait_ge(K.sem("hg_cum"), i * 2 + d + 1)
            act(b.ki[:, d, :], b.g[:, d, :], ACT.Exp, scale=-1.0).then_inc(K.sem("hg_exp"), 1)
            act(b.eg[:, d, :], b.g[:, d, :], ACT.Exp).then_inc(K.sem("hg_exp"), 1)
        for d in range(2):
            e.eng.wait_ge(K.sem("hg_to_end"), i * 2 + d + 1)
            act(b.g[:, d, :], b.g[:, d, :], ACT.Exp).then_inc(K.sem("hg_end_e"), 1)
        if more:
            weight_high(e, c0 + 5 + AHEAD, i)
        for d in range(2):
            for n in range(2):
                use = f"ke{d}{'ab'[n]}"
                ring.wait(use, i)
                ring.read(use, act((b.ke0, b.ke1)[d][0:CH, 4 * n:4 * n + 4, :],
                                   ring.bank(use)[0:CH, :].rearrange("p (c d) -> p c d", d=P), ACT.Copy))
        if more:
            weight_high(e, c0 + 6 + AHEAD, i)
            weight_high(e, c0 + 7 + AHEAD, i)
        e.eng.wait_ge(K.sem("hg_o"), i + 1)
        act(b.g[:, 0, :], K.ps[7][:, :], ACT.Square, scale=P ** -0.5).then_inc(K.sem("hg_o_square"), 1)
        ring.wait("o_norm", i)
        ring.read("o_norm", act(b.g[:, 0, :], ring.bank("o_norm")[:, :], ACT.Ln, bias=K.c("eps")))
        ring.wait_read("o_norm", i)
        act(b.g[:, 0, :], b.g[:, 0, :], ACT.Exp, scale=-0.5).then_inc(K.sem("hg_o_rstd"), 1)

    with e.eng.Fori(0, H8 - 1) as i:
        head(i, True)
    head(H8 - 1, False)
    c0 = FIRST_JOB["hg_gate"]
    split = FIRST_SPLIT["hg_y"]
    with e.eng.Fori(0, DT // SLOTS) as i:
        for r in range(SLOTS):
            weight_high(e, c0 + r + AHEAD, i)
            job_wait(e, c0 + r, i)
            e.eng.wait_ge(K.sem("y_done"), i * SLOTS + r + split)
            act(b.q, bank_of(e, c0 + r)[:, :], ACT.Silu).then_inc(K.job_sems["bank"][(c0 + r) % SLOTS], 1)
            y_pair_scalar(e, "hg_y", i * SLOTS + r)
    ahead_act(e, "hg_out")
    post_act(e, "hg")


def hg_dve(e):
    K, b, nc, c0, st, v = e.K, hg_buffers(e.K), e.K.nc, FIRST_JOB["hg"], e.steps, e.K.nc.vector
    ring = Ring(e, "hg_aux", (4, 5, 6), HG_USES)

    def step(ins):
        st.step(ins)
        st.wait()

    rows = K.param[:, K.cols["hg_lb_logits_2"]:K.cols["hg_lb_logits_2"] + 3 * DT].rearrange("p (a t) -> p a t", a=3)
    step(v.tensor_tensor(b.mx, rows[:, 0, :], rows[:, 1, :], ALU.max))
    step(v.tensor_tensor(b.mx, b.mx, rows[:, 2, :], ALU.max))
    v.tensor_tensor(b.e3, rows, b.mx.unsqueeze(1).broadcast_to([P, 3, DT]), ALU.subtract).then_inc(K.sem("hg_lb_in"), 1)
    prenorm_dve(e, "hg", "pre_mix_norm_2", 0, FIRST_JOB["hg"])
    e.eng.wait_ge(K.sem("hg_lb_e"), 1)
    step(v.tensor_tensor(b.t8, b.e3[:, 0, :], b.e3[:, 1, :], ALU.add))
    step(v.tensor_tensor(b.t8, b.t8, b.e3[:, 2, :], ALU.add))
    step(v.reciprocal(b.t8, b.t8))
    step(v.tensor_tensor(b.lb, b.e3[:, 0, :], b.t8, ALU.mult))
    step(v.tensor_scalar(b.one_lb, b.lb, -1.0, 1.0, ALU.mult, ALU.add))
    ring.begin()
    e.eng.sem_inc(K.sem("hg_begin"), 1)

    def head(i, more):
        step(v.tensor_copy(b.hp[:, 0:1], b.lb[:, bass.ds(i, 1)]))
        step(v.tensor_copy(b.hp[:, 1:2], b.one_lb[:, bass.ds(i, 1)]))
        step(v.tensor_copy(b.hp[:, 2:3], K.param[:, bass.ds(i + K.cols["hg_o_norm_2"], 1)]))
        for d in range(2):
            f = b.f[:, d, :]
            evacuated(e, c0 + 1 + d, i)
            st.step(v.tensor_scalar(f, f, b.hp[:, 1:2], b.hp[:, 0:1], ALU.mult, ALU.add))
            st.wait()
            e.eng.sem_inc(K.sem("hg_f"), 1)
        for d in range(2):
            step(v.tensor_scalar(b.k[:, d, :], b.f[:, d, :], -1.0, 1.0, ALU.mult, ALU.add))
        for n in range(2):
            use = f"vt{n}"
            ring.wait(use, i)
            ring.read(use, v.tensor_copy(b.v_tok[0:CH, 4 * n:4 * n + 4, :],
                                         ring.bank(use)[0:CH, :].rearrange("p (c d) -> p c d", d=P)))
        for d in range(2):
            e.eng.wait_ge(K.sem("hg_log"), i * 2 + d + 1)
            g, lg = b.g[:, d, :], b.eg[:, d, :]
            if d:
                g, lg = g[:, ::-1], lg[:, ::-1]
            step(v.tensor_tensor_scan(g, K.c("restart"), lg, 0.0, ALU.mult, ALU.add))
            e.eng.sem_inc(K.sem("hg_cum"), 1)
        for d in range(2):
            end = CH - 1 if d == 0 else 0
            g = b.g[:, d, :]
            step(v.tensor_copy(b.gl[:, d, :].unsqueeze(2), by_chunk(g)[:, :, end:end + 1]))
            e.eng.wait_ge(K.sem("hg_exp"), i * 4 + 2 * d + 2)
            st.step(v.tensor_tensor(b.ki[:, d, :], b.ki[:, d, :], b.k[:, d, :], ALU.mult))
            st.step(v.tensor_tensor(b.f[:, d, :], b.q, b.eg[:, d, :], ALU.mult))
            step(v.tensor_tensor(by_chunk(g), b.gl[:, d, :].unsqueeze(2).broadcast_to([P, NCH, CH]), by_chunk(g), ALU.subtract))
            e.eng.sem_inc(K.sem("hg_decayed"), 1)
            e.eng.sem_inc(K.sem("hg_to_end"), 1)
        for d in range(2):
            e.eng.wait_ge(K.sem("hg_end_e"), i * 2 + d + 1)
            step(v.tensor_tensor(b.k[:, d, :], b.k[:, d, :], b.g[:, d, :], ALU.mult))
            e.eng.sem_inc(K.sem("hg_k_end"), 1)
        for d in range(2):
            use = f"at{d}"
            ring.wait(use, i)
            mask = K.c("upto" if d == 0 else "from")[0:CH, 0:CH].unsqueeze(1).broadcast_to([CH, NCH, CH])
            ring.read(use, v.tensor_tensor(by_chunk(b.g[0:CH, d, :]), by_chunk(ring.bank(use)[0:CH, :]), mask, ALU.mult))
        for d in range(2):
            order, S_ = HG_ORDER[d], (b.st0, b.st1)[d]
            end = CH - 1 if d == 0 else 0
            for n in range(7):
                c, nxt = order[n], order[n + 1]
                use = f"ks{d}{'ab'[n // 4]}"
                if n % 4 == 0:
                    ring.wait(use, i)
                src = ring.bank(use)[:, (n % 4) * P:(n % 4 + 1) * P]
                if n == 0:
                    ins = v.tensor_copy(S_[:, nxt, :], src)
                else:
                    ins = v.scalar_tensor_tensor(S_[:, nxt, :], S_[:, c, :], b.eg[:, d, c * CH + end:c * CH + end + 1], src,
                                                 ALU.mult, ALU.add)
                step(ins)
                if n in (3, 6):
                    e.eng.sem_inc(ring.free[ring.find(use)[1]], 1)
        e.eng.sem_inc(K.sem("hg_states"), 1)
        e.eng.wait_ge(K.sem("hg_o_rstd"), i + 1)
        step(v.scalar_tensor_tensor(at(K.M, i), K.ps[7][:, :], b.hp[:, 2:3], b.g[:, 0, :], ALU.mult, ALU.mult))

    with e.eng.Fori(0, H8 - 1) as i:
        st.enter(i, HG_STEPS)
        head(i, True)
        st.leave(H8 - 1)
    head(H8 - 1, False)
    c0 = FIRST_JOB["hg_gate"]
    with e.eng.Fori(0, DT // SLOTS) as i:
        for r in range(SLOTS):
            t = i * SLOTS + r
            evacuated(e, c0 + r, i)
            e.eng.wait_ge(K.sem("split_done"), t + FIRST_SPLIT["hg_y"])
            v.tensor_tensor(K.y[:, 0, :], at(K.M, t), b.q, ALU.mult).then_inc(K.sem("y_done"), 1)
            y_pair_vector(e, "hg_y", t)
    out_m_dve(e, "hg_out", "hg")
    post_dve(e, "hg", "post_mix_norm_2", 0)


HG_STEPS = 34


TRIP = DT // SLOTS


def mlp_pe(e, name):
    stat_tensor(e, name)
    c0 = FIRST_JOB[name]
    with e.eng.Fori(0, 4) as q:
        with e.eng.Fori(0, TRIP) as i:
            for r in range(SLOTS):
                if r == 0:
                    job_with_waits(e, c0, q * 2 * TRIP + i, A_TILES, name + "_h")
                else:
                    job(e, c0 + r, q * 2 * TRIP + i)
        with e.eng.Fori(0, TRIP) as i:
            for r in range(SLOTS):
                if r == 0:
                    job_with_waits(e, c0 + DT, q * 2 * TRIP + i, B_TILES, name + "_y", q * DT)
                else:
                    job(e, c0 + DT + r, q * 2 * TRIP + i, B_TILES)
    post_pe(e, name)


def mlp_buffers(K):
    return K.work[:, 0:S]


def mlp_act(e, name):
    K, relu, c0 = e.K, mlp_buffers(e.K), FIRST_JOB[name]
    prenorm_act(e, name)
    with e.eng.Fori(0, 4) as q:
        with e.eng.Fori(0, TRIP) as i:
            for r in range(SLOTS):
                trip, n = q * 2 * TRIP + i, i * SLOTS + r
                weight_high(e, c0 + r + AHEAD, trip)
                job_wait(e, c0 + r, trip)
                e.eng.wait_ge(K.sem("y_done"), q * DT + n + FIRST_SPLIT[name + "_y"])
                K.nc.scalar.activation(relu, bank_of(e, c0 + r)[:, :], ACT.Relu).then_inc(K.sem("relu_done"), 1)
                e.eng.wait_ge(K.sem("y_done"), q * DT + n + FIRST_SPLIT[name + "_y"] + 1)
                K.nc.scalar.activation(at(K.act_hi, n + DT), K.y[:, 0, :], ACT.Copy).then_inc(K.sem("split_high_done"), 1)
        with e.eng.Fori(0, TRIP) as i:
            for r in range(SLOTS):
                weight_high(e, c0 + DT + r + AHEAD, q * 2 * TRIP + i)
    post_act(e, name)


def mlp_dve(e, name, layer):
    K, relu, c0, v = e.K, mlp_buffers(e.K), FIRST_JOB[name], e.K.nc.vector
    relus = 4 * DT * (XSTEPS[:XSTEPS.index(name)].count("mlp0"))
    for k in range(DT):
        e.steps.step(v.memset(K.M[:, k, :], 0.0))
    prenorm_dve(e, name, "pre_mlp_norm_2", layer * DT, c0)
    e.steps.wait()
    with e.eng.Fori(0, 4) as q:
        with e.eng.Fori(0, TRIP) as i:
            for r in range(SLOTS):
                trip, n = q * 2 * TRIP + i, i * SLOTS + r
                first = q * DT + n + FIRST_SPLIT[name + "_y"]
                e.eng.wait_ge(K.sem("relu_done"), q * DT + n + relus + 1)
                e.eng.wait_ge(K.sem("split_done"), first)
                v.scalar_tensor_tensor(K.y[:, 0, :], bank_of(e, c0 + r)[:, :], 0.0, relu, ALU.max, ALU.mult) \
                    .then_inc(K.sem("y_done"), 1)
                e.eng.wait_ge(K.sem("y_done"), first + 1)
                release(e, c0 + r)
                e.eng.wait_ge(K.sem("split_high_done"), first + 1)
                v.tensor_tensor(at(K.act_lo, n + DT), K.y[:, 0, :], at(K.act_hi, n + DT).bitcast(F32),
                                ALU.subtract).then_inc(K.sem("split_done"), 1)
        with e.eng.Fori(0, TRIP) as i:
            for r in range(SLOTS):
                trip, n = q * 2 * TRIP + i, i * SLOTS + r
                m_before = q * DT + n + M_DONE[name] - 4 * DT
                if r == 0:
                    e.eng.wait_ge(K.sem("m_ready"), m_before)
                job_wait(e, c0 + DT + r, trip)
                m = at(K.M, n)
                v.tensor_tensor(m, bank_of(e, c0 + r)[:, :], m, ALU.add).then_inc(K.sem("m_ready"), 1)
                e.eng.wait_ge(K.sem("m_ready"), m_before + 1)
                release(e, c0 + DT + r)
    post_dve(e, name, "post_mlp_norm_2", layer * DT)


PLE_USES = ["e0", "e1", "e2", "e3"]


def ple_embedding(K):
    return K.work[:, S:3 * S].rearrange("p (a s) -> p a s", a=2)


def ple_pe(e, name):
    ring = Ring(e, "ple_aux", (4, 5, 6, 7), PLE_USES)
    c0 = FIRST_JOB[name + "_gate"]
    with e.eng.Fori(0, TRIP) as i:
        for r in range(SLOTS):
            if r == 0:
                job_with_waits(e, c0, i, A_TILES, name + "_h")
            else:
                job(e, c0 + r, i)
    c0 = FIRST_JOB[name + "_proj"]
    split_wait(e, name + "_p", 2)
    for k in range(2):
        job_start(e, c0 + k)
        for t, use in enumerate(PLE_USES):
            ring.claim(use, NTH_PLE[name] * 2 + k)
            ring.written(product(e, c0 + k, ring.bank(use)[:, :], B_TILES[:2], 2 * t))
        e.eng.wait_ge(ring.ready, (NTH_PLE[name] * 2 + k + 1) * len(PLE_USES))
        e.eng.sem_inc(e.K.job_sems["done"], 1)
    ring.wait_read("e3", NTH_PLE[name] * 2 + 1)
    post_pe(e, name)


def ple_act(e, name, layer):
    K, act, emb = e.K, e.K.nc.scalar.activation, ple_embedding(e.K)
    x_wait(e, name, 0)
    e.eng.dma_start(emb, K.p_t[layer].rearrange("(t p) s -> p t s", p=P)).then_inc(K.sem("embedding"), 16)
    for k in range(DT):
        x_wait(e, name, k)
        act(K.act_hi[:, k, :], K.X[:, k, :], ACT.Copy).then_inc(K.sem("split_high_done"), 1)
    e.eng.wait_ge(K.sem("embedding"), 16 * (NTH_PLE[name] + 1))
    for k in range(2):
        act(K.act_hi[:, DT + k, :], emb[:, k, :], ACT.Copy).then_inc(K.sem("split_high_done"), 1)
    c0 = FIRST_JOB[name + "_gate"]
    with e.eng.Fori(0, TRIP) as i:
        for r in range(SLOTS):
            weight_high(e, c0 + r + AHEAD, i)
            job_wait(e, c0 + r, i)
            act(at(K.M, i * SLOTS + r), bank_of(e, c0 + r)[:, :], ACT.Sigmoid).then_inc(K.job_sems["bank"][(c0 + r) % SLOTS], 1)
    for k in range(2):
        weight_high(e, FIRST_JOB[name + "_proj"] + k + AHEAD)
    post_act(e, name)


def ple_dve(e, name, layer):
    K, v, emb = e.K, e.K.nc.vector, ple_embedding(e.K)
    ring = Ring(e, "ple_aux", (4, 5, 6, 7), PLE_USES)
    if NTH_PLE[name] == 0:
        ring.begin()
    e.eng.sem_inc(K.sem("y_done"), DT + 2)
    for k in range(DT):
        split_low(e, name + "_h", k, k, K.X[:, k, :])
    for k in range(2):
        split_low(e, name + "_p", k, DT + k, emb[:, k, :])
    gate, proj = FIRST_JOB[name + "_gate"], FIRST_JOB[name + "_proj"]
    for n in range(DT):
        use = PLE_USES[n % 4]
        if n % 4 == 0:
            job_wait(e, proj + n // 4)
            release(e, proj + n // 4)
        ring.wait(use, NTH_PLE[name] * 2 + n // 4)
        evacuated(e, gate + n)
        v.tensor_tensor(K.M[:, n, :], ring.bank(use)[:, :], K.M[:, n, :], ALU.mult).then_inc(K.sem("m_ready"), 1)
        e.eng.wait_ge(K.sem("m_ready"), M_DONE[name] - DT + n + 1)
        e.eng.sem_inc(ring.free[ring.find(use)[1]], 1)
    post_dve(e, name, "ple_norm_2", layer * DT)


ROPE_TURN = ["second", "rot0", "rot1"]


def mla_uses():
    order = ["n1", "k1", "v0", "v1", "vt0", "vt1"] + MLA_ORDER
    return [f"{u}_{s}" for s in range(2) for u in order]


MLA_ORDER = ["s00", "s01", "t00", "s02", "t01", "s03", "t02", "s10", "t03", "s11", "o0",
             "t10", "s12", "t11", "s13", "t12", "t13", "o1"]
MLA_VECTOR_ORDER = ["s00", "s01", "t00", "s02", "t01", "s03", "t02", "s10", "t03", "s11",
                    "t10", "s12", "o0", "t11", "s13", "t12", "t13", "o1"]


def mla_buffers(K):
    b = Names()
    (b.kr, b.qr, b.kn, b.v_tok0, b.v_tok1, b.p, b.pt, b.mx, b.sum, b.rec) = carve(
        K, (S,), (DT, S), (2, S), (QT, P), (QT, P), (2, S), (QT, S), (2,), (2,), (2,))
    b.qn, b.v, b.qs = K.y, K.sq, K.root[:, :]
    b.cos, b.sin, b.rot, b.k_raw = b.pt[:, 0, :], b.pt[:, 1, :], b.pt[:, 2, :], b.pt[:, 3, :]
    return b


def mla_pe(e):
    K, b, nc, mm, c0 = e.K, mla_buffers(e.K), e.K.nc, e.K.nc.tensor.matmul, FIRST_JOB["mla_in"]
    ident = K.c("ident")
    turn, key = Ring(e, "mla_rope", (4, 5, 6), ROPE_TURN), Ring(e, "mla_key", (4,), ["rot"])
    ring = Ring(e, "mla_aux", (4, 5, 6, 7), mla_uses())
    prenorm_pe(e, "mla")
    for r in range(6):
        job(e, c0 + r)
    stat_tensor(e, "mla_q")
    evacuated(e, c0 + 5)
    key.claim("rot", 0)
    key.written(mm(key.bank("rot")[:, :], K.c("rotate"), b.k_raw, start=True, stop=True))
    stat_tensor(e, "mla_kv")
    split_wait(e, "mla_cq", 3)
    key.wait_read("rot", 0)
    c0 = FIRST_JOB["mla_rope"]
    for k in range(4):
        job_start(e, c0 + k)
        product(e, c0 + k, bank_of(e, c0 + k)[:, :], [8, 9, 10])
        turn.claim("second", k)
        ins = product(e, c0 + k, turn.bank("second")[:, :], [8, 9, 10], 3)
        turn.written(ins)
        e.eng.wait_ge(turn.ready, k * len(ROPE_TURN) + 1)
        e.eng.sem_inc(K.job_sems["done"], 1)
        evacuated(e, c0 + k)
        turn.wait_read("second", k)
        for s in range(2):
            turn.claim(f"rot{s}", k)
            turn.written(mm(turn.bank(f"rot{s}")[:, :], K.c("rotate"), b.qr[:, 2 * k + s, :], start=True, stop=True))
    turn.wait_read("rot0", 3)
    turn.wait_read("rot1", 3)
    split_wait(e, "mla_ckv", 2)
    e.eng.wait_ge(K.sem("mla_begin"), 1)
    for part, out in ((0, "mla_outa"), (1, "mla_outb")):
        c0 = FIRST_JOB[("mla_a", "mla_b")[part]]
        with e.eng.Fori(0, 2) as i:
            for s in range(2):
                trip, c = i + 2 * part, c0 + 2 * s
                mla_pair_pe(e, b, ring, ident, trip, c, i, s)
        out_pe(e, out, "mla_y", A_TILES, part * DT)
    post_pe(e, "mla")


def mla_pair_pe(e, b, ring, ident, trip, c, i, s):
    K, nc, mm = e.K, e.K.nc, e.K.nc.tensor.matmul
    job_start(e, c, i)
    product(e, c, bank_of(e, c)[:, :], [8, 9, 10])
    ring.claim(f"n1_{s}", trip)
    ins = product(e, c, ring.bank(f"n1_{s}")[:, :], [8, 9, 10], 3)
    ring.written(ins)
    ring.wait(f"n1_{s}", trip)
    e.eng.sem_inc(K.job_sems["done"], 1)
    job_start(e, c + 1, i)
    product(e, c + 1, bank_of(e, c + 1)[:, :], [11, 12])
    for n, use in enumerate(("k1", "v0", "v1")):
        ring.claim(f"{use}_{s}", trip)
        ring.written(product(e, c + 1, ring.bank(f"{use}_{s}")[:, :], [11, 12], 2 * n + 2))
    ring.wait(f"v1_{s}", trip)
    e.eng.sem_inc(K.job_sems["done"], 1)
    for h in range(2):
        use = f"vt{h}_{s}"
        ring.claim(use, trip)
        ring.wait_read(f"v{h}_{s}", trip)
        settle(e)
        for t in range(QT):
            ins = nc.tensor.transpose(ring.bank(use)[:, t * P:(t + 1) * P], b.v[:, h, t * P:(t + 1) * P], ident)
        ring.written(ins)
    e.eng.wait_ge(K.sem("mla_staged"), trip * 2 + s + 1)
    evacuated(e, c, i)
    evacuated(e, c + 1, i)
    for what in MLA_ORDER:
        use, h = f"{what}_{s}", int(what[1])
        q = int(what[2]) if what[0] != "o" else 0
        ring.claim(use, trip)
        dst = ring.bank(use)
        if what[0] == "s":
            if what == "s00":
                ring.wait_read(f"n1_{s}", trip)
            settle(e)
            rows = slice(64 * h, 64 * h + 64)
            mm(dst[:, :], b.qn[:, h, q * P:(q + 1) * P], b.kn[:, h, :], start=True, stop=False)
            ins = mm(dst[:, :], b.qs[rows, q * P:(q + 1) * P], b.kr[rows, :], start=False, stop=True)
        elif what[0] == "t":
            e.eng.wait_ge(K.sem("mla_p"), trip * 16 + s * 8 + h * 4 + q + 1)
            settle(e)
            for t in range(QT):
                ins = nc.tensor.transpose(dst[:, t * P:(t + 1) * P], b.p[:, q % 2, t * P:(t + 1) * P], ident)
        else:
            ring.wait_read(f"t{h}3_{s}", trip)
            settle(e)
            for t in range(QT):
                ins = mm(dst[:, :], (b.v_tok0, b.v_tok1)[h][:, t, :], b.pt[:, t, :], start=t == 0, stop=t == QT - 1)
        ring.written(ins)


def mla_act(e):
    K, b, act, c0 = e.K, mla_buffers(e.K), e.K.nc.scalar.activation, FIRST_JOB["mla_in"]
    turn = Ring(e, "mla_rope", (4, 5, 6), ROPE_TURN)
    ring = Ring(e, "mla_aux", (4, 5, 6, 7), mla_uses())
    scale = (128 + 64) ** -0.5
    prenorm_act(e, "mla")
    fetch_positions(e, K.positions_2, ROPES_BEFORE)
    for r in range(6):
        weight_high(e, c0 + r + AHEAD)
        job_wait(e, c0 + r)
        bank = K.job_sems["bank"][(c0 + r) % SLOTS]
        act(K.M[:, r, :] if r < 5 else b.k_raw, bank_of(e, c0 + r)[:, :], ACT.Copy).then_inc(bank, 1)
    rope_sines(e, b.cos, b.sin, ROPES_BEFORE)
    stat_scalar(e, "mla_q", K.M, lambda k: evacuated(e, c0 + k))
    norm_split_scalar(e, "mla_cq", 3, DT)
    stat_scalar(e, "mla_kv", K.M[:, 3:5, :], lambda k: evacuated(e, c0 + 3 + k))
    norm_split_scalar(e, "mla_ckv", 2, DT + 3)
    c0 = FIRST_JOB["mla_rope"]
    for k in range(4):
        weight_high(e, c0 + k + AHEAD)
        job_wait(e, c0 + k)
        act(b.qr[:, 2 * k, :], bank_of(e, c0 + k)[:, :], ACT.Copy, scale=scale).then_inc(K.job_sems["bank"][(c0 + k) % SLOTS], 1)
        turn.wait("second", k)
        turn.read("second", act(b.qr[:, 2 * k + 1, :], turn.bank("second")[:, :], ACT.Copy, scale=scale))
    for part, out in ((0, "mla_outa"), (1, "mla_outb")):
        c0 = FIRST_JOB[("mla_a", "mla_b")[part]]
        with e.eng.Fori(0, 2) as i:
            for s in range(2):
                trip, c, per = i + 2 * part, c0 + 2 * s, len(mla_uses())
                weight_high(e, c + AHEAD, i)
                job_wait(e, c, i)
                act(b.qn[:, 0, :], bank_of(e, c)[:, :], ACT.Copy, scale=scale).then_inc(K.job_sems["bank"][c % SLOTS], 1)
                ring.wait(f"n1_{s}", trip)
                ring.read(f"n1_{s}", act(b.qn[:, 1, :], ring.bank(f"n1_{s}")[:, :], ACT.Copy, scale=scale))
                weight_high(e, c + 1 + AHEAD, i)
                for h in range(2):
                    use = f"v{h}_{s}"
                    ring.wait(use, trip)
                    ring.read(use, act(b.v[:, h, :], ring.bank(use)[:, :], ACT.Copy))
                for what in MLA_ORDER:
                    use, h = f"{what}_{s}", int(what[1])
                    q = int(what[2]) if what[0] != "o" else 0
                    if what[0] == "s":
                        e.eng.wait_ge(K.sem("mla_max"), trip * 16 + s * 8 + h * 4 + q + 1)
                        if not (h == 0 and q < 2):
                            ring.wait(f"t{h}{q - 2}_{s}" if q >= 2 else f"t0{q + 2}_{s}", trip)
                        ring.read(use, act(b.p[:, q % 2, :], ring.bank(use)[:, :], ACT.Exp, bias=b.mx[:, q % 2:q % 2 + 1],
                                           accum_out=b.sum[:, q % 2:q % 2 + 1]))
                    elif what[0] == "t":
                        ring.wait(use, trip)
                        ring.read(use, act(b.pt[:, :, q * P:(q + 1) * P],
                                           ring.bank(use)[:, :].rearrange("p (a d) -> p a d", d=P), ACT.Copy))
                    else:
                        ring.wait(use, trip)
                        act(at(K.act_hi, i * 4 + 2 * s + h), ring.bank(use)[:, :], ACT.Copy) \
                            .then_inc(K.sem("split_high_done"), 1)
        ahead_act(e, out)
    post_act(e, "mla")


def mla_dve(e):
    K, b, v, st, c0 = e.K, mla_buffers(e.K), e.K.nc.vector, e.steps, FIRST_JOB["mla_in"]
    turn, key = Ring(e, "mla_rope", (4, 5, 6), ROPE_TURN), Ring(e, "mla_key", (4,), ["rot"])
    ring = Ring(e, "mla_aux", (4, 5, 6, 7), mla_uses())

    def step(ins):
        st.step(ins)
        st.wait()

    prenorm_dve(e, "mla", "pre_mix_norm_2", DT, c0)
    e.eng.sem_inc(K.sem("position_room"), 1)
    rope_angles(e, "mla_freq", b.cos, b.sin, ROPES_BEFORE)
    for r in (turn, key):
        r.begin()
    e.eng.wait_ge(K.sem("tables"), 2 * ROPES_BEFORE + 2)
    stat_vector(e, "mla_q")
    norm_split_vector(e, "mla_q", "mla_cq", K.M, "mla_q_norm_2", 0, 3, DT)
    stat_vector(e, "mla_kv")
    norm_split_vector(e, "mla_kv", "mla_ckv", K.M[:, 3:5, :], "mla_kv_norm_2", 0, 2, DT + 3)
    evacuated(e, c0 + 5)
    step(v.tensor_tensor(b.kr, b.k_raw, b.cos, ALU.mult))
    key.wait("rot", 0)
    key.read("rot", v.tensor_tensor(b.rot, key.bank("rot")[:, :], b.sin, ALU.mult))
    key.wait_read("rot", 0)
    step(v.tensor_tensor(b.kr, b.kr, b.rot, ALU.add))
    for k in range(4):
        for s in range(2):
            q, use = b.qr[:, 2 * k + s, :], f"rot{s}"
            turn.wait(use, k)
            step(v.tensor_tensor(q, q, b.cos, ALU.mult))
            turn.read(use, v.tensor_tensor(b.rot, turn.bank(use)[:, :], b.sin, ALU.mult))
            turn.wait_read(use, k)
            step(v.tensor_tensor(q, q, b.rot, ALU.add))
    ring.begin()
    e.eng.sem_inc(K.sem("mla_begin"), 1)
    e.eng.sem_inc(K.sem("y_done"), 2 * DT)
    for part, out in ((0, "mla_outa"), (1, "mla_outb")):
        c0 = FIRST_JOB[("mla_a", "mla_b")[part]]
        with e.eng.Fori(0, 2) as i:
            st.enter(i, 2 * MLA_STEPS)
            for s in range(2):
                trip, c = i + 2 * part, c0 + 2 * s
                step(v.tensor_copy(b.qs, at(b.qr, i * 2 + s + 4 * part)))
                e.eng.sem_inc(K.sem("mla_staged"), 1)
                job_wait(e, c + 1, i)
                v.tensor_copy(b.kn[:, 0, :], bank_of(e, c + 1)[:, :]).then_inc(K.job_sems["bank"][(c + 1) % SLOTS], 1)
                ring.wait(f"k1_{s}", trip)
                ring.read(f"k1_{s}", v.tensor_copy(b.kn[:, 1, :], ring.bank(f"k1_{s}")[:, :]))
                for h in range(2):
                    use = f"vt{h}_{s}"
                    ring.wait(use, trip)
                    ring.read(use, v.tensor_copy((b.v_tok0, b.v_tok1)[h],
                                                 ring.bank(use)[:, :].rearrange("p (a d) -> p a d", d=P)))
                for what in MLA_VECTOR_ORDER:
                    use, h = f"{what}_{s}", int(what[1])
                    q = int(what[2]) if what[0] != "o" else 0
                    mx, rec = b.mx[:, q % 2:q % 2 + 1], b.rec[:, q % 2:q % 2 + 1]
                    if what[0] == "s":
                        ring.wait(use, trip)
                        step(v.tensor_reduce(mx, ring.bank(use)[:, :], AX.X, ALU.max))
                        v.tensor_scalar(mx, mx, -1.0, None, ALU.mult).then_inc(K.sem("mla_max"), 1)
                    elif what[0] == "t":
                        ring.wait_read(f"s{h}{q}_{s}", trip)
                        step(v.reciprocal(rec, b.sum[:, q % 2:q % 2 + 1]))
                        v.tensor_scalar(b.p[:, q % 2, :], b.p[:, q % 2, :], rec, None, ALU.mult).then_inc(K.sem("mla_p"), 1)
                    else:
                        t = i * 4 + 2 * s + h
                        e.eng.wait_ge(K.sem("split_high_done"), t + part * DT + FIRST_SPLIT["mla_y"] + 1)
                        v.tensor_tensor(at(K.act_lo, t), ring.bank(use)[:, :], at(K.act_hi, t).bitcast(F32),
                                        ALU.subtract).then_inc(K.sem("split_done"), 1)
                        e.eng.wait_ge(K.sem("split_done"), t + part * DT + FIRST_SPLIT["mla_y"] + 1)
                        e.eng.sem_inc(ring.free[ring.find(use)[1]], 1)
            st.leave(2)
        out_m_dve(e, out, "mla", add=part == 1, before_end=(2 - part) * DT)
    post_dve(e, "mla", "post_mix_norm_2", DT)


MLA_STEPS = 17
ROPES_BEFORE = int("swa" in XSTEPS)


PROGRAM = {
    "conv": (conv_pe, conv_act, conv_dve),
    "fox": (fox_pe, fox_act, fox_dve),
    "gdn": (gdn_pe, gdn_act, gdn_dve),
    "swa": (swa_pe, swa_act, swa_dve),
    "final": (final_pe, final_act, final_dve),
    "hg": (hg_pe, hg_act, hg_dve),
    "mlp0": (lambda e: mlp_pe(e, "mlp0"), lambda e: mlp_act(e, "mlp0"), lambda e: mlp_dve(e, "mlp0", 0)),
    "ple0": (lambda e: ple_pe(e, "ple0"), lambda e: ple_act(e, "ple0", 0), lambda e: ple_dve(e, "ple0", 0)),
    "mla": (mla_pe, mla_act, mla_dve),
    "mlp1": (lambda e: mlp_pe(e, "mlp1"), lambda e: mlp_act(e, "mlp1"), lambda e: mlp_dve(e, "mlp1", 1)),
    "ple1": (lambda e: ple_pe(e, "ple1"), lambda e: ple_act(e, "ple1", 1), lambda e: ple_dve(e, "ple1", 1)),
}
STAGES = list(PROGRAM)


def chunked(w):
    n = w.shape[0] // P
    a = np.zeros((P, D), w.dtype)
    a[:, :n * P] = w.reshape(n, P, P).transpose(1, 0, 2).reshape(P, n * P)
    return a


def tiles_of(w, first, n=DT):
    return [chunked(w[:, first + k * P:first + (k + 1) * P]) for k in range(n)]


def wide(parts):
    a = np.zeros((parts[0][1].shape[0], P), parts[0][1].dtype)
    for place, w in parts:
        a[:, place:place + w.shape[1]] = w
    return a


def weight_jobs(w):
    jobs = []

    def per_head(m, parts, n=H8):
        return [chunked(m[:, q * D + h * P:q * D + (h + 1) * P]) for h in range(n) for q in parts]

    jobs += per_head(w["conv_w_in"][0], range(4)) + tiles_of(w["conv_w_out"][0], 0)
    fox = w["fox_w_in"][0]
    jobs += [chunked(wide([(0, fox[:, 4 * D:])]))] + per_head(fox, range(4)) + tiles_of(w["fox_w_out"][0], 0)
    gdn = w["gdn_w_in"][0]
    jobs += [chunked(wide([(0, gdn[:, 4 * D:4 * D + H8]), (32, gdn[:, 4 * D + H8:])]))]
    jobs += per_head(gdn, range(4)) + tiles_of(w["gdn_w_out"][0], 0)
    swa, swa_out, rows = w["swa_w_in"][0], w["swa_w_out"][0], []
    for p in range(2):
        jobs += [chunked(swa[:, D + p * P:D + (p + 1) * P]), chunked(swa[:, D + 256 + p * P:D + 256 + (p + 1) * P])]
        for g in range(4):
            two = np.concatenate([np.arange(64) + 64 * (4 * kv + g) for kv in (2 * p, 2 * p + 1)])
            jobs += [chunked(swa[:, two]), chunked(swa[:, D + 512 + two])]
            rows.append(two)
    jobs += tiles_of(swa_out[np.concatenate(rows)], 0)
    hg = w["hg_w_in_2"][0]
    jobs += per_head(hg, range(4)) + tiles_of(hg, 4 * D) + tiles_of(w["hg_w_out_2"][0], 0)

    def mlp(l):
        out = []
        for q in range(4):
            out += tiles_of(w["w_mlp_in_2"][l], q * D) + tiles_of(w["w_mlp_out_2"][l][q * D:(q + 1) * D], 0)
        return out

    def ple(l):
        proj = w["w_ple_proj_2"][l]
        return tiles_of(w["w_ple_gate_2"][l], 0) + [
            chunked(np.concatenate([proj[:, (4 * k + t) * P:(4 * k + t + 1) * P] for t in range(4)])) for k in range(2)]

    jobs += mlp(0) + ple(0)
    win, uq, ukv, wo = w["mla_w_in_2"][0], w["mla_w_uq_2"][0], w["mla_w_ukv_2"][0], w["mla_w_o_2"][0]
    jobs += tiles_of(win, 0, 5) + [chunked(wide([(0, win[:, 640:]), (64, win[:, 640:])]))]
    for k in range(4):
        jobs.append(chunked(np.concatenate(
            [np.concatenate([uq[:, (2 * t + s) * 192 + 128:(2 * t + s + 1) * 192] for s in range(2)], 1)
             for t in (2 * k, 2 * k + 1)])))
    for part in range(2):
        for t in range(4 * part, 4 * part + 4):
            jobs.append(chunked(np.concatenate([uq[:, h * 192:h * 192 + 128] for h in (2 * t, 2 * t + 1)])))
            jobs.append(chunked(np.concatenate([ukv[:, h * 256 + o:h * 256 + o + P]
                                                for o in (0, P) for h in (2 * t, 2 * t + 1)])))
        jobs += tiles_of(wo[part * D:(part + 1) * D], 0)
    jobs += mlp(1) + ple(1)
    assert len(jobs) == N_JOBS, (len(jobs), N_JOBS)
    jobs += [jobs[0]] * (PADDED_JOBS - N_JOBS)
    return np.stack(jobs)


def feature_columns(a):
    return np.ascontiguousarray(a.reshape(-1, P).T)


def parameter_block(w):
    parts = []
    for name, n in PARAMS:
        a = w[name]
        if name == "conv_w_conv":
            a = a[0].reshape(3, DT, P).transpose(1, 0, 2)
        if name == "gdn_w_conv":
            a = a[0].reshape(4, 3, H8, P).transpose(2, 1, 0, 3)
        a = feature_columns(a)
        assert a.shape[1] == n, (name, a.shape)
        parts.append(a)
    for name in HEAD_COLS:
        a = np.zeros((P, 1), np.float32)
        at_row = 0 if name == "fox_b_f" else 32
        a[at_row:at_row + H8, 0] = w[name][0]
        parts.append(a)
    return np.concatenate(parts, 1)


def kernel(**inputs):
    from concourse import bacc
    from concourse.bass_utils import run_bass_kernel_spmd

    w = {k: np.asarray(v) for k, v in inputs.items()}
    nc = bacc.Bacc("TRN2", target_bir_lowering=False, num_devices=1)
    arrays = {
        "weights": weight_jobs(w),
        "x_t": np.ascontiguousarray(w["x"][0].T),
        "p_t": np.ascontiguousarray(w["p_2"][:, 0].transpose(0, 2, 1)),
        "consts": np.concatenate(list(const_layout().values()), 1),
        "params": parameter_block(w),
        "positions": w["positions"], "positions_2": w["positions_2"], "sinks": w["swa_sinks"][0],
    }
    args = [nc.dram_tensor(k, a.shape, mybir.dt.from_np(a.dtype), kind="ExternalInput").ap() for k, a in arrays.items()]
    out = nc.dram_tensor("out_t", (D, S), F32, kind="ExternalOutput").ap()
    hybrid_stack(nc, *args, out)
    r = run_bass_kernel_spmd(nc, [arrays], core_ids=[0])
    return np.ascontiguousarray(np.asarray(r.results[0]["out_t"]).T)[None]
```

```python
import math
from contextlib import ExitStack

import concourse.bass as bass
import numpy as np
from concourse import mybir

F32 = mybir.dt.float32
F32R = mybir.dt.float32r
I32 = mybir.dt.int32
ALU = mybir.AluOpType
ACT = mybir.ActivationFunctionType
AX = mybir.AxisListType

P = 128
S = 512
D = 1024
DT = D // P
EPS = 1e-6
NEG = -1.0e30
SLOTS = 4
AHEAD = SLOTS - 1
CH = 64
NCH = S // CH
H8 = 8
QT = S // P
WORK = 10256


def const_layout():
    i = np.arange(P)
    c = {}
    c["ident"] = np.eye(P)
    c["ones"] = np.ones((P, S))
    c["eps"] = np.full((P, 1), EPS)
    c["causal"] = np.where(i[None, :] <= i[:, None], 0.0, NEG)
    c["before"] = np.where(i[None, :] > i[:, None], 0.0, NEG)
    rot = np.zeros((P, P))
    for g in range(0, P, 64):
        for j in range(32):
            rot[g + j + 32, g + j] = -1.0
            rot[g + j, g + j + 32] = 1.0
    c["rotate"] = rot
    k = np.arange(CH)
    m = np.zeros((P, CH)); m[:CH] = np.where(k[:, None] <= k[None, :], 1.0, 0.0)
    c["upto"] = m
    m = np.zeros((P, CH)); m[:CH] = np.where(k[:, None] >= k[None, :], 1.0, 0.0)
    c["from"] = m
    m = np.zeros((P, CH)); m[:CH] = np.where(k[:, None] <= k[None, :], 0.0, NEG)
    c["upto_neg"] = m
    for lvl in range(6):
        b = 1 << lvl
        up = (k[:, None] // (2 * b) == k[None, :] // (2 * b)) & (k[:, None] // b % 2 == 0) & (k[None, :] // b % 2 == 1)
        m = np.zeros((P, CH)); m[:CH] = up
        c[f"level{lvl}"] = m
    c["restart"] = np.tile(np.where(np.arange(S) % CH == 0, 0.0, 1.0), (P, 1))
    half = 32
    f = (10000.0 ** (-np.arange(half, dtype=np.float32) / np.float32(half))).astype(np.float32)
    c["swa_freq"] = np.tile(f, 4)[:, None]
    f = (1.0 / (10000.0 ** (np.arange(0, 64, 2, dtype=np.float32) / np.float32(64)))).astype(np.float32)
    c["mla_freq"] = np.tile(f, 4)[:, None]
    return {k: np.asarray(v, np.float32) for k, v in c.items()}


PARAMS = [("norm_w", 4 * DT), ("final_norm_w", DT), ("conv_w_conv", 3 * DT), ("gdn_w_conv", 4 * 3 * DT),
          ("gdn_norm_w", 1), ("pre_mix_norm_2", 2 * DT), ("post_mix_norm_2", 2 * DT),
          ("pre_mlp_norm_2", 2 * DT), ("post_mlp_norm_2", 2 * DT), ("ple_norm_2", 2 * DT),
          ("hg_lb_logits_2", 3 * DT), ("hg_o_norm_2", DT), ("mla_q_norm_2", 3), ("mla_kv_norm_2", 2)]
HEAD_COLS = ["fox_b_f", "gdn_dt_bias", "gdn_a_log"]


def const_at(name):
    n = 0
    for k, a in const_layout().items():
        if k == name:
            return n
        n += a.shape[1]


def param_columns():
    at, cols = 0, {}
    for name, n in PARAMS:
        cols[name] = at
        at += n
    for name in HEAD_COLS:
        cols[name] = at
        at += 1
    return cols, at


JOBS = [("conv", 4 * DT), ("conv_out", DT),
        ("fox_f", 1), ("fox", 4 * H8), ("fox_out", DT),
        ("gdn_ba", 1), ("gdn", 4 * H8), ("gdn_out", DT),
        ("swa0", 10), ("swa1", 10), ("swa_out", DT),
        ("hg", 4 * H8), ("hg_gate", DT), ("hg_out", DT),
        ("mlp0", 64), ("ple0_gate", DT), ("ple0_proj", 2),
        ("mla_in", 6), ("mla_rope", 4), ("mla_a", 8), ("mla_outa", DT), ("mla_b", 8), ("mla_outb", DT),
        ("mlp1", 64), ("ple1_gate", DT), ("ple1_proj", 2)]
FIRST_JOB = {}
N_JOBS = 0
for _name, _n in JOBS:
    FIRST_JOB[_name] = N_JOBS
    N_JOBS += _n
PADDED_JOBS = N_JOBS + AHEAD

SPLITS = [("conv_h", DT), ("conv_y", DT), ("fox_h", DT), ("fox_y", DT), ("gdn_h", DT), ("gdn_y", DT),
          ("swa_h", DT), ("swa_y", DT), ("hg_h", DT), ("hg_y", DT),
          ("mlp0_h", DT), ("mlp0_y", 4 * DT), ("ple0_h", DT), ("ple0_p", 2),
          ("mla_h", DT), ("mla_cq", 3), ("mla_ckv", 2), ("mla_y", 2 * DT),
          ("mlp1_h", DT), ("mlp1_y", 4 * DT), ("ple1_h", DT), ("ple1_p", 2)]
FIRST_SPLIT, _t = {}, 0
for _name, _n in SPLITS:
    FIRST_SPLIT[_name] = _t
    _t += _n

STATS = [("conv", DT, D), ("fox", DT, D), ("gdn", DT, D), ("swa", DT, D), ("final", DT, D),
         ("hg", DT, D), ("hg_post", DT, D), ("mlp0", DT, D), ("mlp0_post", DT, D), ("ple0_post", DT, D),
         ("mla", DT, D), ("mla_q", 3, 384), ("mla_kv", 2, 256),
         ("mla_post", DT, D), ("mlp1", DT, D), ("mlp1_post", DT, D), ("ple1_post", DT, D)]
FIRST_SQUARE, STAT_NO, STAT_SIZE, _t = {}, {}, {}, 0
for _k, (_name, _n, _f) in enumerate(STATS):
    FIRST_SQUARE[_name], STAT_NO[_name], STAT_SIZE[_name] = _t, _k, (_n, _f)
    _t += _n

MSTEPS = [("hg", DT), ("mlp0", 4 * DT), ("ple0", DT), ("mla", 2 * DT), ("mlp1", 4 * DT), ("ple1", DT)]
M_DONE = {name: sum(n for _, n in MSTEPS[:k + 1]) for k, (name, _) in enumerate(MSTEPS)}
NTH_PLE = {name: k for k, name in enumerate(name for name, _ in MSTEPS if name.startswith("ple"))}

XSTEPS = ["load", "conv", "fox", "gdn", "swa", "final", "hg", "mlp0", "ple0", "mla", "mlp1", "ple1"]
X_DONE = {name: (k + 1) * DT for k, name in enumerate(XSTEPS)}


SUMMED = {"fox": "conv_out", "gdn": "fox_out", "swa": "gdn_out", "final": "swa_out", "hg_post": "hg_out",
          "mla_post": "mla_outb"}
SUMMED_BY = {phase: stage for stage, phase in SUMMED.items()}


def settle(e):
    e.eng.sem_inc(e.K.sem("waits_ended"), 1)


class Names:
    pass


class Chain:

    def __init__(self, eng, sem):
        self.eng, self.sem, self.base, self.k = eng, sem, 0, 0

    def step(self, ins):
        ins.then_inc(self.sem, 1)
        self.k += 1

    def wait(self):
        self.eng.wait_ge(self.sem, self.base + self.k)

    def enter(self, i, per):
        self.entry = self.base + self.k
        self.base, self.k, self.per = self.entry + i * per, 0, per

    def leave(self, trips):
        assert self.k == self.per, (self.k, self.per)
        self.base, self.k = self.entry + trips * self.per, 0


def at(buf, i, n=None):
    return buf[:, bass.ds(i, 1), :].rearrange("p a n -> p (a n)")


def hybrid_stack(nc, weights, x_t, p_t, consts, params, positions, positions_2, sinks, out):
    const_cols = {}
    n = 0
    for name, a in const_layout().items():
        const_cols[name] = (n, a.shape[1])
        n += a.shape[1]
    n_const = n
    cols, n_params = param_columns()

    ctx = ExitStack()
    with ctx:
        def sb(name, shape, dt=F32):
            return ctx.enter_context(nc.sbuf_tensor(name, shape, dt))

        sems = {}

        def sem(name):
            if name not in sems:
                sems[name] = ctx.enter_context(nc.semaphore(name))
            return sems[name]

        K = Names()
        K.nc, K.sem, K.cols, K.out, K.weights, K.x_t, K.p_t = nc, sem, cols, out, weights, x_t, p_t
        K.consts_in, K.params_in, K.positions, K.positions_2, K.sinks_in = consts, params, positions, positions_2, sinks
        K.const = sb("const", [P, n_const])
        K.param = sb("param", [P, n_params])
        K.sinks = sb("sink_rows", [P, 16])
        K.raw = sb("weights_raw", [P, SLOTS, D])
        K.w_hi = sb("weights_high", [P, SLOTS, D], F32R)
        K.w_lo = sb("weights_low", [P, SLOTS, D], F32R)
        K.X = sb("residual", [P, DT, S])
        K.M = sb("mixed", [P, DT, S])
        K.act_hi = sb("activations_high", [P, 2 * DT, S], F32R)
        K.act_lo = sb("activations_low", [P, 2 * DT, S], F32R)
        K.ident_r = sb("ident_r", [P, P], F32R)
        K.mask_r = sb("mask_r", [P, 2 * P], F32R)
        K.sq = sb("squares", [P, 2, S])
        K.rstd = sb("rstd", [P, S])
        K.root = sb("root", [P, S])
        K.y = sb("to_split", [P, 2, S])
        K.work = sb("work", [P, WORK])
        K.ps = [ctx.enter_context(nc.psum_tensor(f"bank{k}", [P, S], F32)) for k in range(8)]
        K.job_sems = dict(raw=[sem(f"raw_full{k}") for k in range(SLOTS)], high=sem("weights_high_ready"),
                          low=sem("weights_low_ready"), done=sem("jobs_done"),
                          bank=[sem(f"bank_free{k}") for k in range(SLOTS)])

        def c(name, parts=P):
            a, w = const_cols[name]
            return K.const[0:parts, a:a + w]
        K.c = c
        K.col = lambda name, j: K.param[:, cols[name] + j:cols[name] + j + 1]
        for name in ("constants_in", "x_in", "x_ready", "y_done", "split_high_done", "split_done",
                     "square_ready", "square_used", "rstd_ready", "vector_steps", "scalar_steps", "stored", "finished", "masks_ready", "position", "waits_ended"):
            sem(name)

        block = ctx.enter_context(nc.Block())
        stages = STAGES

        @block.sync
        def _(sync):
            sync.dma_start(K.const[:, :], consts).then_inc(sem("constants_in"), 16)
            sync.dma_start(K.param[:, :], params).then_inc(sem("constants_in"), 16)
            sync.dma_start(K.sinks[:, :], sinks[None, :].broadcast_to([P, 16])).then_inc(sem("constants_in"), 16)
            def fill(r, j):
                sync.wait_ge(K.job_sems["low"], j + 1)
                sync.dma_start(K.raw[:, r, :], weights[bass.ds(j, 1)].rearrange("a p n -> p (a n)")) \
                    .then_inc(K.job_sems["raw"][r], 16)

            with sync.Fori(0, PADDED_JOBS // SLOTS) as i:
                for r in range(SLOTS):
                    fill(r, i * SLOTS + r)
            for r in range(PADDED_JOBS % SLOTS):
                fill(r, PADDED_JOBS // SLOTS * SLOTS + r)
            sync.wait_ge(sem("finished"), 1)
            sync.dma_start(out.rearrange("(t p) s -> p t s", p=P), K.X[:, :, :]).then_inc(sem("stored"), 16)
            sync.wait_ge(sem("stored"), 16)

        @block.gpsimd
        def _(pool):
            pool.sem_inc(K.job_sems["low"], SLOTS)
            pool.dma_start(K.X[:, :, :], x_t.rearrange("(t p) s -> p t s", p=P)).then_inc(sem("x_in"), 16)

            def low(r, j):
                pool.wait_ge(K.job_sems["high"], j + 1)
                nc.gpsimd.tensor_tensor(K.w_lo[:, r, :], K.raw[:, r, :], K.w_hi[:, r, :].bitcast(F32),
                                        ALU.subtract).then_inc(K.job_sems["low"], 1)

            with pool.Fori(0, PADDED_JOBS // SLOTS) as i:
                for r in range(SLOTS):
                    low(r, i * SLOTS + r)
            for r in range(PADDED_JOBS % SLOTS):
                low(r, PADDED_JOBS // SLOTS * SLOTS + r)

        @block.scalar
        def _(act):
            e = Names()
            e.eng, e.K, e.steps = act, K, Chain(act, sem("scalar_steps"))
            act.wait_ge(sem("constants_in"), 48)
            for j in range(AHEAD):
                weight_high(e, j)
            for name in stages:
                PROGRAM[name][1](e)

        @block.tensor
        def _(pe):
            e = Names()
            e.eng, e.K = pe, K
            pe.wait_ge(sem("constants_in"), 48)
            pe.wait_ge(sem("masks_ready"), 1)
            for name in stages:
                PROGRAM[name][0](e)

        @block.vector
        def _(dve):
            e = Names()
            e.eng, e.K, e.steps = dve, K, Chain(dve, sem("vector_steps"))
            for k in range(SLOTS):
                dve.sem_inc(K.job_sems["bank"][k], 1)
            dve.wait_ge(sem("constants_in"), 48)
            e.steps.step(nc.vector.tensor_copy(K.ident_r[:, :], K.c("ident")))
            e.steps.step(nc.vector.tensor_copy(K.mask_r[:, 0:P], K.c("before")))
            nc.vector.tensor_copy(K.mask_r[:, P:2 * P], K.c("causal")).then_inc(sem("masks_ready"), 1)
            dve.wait_ge(sem("x_in"), 16)
            dve.sem_inc(sem("x_ready"), DT)
            for name in stages:
                PROGRAM[name][2](e)
            dve.wait_ge(sem("x_ready"), X_DONE[stages[-1]])
            dve.sem_inc(sem("finished"), 1)



def weight_high(e, c, i=None):
    js, s, off = e.K.job_sems, c % SLOTS, 0 if i is None else i
    e.eng.wait_ge(js["raw"][s], off * 16 + 16 * (c // SLOTS + 1))
    if c >= SLOTS:
        e.eng.wait_ge(js["done"], off * SLOTS + c - SLOTS + 1)
    e.K.nc.scalar.activation(e.K.w_hi[:, s, :], e.K.raw[:, s, :], ACT.Copy).then_inc(js["high"], 1)


def job_wait(e, c, i=None):
    off = 0 if i is None else i
    e.eng.wait_ge(e.K.job_sems["done"], off * SLOTS + c + 1)


def bank_of(e, c):
    return e.K.ps[c % SLOTS]


def release(e, c):
    e.eng.sem_inc(e.K.job_sems["bank"][c % SLOTS], 1)


def job_start(e, c, i=None):
    off = 0 if i is None else i
    js = e.K.job_sems
    e.eng.wait_ge(js["low"], off * SLOTS + c + 1 + SLOTS)
    e.eng.wait_ge(js["bank"][c % SLOTS], off + c // SLOTS + 1)


def product(e, c, dst, tiles, chunk0=0, start=True, stop=True):
    K, s = e.K, c % SLOTS
    for n, t in enumerate(tiles):
        k = chunk0 + n
        wh, wl = K.w_hi[:, s, k * P:(k + 1) * P], K.w_lo[:, s, k * P:(k + 1) * P]
        first, last = start and n == 0, stop and n == len(tiles) - 1
        K.nc.tensor.matmul(dst, wh, K.act_hi[:, t, :], start=first, stop=False)
        K.nc.tensor.matmul(dst, wh, K.act_lo[:, t, :], start=False, stop=False)
        ins = K.nc.tensor.matmul(dst, wl, K.act_hi[:, t, :], start=False, stop=last)
    return ins


A_TILES = list(range(DT))
B_TILES = list(range(DT, 2 * DT))


def job(e, c, i=None, tiles=A_TILES):
    job_start(e, c, i)
    product(e, c, bank_of(e, c)[:, :], tiles).then_inc(e.K.job_sems["done"], 1)


def split_wait(e, stage, n):
    e.eng.wait_ge(e.K.sem("split_done"), FIRST_SPLIT[stage] + n)


def split_high(e, stage, k, tile, src):
    e.eng.wait_ge(e.K.sem("y_done"), FIRST_SPLIT[stage] + k + 1)
    e.K.nc.scalar.activation(at(e.K.act_hi, tile), src, ACT.Copy).then_inc(e.K.sem("split_high_done"), 1)


def split_low(e, stage, k, tile, src):
    e.eng.wait_ge(e.K.sem("split_high_done"), FIRST_SPLIT[stage] + k + 1)
    e.K.nc.vector.tensor_tensor(at(e.K.act_lo, tile), src, at(e.K.act_hi, tile).bitcast(F32),
                                ALU.subtract).then_inc(e.K.sem("split_done"), 1)


STAT_BANK = 7


def stat_scalar(e, stage, source, ready):
    K, (n, feats) = e.K, STAT_SIZE[stage]
    for k in range(0 if stage in SUMMED else n):
        t = FIRST_SQUARE[stage] + k
        ready(k)
        if t >= 2:
            e.eng.wait_ge(K.sem("square_used"), t - 1)
        K.nc.scalar.activation(K.sq[:, t % 2, :], source[:, k, :], ACT.Square, scale=feats ** -0.5) \
            .then_inc(K.sem("square_ready"), 1)
    root_scalar(e, stage)


def stat_tensor(e, stage):
    K, (n, _) = e.K, STAT_SIZE[stage]
    if STAT_NO[stage]:
        e.eng.wait_ge(K.sem("rstd_ready"), STAT_NO[stage])
    if stage in SUMMED:
        e.eng.wait_ge(K.sem("square_used"), FIRST_SQUARE[stage] + n)
        K.nc.tensor.matmul(K.ps[STAT_BANK][:, :], K.c("ones")[:, 0:P], K.root[:, :], start=True, stop=True) \
            .then_inc(K.sem("sum_ready"), 1)
        return
    for k in range(n):
        t = FIRST_SQUARE[stage] + k
        e.eng.wait_ge(K.sem("square_ready"), t + 1)
        K.nc.tensor.matmul(K.ps[STAT_BANK][:, :], K.c("ones")[:, 0:P], K.sq[:, t % 2, :],
                           start=k == 0, stop=k == n - 1).then_inc(K.sem("square_used"), 1)


def inverse_root(e, out, tmp, src):
    e.steps.step(e.K.nc.scalar.activation(tmp, src, ACT.Ln, bias=e.K.c("eps")))
    e.steps.wait()
    return e.K.nc.scalar.activation(out, tmp, ACT.Exp, scale=-0.5)


def root_scalar(e, stage):
    K, (n, _) = e.K, STAT_SIZE[stage]
    if stage in SUMMED:
        e.eng.wait_ge(K.sem("sum_ready"), list(SUMMED).index(stage) + 1)
    else:
        e.eng.wait_ge(K.sem("square_used"), FIRST_SQUARE[stage] + n)
    inverse_root(e, K.rstd[:, :], K.root[:, :], K.ps[STAT_BANK][:, :]).then_inc(K.sem("rstd_ready"), 1)


def stat_vector(e, stage):
    e.eng.wait_ge(e.K.sem("rstd_ready"), STAT_NO[stage] + 1)


def norm_split_vector(e, stage, split, source, weight, col0, n, tile0=0, free_after=None):
    K = e.K
    if free_after is not None:
        e.eng.wait_ge(K.job_sems["done"], free_after)
    for k in range(n + 1):
        if k < n:
            if FIRST_SPLIT[split] + k >= 2:
                e.eng.wait_ge(K.sem("split_done"), FIRST_SPLIT[split] + max(k - 1, 0))
            K.nc.vector.scalar_tensor_tensor(K.y[:, k % 2, :], source[:, k, :], K.col(weight, col0 + k), K.rstd[:, :],
                                             ALU.mult, ALU.mult).then_inc(K.sem("y_done"), 1)
        if k:
            split_low(e, split, k - 1, tile0 + k - 1, K.y[:, (k - 1) % 2, :])


def norm_split_scalar(e, split, n, tile0=0):
    for k in range(n):
        split_high(e, split, k, tile0 + k, e.K.y[:, k % 2, :])


def x_wait(e, stage, k):
    e.eng.wait_ge(e.K.sem("x_ready"), X_DONE[XSTEPS[XSTEPS.index(stage) - 1]] - DT + k + 1)


def prenorm_pe(e, stage, first_job=None):
    stat_tensor(e, stage)
    if first_job is not None:
        job_with_waits(e, first_job, None, A_TILES, stage + "_h")


def prenorm_act(e, stage):
    stat_scalar(e, stage, e.K.X, lambda k: x_wait(e, stage, k))
    norm_split_scalar(e, stage + "_h", DT)


def prenorm_dve(e, stage, weight, col0, free_after=None):
    stat_vector(e, stage)
    norm_split_vector(e, stage, stage + "_h", e.K.X, weight, col0, DT, 0, free_after)


def out_pe(e, phase, split, tiles=B_TILES, skip=0):
    c0 = FIRST_JOB[phase]
    with e.eng.Fori(0, DT // SLOTS) as i:
        for r in range(SLOTS):
            if r == 0:
                job_with_waits(e, c0, i, tiles, split, skip)
            else:
                job(e, c0 + r, i, tiles)


def ahead_act(e, phase):
    c0 = FIRST_JOB[phase]
    with e.eng.Fori(0, DT // SLOTS) as i:
        for r in range(SLOTS):
            weight_high(e, c0 + r + AHEAD, i)
            if phase in SUMMED_BY:
                square_tile(e, SUMMED_BY[phase], i, r)


def square_tile(e, stage, i, r):
    K, n, first = e.K, i * SLOTS + r, FIRST_SQUARE[stage]
    if stage.endswith("_post"):
        e.eng.wait_ge(K.sem("m_ready"), n + M_DONE[stage[:-5]] - DT + 1)
        source = K.M
    else:
        e.eng.wait_ge(K.sem("x_ready"), n + X_DONE[XSTEPS[XSTEPS.index(stage) - 1]] - DT + 1)
        source = K.X
    e.eng.wait_ge(K.sem("square_used"), n + first - 1)
    K.nc.scalar.activation(K.sq[:, (first + r) % 2, :], at(source, n), ACT.Square, scale=D ** -0.5) \
        .then_inc(K.sem("square_ready"), 1)


def add_square(e, stage, i, r):
    K, n, first = e.K, i * SLOTS + r, FIRST_SQUARE[stage]
    e.eng.wait_ge(K.sem("square_ready"), n + first + 1)
    e.eng.wait_ge(K.sem("square_used"), n + first)
    K.nc.vector.tensor_tensor(K.root[:, :], K.root[:, :], K.sq[:, (first + r) % 2, :], ALU.add) \
        .then_inc(K.sem("square_used"), 1)


def out_residual_dve(e, phase):
    K, c0 = e.K, FIRST_JOB[phase]
    e.steps.step(K.nc.vector.memset(K.root[:, :], 0.0))
    e.steps.wait()
    with e.eng.Fori(0, DT // SLOTS) as i:
        e.steps.enter(i, SLOTS)
        for r in range(SLOTS):
            job_wait(e, c0 + r, i)
            x = at(K.X, i * SLOTS + r)
            e.steps.step(K.nc.vector.tensor_tensor(x, bank_of(e, c0 + r)[:, :], x, ALU.add))
            e.steps.wait()
            release(e, c0 + r)
            e.eng.sem_inc(K.sem("x_ready"), 1)
            add_square(e, SUMMED_BY[phase], i, r)
        e.steps.leave(DT // SLOTS)


def conv_pe(e):
    prenorm_pe(e, "conv")
    c0 = FIRST_JOB["conv"]
    with e.eng.Fori(0, DT) as i:
        job_with_waits(e, c0, i, A_TILES, "conv_h")
        for r in range(1, 4):
            job(e, c0 + r, i)
    out_pe(e, "conv_out", "conv_y")


def conv_buffers(K):
    w = K.work
    b = Names()
    b.c, b.z, b.u, b.t, b.taps = w[:, 0:512], w[:, 512:1024], w[:, 1024:1538], w[:, 1540:2052], w[:, 2052:2055]
    return b


def conv_act(e):
    K, b, c0 = e.K, conv_buffers(e.K), FIRST_JOB["conv"]
    prenorm_act(e, "conv")
    with e.eng.Fori(0, DT) as i:
        for r in range(4):
            weight_high(e, c0 + r + AHEAD, i)
            if r == 1:
                e.eng.wait_ge(K.sem("conv_u"), i + 1)
                job_wait(e, c0 + 1, i)
                K.nc.scalar.activation(b.c, bank_of(e, c0 + 1)[:, :], ACT.Copy).then_inc(K.sem("conv_c"), 1)
                e.eng.wait_ge(K.sem("conv_c"), i + 1)
                release(e, c0 + 1)
        job_wait(e, c0 + 3, i)
        K.nc.scalar.activation(b.z, bank_of(e, c0 + 3)[:, :], ACT.Silu).then_inc(K.sem("conv_z"), 1)
        e.eng.wait_ge(K.sem("conv_z"), i + 1)
        release(e, c0 + 3)
        e.eng.wait_ge(K.sem("y_done"), i + FIRST_SPLIT["conv_y"] + 1)
        K.nc.scalar.activation(at(K.act_hi, i + DT), K.y[:, 0, :], ACT.Copy).then_inc(K.sem("split_high_done"), 1)
    ahead_act(e, "conv_out")


def conv_dve(e):
    K, b, c0, v = e.K, conv_buffers(e.K), FIRST_JOB["conv"], e.K.nc.vector
    prenorm_dve(e, "conv", "norm_w", 0)
    e.steps.step(v.memset(b.u[:, 0:2], 0.0))
    e.steps.wait()
    e.eng.sem_inc(K.sem("conv_u"), 1)
    with e.eng.Fori(0, DT) as i:
        e.steps.enter(i, 6)
        e.steps.wait()
        e.eng.wait_ge(K.sem("split_done"), i + FIRST_SPLIT["conv_y"])
        e.steps.step(v.tensor_copy(b.taps, K.param[:, bass.ds(i * 3 + K.cols["conv_w_conv"], 3)]))
        job_wait(e, c0 + 2, i)
        e.eng.wait_ge(K.sem("conv_c"), i + 1)
        e.steps.step(v.tensor_tensor(b.u[:, 2:514], bank_of(e, c0 + 2)[:, :], b.c, ALU.mult))
        e.steps.wait()
        release(e, c0 + 2)
        e.eng.sem_inc(K.sem("conv_u"), 1)
        e.steps.step(v.tensor_scalar(b.t, b.u[:, 0:512], b.taps[:, 0:1], None, ALU.mult))
        e.steps.wait()
        e.steps.step(v.scalar_tensor_tensor(b.t, b.u[:, 1:513], b.taps[:, 1:2], b.t, ALU.mult, ALU.add))
        e.steps.wait()
        e.steps.step(v.scalar_tensor_tensor(b.t, b.u[:, 2:514], b.taps[:, 2:3], b.t, ALU.mult, ALU.add))
        e.steps.wait()
        e.steps.step(v.tensor_tensor(b.t, bank_of(e, c0)[:, :], b.t, ALU.mult))
        e.steps.wait()
        release(e, c0)
        e.eng.wait_ge(K.sem("conv_z"), i + 1)
        v.tensor_tensor(K.y[:, 0, :], b.t, b.z, ALU.mult).then_inc(K.sem("y_done"), 1)
        split = FIRST_SPLIT["conv_y"]
        e.eng.wait_ge(K.sem("split_high_done"), i + split + 1)
        v.tensor_tensor(at(K.act_lo, i + DT), K.y[:, 0, :], at(K.act_hi, i + DT).bitcast(F32),
                        ALU.subtract).then_inc(K.sem("split_done"), 1)
        e.steps.leave(DT)
    out_residual_dve(e, "conv_out")


def evacuated(e, c, i=None):
    off = 0 if i is None else i
    e.eng.wait_ge(e.K.job_sems["bank"][c % SLOTS], off + c // SLOTS + 2)


def carve(K, *shapes):
    views, a = [], 0
    for shape in shapes:
        n = math.prod(shape)
        v = K.work[:, a:a + n]
        views.append(v if len(shape) == 1 else v.rearrange("p (a b) -> p a b", a=shape[0]))
        a += n + (n & 1)
    assert a <= WORK, a
    return views


def y_pair_scalar(e, split, i):
    e.eng.wait_ge(e.K.sem("y_done"), i + FIRST_SPLIT[split] + 1)
    e.K.nc.scalar.activation(at(e.K.act_hi, i + DT), e.K.y[:, 0, :], ACT.Copy).then_inc(e.K.sem("split_high_done"), 1)


def y_pair_vector(e, split, i):
    e.eng.wait_ge(e.K.sem("split_high_done"), i + FIRST_SPLIT[split] + 1)
    e.K.nc.vector.tensor_tensor(at(e.K.act_lo, i + DT), e.K.y[:, 0, :], at(e.K.act_hi, i + DT).bitcast(F32),
                                ALU.subtract).then_inc(e.K.sem("split_done"), 1)


def fox_buffers(K):
    b = Names()
    (b.q, b.k, b.v, b.z, b.neg_c, b.x, b.e, b.sel, b.v_tok, b.p, b.pt, b.mx, b.nmax, b.sum, b.rec) = carve(
        K, (S,), (S,), (S,), (S,), (S,), (S,), (S,), (P,), (QT, P), (2, S), (QT, S), (QT,), (QT,), (QT,), (QT,))
    return b


TRANSPOSE_BANK = 6
OUT_BANK = 7


def fox_pe(e):
    K, b, nc, c0 = e.K, fox_buffers(e.K), e.K.nc, FIRST_JOB["fox"]
    prenorm_pe(e, "fox", FIRST_JOB["fox_f"])
    tb = K.ps[TRANSPOSE_BANK]
    for r in range(3):
        job(e, c0 + r)
    e.eng.wait_ge(K.sem("fox_c"), 1)

    def head(i, more):
        fill = all_parts(*[job_parts(e, c0 + 3 + r, i) for r in range(4 if more else 1)])
        evacuated(e, c0 + 2, i)
        e.eng.wait_ge(K.sem("fox_t_used"), i * 5 + 1)
        settle(e)
        for t in range(QT):
            ins = nc.tensor.transpose(tb[:, t * P:(t + 1) * P], b.v[:, t * P:(t + 1) * P], K.c("ident"))
        ins.then_inc(K.sem("fox_t_ready"), 1)
        evacuated(e, c0, i)
        evacuated(e, c0 + 1, i)
        e.eng.wait_ge(K.sem("fox_sel"), i + 1)

        def scores(q):
            bank, n = K.ps[4 + q % 2], (q + 1) * P
            e.eng.wait_ge(K.sem("fox_s_used"), i * QT + q + 1)
            settle(e)
            nc.tensor.matmul(bank[:, 0:n], b.q[:, q * P:n], b.k[:, 0:n], start=True, stop=False)
            nc.tensor.matmul(bank[:, 0:n], b.sel[0:H8, :], b.neg_c[0:H8, 0:n], start=False, stop=False)
            nc.tensor.matmul(bank[:, q * P:n], K.ident_r[:, :], K.mask_r[:, P:2 * P], start=False, stop=True) \
                .then_inc(K.sem("fox_s_ready"), 1)

        def transposed(q):
            e.eng.wait_ge(K.sem("fox_p_ready"), i * QT + q + 1)
            e.eng.wait_ge(K.sem("fox_t_used"), i * 5 + q + 2)
            settle(e)
            for t in range(q + 1):
                ins = nc.tensor.transpose(tb[:, t * P:(t + 1) * P], b.p[:, q % 2, t * P:(t + 1) * P], K.c("ident"))
            ins.then_inc(K.sem("fox_t_ready"), 1)

        for step, q, parts in ((scores, 0, 1), (scores, 1, 4), (transposed, 0, 2), (scores, 2, 3), (transposed, 1, 2),
                               (scores, 3, 4), (transposed, 2, 4), (transposed, 3, 2)):
            step(q)
            take(fill, parts)
        e.eng.wait_ge(K.sem("fox_t_used"), i * 5 + 6)
        e.eng.wait_ge(K.sem("fox_o_used"), i + 1)
        settle(e)
        for t in range(QT):
            ins = nc.tensor.matmul(K.ps[OUT_BANK][:, t * P:S], b.v_tok[:, t, :], b.pt[:, t, t * P:S],
                                   start=t == 0, stop=t == QT - 1)
        ins.then_inc(K.sem("fox_o_ready"), 1)
        take(fill, 10)

    with e.eng.Fori(0, H8 - 1) as i:
        head(i, True)
    head(H8 - 1, False)
    out_pe(e, "fox_out", "fox_y")


def fox_act(e):
    K, b, nc, c0, cf = e.K, fox_buffers(e.K), e.K.nc, FIRST_JOB["fox"], FIRST_JOB["fox_f"]
    prenorm_act(e, "fox")
    weight_high(e, cf + AHEAD)
    st = e.steps
    e.eng.wait_ge(K.sem("fox_x"), 1)
    st.step(nc.scalar.activation(b.e[0:H8, :], b.e[0:H8, :], ACT.Exp))
    st.wait()
    nc.scalar.activation(b.e[0:H8, :], b.e[0:H8, :], ACT.Ln, bias=K.c("ones")[0:H8, 0:1]).then_inc(K.sem("fox_ln"), 1)
    for r in range(3):
        weight_high(e, c0 + r + AHEAD)

    def head(i, more):
        for r in range(3):
            job_wait(e, c0 + r, i)
            nc.scalar.activation((b.q, b.k, b.v)[r], bank_of(e, c0 + r)[:, :], ACT.Copy,
                                 scale=P ** -0.5 if r == 0 else 1.0).then_inc(K.job_sems["bank"][(c0 + r) % SLOTS], 1)
        weight_high(e, c0 + 3 + AHEAD, i)
        for q in range(QT):
            e.eng.wait_ge(K.sem("fox_nmax"), i * QT + q + 1)
            if q >= 2:
                e.eng.wait_ge(K.sem("fox_t_ready"), i * 5 + q)
            nc.scalar.activation(b.p[:, q % 2, 0:(q + 1) * P], K.ps[4 + q % 2][:, 0:(q + 1) * P], ACT.Exp,
                                 bias=b.nmax[:, q:q + 1], accum_out=b.sum[:, q:q + 1]).then_inc(K.sem("fox_e"), 1)
            if more and q >= 2:
                weight_high(e, c0 + q + 2 + AHEAD, i)
        job_wait(e, c0 + 3, i)
        nc.scalar.activation(b.z, bank_of(e, c0 + 3)[:, :], ACT.Silu).then_inc(K.job_sems["bank"][(c0 + 3) % SLOTS], 1)
        y_pair_scalar(e, "fox_y", i)
        if more:
            weight_high(e, c0 + 6 + AHEAD, i)

    with e.eng.Fori(0, H8 - 1) as i:
        head(i, True)
    head(H8 - 1, False)
    ahead_act(e, "fox_out")


def fox_dve(e):
    K, b, nc, c0, cf, st = e.K, fox_buffers(e.K), e.K.nc, FIRST_JOB["fox"], FIRST_JOB["fox_f"], e.steps
    v = nc.vector
    prenorm_dve(e, "fox", "norm_w", DT, FIRST_JOB["fox_f"])
    job_wait(e, cf)
    x, ee, ncum = b.x[0:H8, :], b.e[0:H8, :], b.neg_c[0:H8, :]
    st.step(v.tensor_scalar(x, bank_of(e, cf)[0:H8, :], K.col("fox_b_f", 0)[0:H8, :], None, ALU.add))
    st.wait()
    release(e, cf)
    v.scalar_tensor_tensor(ee, x, -1.0, x, ALU.mult, ALU.min).then_inc(K.sem("fox_x"), 1)
    e.eng.wait_ge(K.sem("fox_x"), 1)
    st.step(v.tensor_scalar(x, x, 0.0, None, ALU.min))
    st.wait()
    e.eng.wait_ge(K.sem("fox_ln"), 1)
    st.step(v.tensor_tensor(x, ee, x, ALU.subtract))
    st.wait()
    v.tensor_tensor_scan(ncum, K.c("ones")[0:H8, :], x, 0.0, ALU.mult, ALU.add).then_inc(K.sem("fox_c"), 1)
    e.eng.wait_ge(K.sem("fox_c"), 1)
    e.eng.sem_inc(K.sem("fox_t_used"), 1)
    e.eng.sem_inc(K.sem("fox_s_used"), 2)
    e.eng.sem_inc(K.sem("fox_o_used"), 1)
    ident = K.c("ident")
    a0 = const_at("ident")
    tb = K.ps[TRANSPOSE_BANK]
    with e.eng.Fori(0, H8) as i:
        st.enter(i, 8)
        v.tensor_copy(b.sel[0:H8, :], K.const[0:H8, bass.ds(i + a0, 1)].broadcast_to([H8, P])).then_inc(K.sem("fox_sel"), 1)
        e.eng.wait_ge(K.sem("fox_t_ready"), i * 5 + 1)
        v.tensor_copy(b.v_tok, tb[:, :].rearrange("p (a b) -> p a b", a=QT)).then_inc(K.sem("fox_t_used"), 1)

        def top(q):
            e.eng.wait_ge(K.sem("fox_s_ready"), i * QT + q + 1)
            st.step(v.tensor_reduce(b.mx[:, q:q + 1], K.ps[4 + q % 2][:, 0:(q + 1) * P], AX.X, ALU.max))
            st.wait()
            v.tensor_scalar(b.nmax[:, q:q + 1], b.mx[:, q:q + 1], -1.0, None, ALU.mult).then_inc(K.sem("fox_nmax"), 1)

        def share(q):
            e.eng.wait_ge(K.sem("fox_e"), i * QT + q + 1)
            e.eng.sem_inc(K.sem("fox_s_used"), 1)
            st.step(v.reciprocal(b.rec[:, q:q + 1], b.sum[:, q:q + 1]))
            st.wait()
            p = b.p[:, q % 2, 0:(q + 1) * P]
            v.tensor_scalar(p, p, b.rec[:, q:q + 1], None, ALU.mult).then_inc(K.sem("fox_p_ready"), 1)

        def evacuate(q):
            e.eng.wait_ge(K.sem("fox_t_ready"), i * 5 + q + 2)
            v.tensor_copy(b.pt[:, 0:q + 1, q * P:(q + 1) * P],
                          tb[:, 0:(q + 1) * P].rearrange("p (a b) -> p a b", b=P)).then_inc(K.sem("fox_t_used"), 1)

        for step, q in ((top, 0), (top, 1), (share, 0), (evacuate, 0), (top, 2), (share, 1), (evacuate, 1),
                        (top, 3), (share, 2), (evacuate, 2), (share, 3), (evacuate, 3)):
            step(q)
        e.eng.wait_ge(K.sem("fox_o_ready"), i + 1)
        evacuated(e, c0 + 3, i)
        e.eng.wait_ge(K.sem("split_done"), i + FIRST_SPLIT["fox_y"])
        v.tensor_tensor(K.y[:, 0, :], K.ps[OUT_BANK][:, :], b.z, ALU.mult).then_inc(K.sem("y_done"), 1)
        y_pair_vector(e, "fox_y", i)
        e.eng.sem_inc(K.sem("fox_o_used"), 1)
        st.leave(H8)
    out_residual_dve(e, "fox_out")


class Ring:

    def __init__(self, e, name, banks, uses):
        self.e, self.banks, self.uses = e, banks, list(uses)
        self.ready = e.K.sem(name + "_ready")
        self.free = [e.K.sem(f"{name}_free{b}") for b in banks]

    def find(self, use):
        u = self.uses.index(use)
        b = u % len(self.banks)
        per_trip = len(range(b, len(self.uses), len(self.banks)))
        return u, b, u // len(self.banks), per_trip

    def bank(self, use):
        return self.e.K.ps[self.banks[self.find(use)[1]]]

    def begin(self):
        for f in self.free:
            self.e.eng.sem_inc(f, 1)

    def claim(self, use, i):
        _, b, k, per = self.find(use)
        self.e.eng.wait_ge(self.free[b], i * per + k + 1)

    def written(self, ins):
        ins.then_inc(self.ready, 1)

    def wait(self, use, i):
        self.e.eng.wait_ge(self.ready, i * len(self.uses) + self.find(use)[0] + 1)

    def read(self, use, ins):
        ins.then_inc(self.free[self.find(use)[1]], 1)

    def wait_read(self, use, i):
        _, b, k, per = self.find(use)
        self.e.eng.wait_ge(self.free[b], i * per + k + 2)


def job_with_waits(e, c, i, tiles, split, skip=0):
    parts = job_parts(e, c, i, tiles)
    for k in range(len(tiles)):
        split_wait(e, split, k + 1 + skip)
        next(parts)


def job_parts(e, c, i=None, tiles=A_TILES):
    K, s, dst = e.K, c % SLOTS, bank_of(e, c)[:, :]
    job_start(e, c, i)
    for k, t in enumerate(tiles):
        wh, wl = K.w_hi[:, s, k * P:(k + 1) * P], K.w_lo[:, s, k * P:(k + 1) * P]
        K.nc.tensor.matmul(dst, wh, K.act_hi[:, t, :], start=k == 0, stop=False)
        K.nc.tensor.matmul(dst, wh, K.act_lo[:, t, :], start=False, stop=False)
        ins = K.nc.tensor.matmul(dst, wl, K.act_hi[:, t, :], start=False, stop=k == len(tiles) - 1)
        if k == len(tiles) - 1:
            ins.then_inc(K.job_sems["done"], 1)
        yield


def take(parts, n):
    for _ in range(n):
        next(parts, None)


def all_parts(*gens):
    for g in gens:
        yield from g


GDN_LEVELS = range(1, 6)
GDN_USES = (["beta", "grow", "gi", "gram", "qk", "kt0", "kt1", "t1", "vt0", "vt1"]
            + [f"{w}{l}" for l in GDN_LEVELS for w in ("w", "dt", "ds") if (w, l) != ("dt", 5)]
            + ["wt"] + [f"{w}{c}" for c in range(NCH) for w in ("v", "k") if (w, c) != ("k", NCH - 1)] + ["o_norm"])


def gdn_buffers(K):
    b = Names()
    (b.u, b.t, b.x, b.taps, b.sel, b.bg, b.eg, b.tok, b.f1, b.hb, b.hg, b.hf, b.egl, b.ea, b.umat, b.um1, b.s, b.tt,
     b.qkt, b.nwt, b.vn, b.st) = carve(
        K, (3, 516), (3, S), (3, S), (12,), (P,), (S,), (S,), (NCH, 64), (NCH, H8), (NCH,), (NCH,), (NCH,), (NCH,),
        (2,), (S,), (S,), (S,), (S,), (S,), (S,), (2, P), (2, P))
    b.um = [K.root, b.um1]
    b.w, b.z, b.dt = K.rstd, K.sq[:, 0, :], K.sq[:, 1, :]
    m = K.M[:, :, :].rearrange("p a b -> p (a b)")
    b.kbe, b.kd, b.vb = (m[0:CH, k * 1024:(k + 1) * 1024].rearrange("p (a b) -> p a b", b=P) for k in range(3))
    b.qd, b.o = m[:, 3072:3584], m[:, 3584:4096]
    return b


def by_chunk(a):
    return a.rearrange("p (c j) -> p c j", j=CH)


def chunk(a, c):
    return a[:, c * CH:(c + 1) * CH]


def gdn_pe(e):
    K, b, nc, c0, mm = e.K, gdn_buffers(e.K), e.K.nc, FIRST_JOB["gdn"], e.K.nc.tensor.matmul
    ring = Ring(e, "gdn_aux", (4, 5, 6), GDN_USES)
    ident, ones = K.c("ident"), K.c("ones")[:, 0:P]
    prenorm_pe(e, "gdn", FIRST_JOB["gdn_ba"])
    e.eng.wait_ge(K.sem("gdn_gates"), 1)
    for c in range(NCH):
        ins = nc.tensor.transpose(K.ps[4][0:CH, c * CH:(c + 1) * CH], chunk(b.bg, c)[0:CH, :], ident[0:CH, 0:CH])
    ins.then_inc(K.sem("gdn_gates_t"), 1)
    e.eng.wait_ge(K.sem("gdn_begin"), 1)
    for r in range(3):
        job(e, c0 + r)

    def norm_sum(part, j, c):
        e.eng.wait_ge(K.sem("gdn_square"), j * 2 + part + 1)
        mm(bank_of(e, c)[:, :], ones, b.t[:, part, :], start=True, stop=True).then_inc(K.sem("gdn_norm_sum"), 1)

    for part in range(2):
        norm_sum(part, 0, c0 + part)
    job(e, c0 + 3)

    def head(i, more):
        S_, T_, U_ = b.s[0:CH, :], b.tt[0:CH, :], [u[0:CH, :] for u in b.um]

        def bank64(use):
            return ring.bank(use)[0:CH, :]

        fill = all_parts(*[job_parts(e, c0 + 4 + r, i) for r in range(4)]) if more else iter(())
        e.eng.wait_ge(K.sem("gdn_head"), i + 1)
        ring.claim("beta", i)
        settle(e)
        ring.written(mm(bank64("beta"), b.sel[0:H8, 0:CH], b.bg[0:H8, :], start=True, stop=True))
        ring.claim("grow", i)
        ring.written(mm(ring.bank("grow")[:, :], b.sel[32:40, :], b.eg[32:40, :], start=True, stop=True))
        ring.claim("gi", i)
        settle(e)
        ring.written(mm(bank64("gi"), b.sel[32:40, 0:CH], b.bg[32:40, :], start=True, stop=True))
        take(fill, 2)
        e.eng.wait_ge(K.sem("gdn_normed"), i * 2 + 2)
        for use, rhs in (("gram", 1), ("qk", 0)):
            ring.claim(use, i)
            settle(e)
            for c in range(NCH):
                ins = mm(chunk(bank64(use), c), chunk(b.x[:, 1, :], c), chunk(b.x[:, rhs, :], c), start=True, stop=True)
            ring.written(ins)
        def token_major(use, part):
            ring.claim(use, i)
            settle(e)
            for c in range(4):
                cc = c + (4 if use[-1] == "1" else 0)
                ins = nc.tensor.transpose(ring.bank(use)[0:CH, c * P:(c + 1) * P], chunk(b.x[:, part, :], cc), ident)
            ring.written(ins)

        token_major("kt0", 1)
        token_major("kt1", 1)
        take(fill, 3)
        e.eng.wait_ge(K.sem("gdn_s"), i + 1)
        ring.claim("t1", i)
        settle(e)
        for c in range(NCH):
            ins = nc.tensor.transpose(chunk(bank64("t1"), c), chunk(S_, c), ident[0:CH, 0:CH])
        ring.written(ins)
        token_major("vt0", 2)
        token_major("vt1", 2)
        take(fill, 2)
        for l in GDN_LEVELS:
            e.eng.wait_ge(K.sem("gdn_um"), i * 5 + l)
            ring.wait_read("t1" if l == 1 else f"dt{l - 1}", i)
            ring.claim(f"w{l}", i)
            settle(e)
            for c in range(NCH):
                ins = mm(chunk(bank64(f"w{l}"), c), chunk(U_[l % 2], c), chunk(T_, c), start=True, stop=True)
            ring.written(ins)
            take(fill, 2)
            ring.wait_read(f"w{l}", i)
            W = b.w[0:CH, :]
            if l > 1:
                ring.wait_read(f"ds{l - 1}", i)
            for use, lhs, rhs in ((f"dt{l}", S_, W), (f"ds{l}", W, S_)):
                if use in GDN_USES:
                    ring.claim(use, i)
                    settle(e)
                    for c in range(NCH):
                        ins = mm(chunk(bank64(use), c), chunk(lhs, c), chunk(rhs, c), start=True, stop=True)
                    ring.written(ins)
            take(fill, 0 if l < 5 else 2)
        ring.wait_read("ds5", i)
        ring.claim("wt", i)
        e.eng.wait_ge(K.sem("gdn_tok"), i + 1)
        settle(e)
        for c in range(NCH):
            ins = mm(chunk(ring.bank("wt"), c), b.kbe[:, c, :], chunk(S_, c), start=True, stop=True)
        ring.written(ins)
        take(fill, 2)
        e.eng.wait_ge(K.sem("gdn_o_free"), i + 1)
        O = K.ps[7]
        for c in range(NCH):
            st = b.st[:, c % 2, :]
            ring.claim(f"v{c}", i)
            vb = ring.bank(f"v{c}")[0:CH, 0:P]
            settle(e)
            ins = mm(vb, chunk(S_, c), b.vb[:, c, :], start=True, stop=c == 0)
            if c == 0:
                ring.wait_read("wt", i)
            else:
                ring.wait_read(f"k{c - 1}", i)
                settle(e)
                ins = mm(vb, chunk(b.nwt, c), st, start=False, stop=True)
            ring.written(ins)
            if c in (1, 2, 3):
                take(fill, 1)
            if c:
                mm(chunk(O, c), st, chunk(b.qd, c), start=True, stop=False)
            ring.wait_read(f"v{c}", i)
            vn = b.vn[0:CH, c % 2, :]
            settle(e)
            if c < NCH - 1:
                ring.claim(f"k{c}", i)
                settle(e)
                ring.written(mm(ring.bank(f"k{c}")[:, 0:P], b.kd[:, c, :], vn, start=True, stop=True))
            ins = mm(chunk(O, c), vn, chunk(b.qkt[0:CH, :], c), start=c == 0, stop=True)
            if more and c in (4, 5):
                norm_sum(c - 4, i + 1, c0 + c)
        ins.then_inc(K.sem("gdn_o"), 1)
        take(fill, 3)
        e.eng.wait_ge(K.sem("gdn_o_square"), i + 1)
        ring.claim("o_norm", i)
        ring.written(mm(ring.bank("o_norm")[:, :], ones, b.o, start=True, stop=True))
        take(fill, 5)

    with e.eng.Fori(0, H8 - 1) as i:
        head(i, True)
    head(H8 - 1, False)
    out_pe(e, "gdn_out", "gdn_y")


def gdn_act(e):
    K, b, nc, c0, st = e.K, gdn_buffers(e.K), e.K.nc, FIRST_JOB["gdn"], e.steps
    act = nc.scalar.activation
    ring = Ring(e, "gdn_aux", (4, 5, 6), GDN_USES)
    prenorm_act(e, "gdn")
    cb = FIRST_JOB["gdn_ba"]
    weight_high(e, cb + AHEAD)
    job_wait(e, cb)
    one = K.c("ones")[:, 0:1]
    act(b.bg[0:H8, :], bank_of(e, cb)[0:H8, :], ACT.Exp, scale=-1.0).then_inc(K.sem("gdn_beta_e"), 1)
    st.step(act(b.ea[32:40, 0:1], K.col("gdn_a_log", 0)[32:40, :], ACT.Exp))
    e.eng.wait_ge(K.sem("gdn_dt"), 1)
    st.step(act(b.eg[32:40, :], b.eg[32:40, :], ACT.Exp))
    st.wait()
    act(b.eg[32:40, :], b.eg[32:40, :], ACT.Ln, bias=one[32:40, :]).then_inc(K.sem("gdn_ln"), 1)
    e.eng.wait_ge(K.sem("gdn_gates"), 1)
    st.step(act(b.eg[32:40, :], b.bg[32:40, :], ACT.Exp))
    e.eng.wait_ge(K.sem("gdn_tok_in"), 1)
    st.wait()
    act(b.f1[0:CH], b.tok[0:CH, :, 32:40], ACT.Exp).then_inc(K.sem("gdn_f1_e"), 1)

    def fetch(r, i=None):
        j, c = (0, c0 + r) if i is None else (i + 1, c0 + 4 + r)
        job_wait(e, c, i)
        act(b.u[:, r, 3:515], bank_of(e, c)[:, :], ACT.Copy).then_inc(K.sem("gdn_fetched"), 1)
        if r == 2:
            e.eng.wait_ge(K.sem("gdn_fetched"), j * 3 + 3)
            release(e, c)

    def front(i=None):
        j, c = (0, c0) if i is None else (i + 1, c0 + 4)
        for part in range(3):
            e.eng.wait_ge(K.sem("gdn_conv"), j * 3 + part + 1)
            act(b.x[:, part, :], b.t[:, part, :], ACT.Silu).then_inc(K.sem("gdn_silu"), 1)
            if part < 2:
                e.eng.wait_ge(K.sem("gdn_silu"), j * 3 + part + 1)
                act(b.t[:, part, :], b.x[:, part, :], ACT.Square).then_inc(K.sem("gdn_square"), 1)
        for part in range(2):
            e.eng.wait_ge(K.sem("gdn_norm_sum"), j * 2 + part + 1)
            act(b.t[:, part, :], bank_of(e, c + part)[:, :], ACT.Ln, bias=K.c("eps")) \
                .then_inc(K.job_sems["bank"][(c + part) % SLOTS], 1)
        for part in range(2):
            evacuated(e, c + part, i)
            act(b.t[:, part, :], b.t[:, part, :], ACT.Exp, scale=-0.5).then_inc(K.sem("gdn_rstd"), 1)

    for r in range(3):
        weight_high(e, c0 + r + AHEAD)
        fetch(r)
    front()

    def head(i, more):
        e.eng.wait_ge(K.sem("gdn_decay_in"), i + 1)
        act(b.dt[0:CH, :], b.dt[0:CH, :], ACT.Exp).then_inc(K.sem("gdn_decay"), 1)
        ring.wait("t1", i)
        ring.read("t1", act(b.tt[0:CH, :], ring.bank("t1")[0:CH, :], ACT.Copy))
        for l in GDN_LEVELS:
            ring.wait(f"w{l}", i)
            ring.read(f"w{l}", act(b.w[0:CH, :], ring.bank(f"w{l}")[0:CH, :], ACT.Copy))
            if l == 1:
                weight_high(e, c0 + 3 + AHEAD, i)
                job_wait(e, c0 + 3, i)
                act(b.z, bank_of(e, c0 + 3)[:, :], ACT.Copy).then_inc(K.job_sems["bank"][(c0 + 3) % SLOTS], 1)
            if more and l == 2:
                weight_high(e, c0 + 4 + AHEAD, i)
            if more and l == 3:
                fetch(0, i)
            if more and l == 4:
                weight_high(e, c0 + 5 + AHEAD, i)
            if more and l == 5:
                fetch(1, i)
        ring.wait("wt", i)
        ring.read("wt", act(b.nwt, ring.bank("wt")[:, :], ACT.Copy, scale=-1.0))
        if more:
            weight_high(e, c0 + 6 + AHEAD, i)
            fetch(2, i)
        evacuated(e, c0 + 3, i)
        act(b.z, b.z, ACT.Silu).then_inc(K.sem("gdn_z"), 1)
        if more:
            front(i)
        e.eng.wait_ge(K.sem("gdn_o"), i + 1)
        act(b.o, K.ps[7][:, :], ACT.Square, scale=P ** -0.5).then_inc(K.sem("gdn_o_square"), 1)
        ring.wait("o_norm", i)
        ring.read("o_norm", act(b.o, ring.bank("o_norm")[:, :], ACT.Ln, bias=K.c("eps")))
        ring.wait_read("o_norm", i)
        act(b.o, b.o, ACT.Exp, scale=-0.5).then_inc(K.sem("gdn_o_rstd"), 1)
        y_pair_scalar(e, "gdn_y", i)

    with e.eng.Fori(0, H8 - 1) as i:
        head(i, True)
    head(H8 - 1, False)
    ahead_act(e, "gdn_out")


def gdn_dve(e):
    K, b, nc, c0, st, v = e.K, gdn_buffers(e.K), e.K.nc, FIRST_JOB["gdn"], e.steps, e.K.nc.vector
    ring = Ring(e, "gdn_aux", (4, 5, 6), GDN_USES)
    cb = FIRST_JOB["gdn_ba"]
    prenorm_dve(e, "gdn", "norm_w", 2 * DT, cb)
    st.step(v.memset(b.u[:, :, 0:3], 0.0))
    st.wait()
    e.eng.wait_ge(K.sem("gdn_beta_e"), 1)
    st.step(v.tensor_scalar(b.bg[0:H8, :], b.bg[0:H8, :], 1.0, None, ALU.add))
    st.step(v.memset(b.umat[0:CH, :], 0.0))
    st.wait()
    st.step(v.reciprocal(b.umat[0:H8, :], b.bg[0:H8, :]))
    x, eg, g = b.s[32:40, :], b.eg[32:40, :], b.umat[32:40, :]
    st.step(v.tensor_scalar(x, bank_of(e, cb)[32:40, :], K.col("gdn_dt_bias", 0)[32:40, :], None, ALU.add))
    st.wait()
    release(e, cb)
    v.scalar_tensor_tensor(eg, x, -1.0, x, ALU.mult, ALU.min).then_inc(K.sem("gdn_dt"), 1)
    e.eng.wait_ge(K.sem("gdn_dt"), 1)
    st.step(v.tensor_scalar(x, x, 0.0, None, ALU.max))
    st.wait()
    e.eng.wait_ge(K.sem("gdn_ln"), 1)
    st.step(v.tensor_tensor(x, x, eg, ALU.add))
    st.wait()
    st.step(v.tensor_scalar(x, x, b.ea[32:40, 0:1], -1.0, ALU.mult, ALU.mult))
    st.wait()
    st.step(v.tensor_tensor_scan(g, K.c("restart")[32:40, :], x, 0.0, ALU.mult, ALU.add))
    st.wait()
    v.tensor_copy(b.bg[0:CH, :], b.umat[0:CH, :]).then_inc(K.sem("gdn_gates"), 1)
    e.eng.wait_ge(K.sem("gdn_gates_t"), 1)
    tok = b.tok[0:CH]
    v.tensor_copy(tok, by_chunk(K.ps[4][0:CH, :])).then_inc(K.sem("gdn_tok_in"), 1)
    e.eng.wait_ge(K.sem("gdn_f1_e"), 1)
    v.tensor_tensor(b.f1[0:CH], b.f1[0:CH], tok[:, :, 0:H8], ALU.mult).then_inc(K.sem("gdn_begin"), 1)
    e.eng.wait_ge(K.sem("gdn_begin"), 1)
    ring.begin()
    e.eng.sem_inc(K.sem("gdn_o_free"), 1)
    n_ident = const_at("ident")

    def bc(a, n=CH):
        return a.unsqueeze(2).broadcast_to([CH, a.shape[1], n])

    def each(name):
        return K.c(name)[0:CH, 0:CH].unsqueeze(1).broadcast_to([CH, NCH, CH])

    def step(ins):
        st.step(ins)
        st.wait()

    def convolutions(i=None):
        j = 0 if i is None else i + 1
        step(v.tensor_copy(b.taps, K.param[:, bass.ds(j * 12 + K.cols["gdn_w_conv"], 12)]))
        for part in range(3):
            e.eng.wait_ge(K.sem("gdn_fetched"), j * 3 + part + 1)
            u, t = b.u[:, part, :], b.t[:, part, :]
            step(v.tensor_scalar(t, u[:, 0:S], b.taps[:, 4 * part:4 * part + 1], None, ALU.mult))
            yield
            for n in range(1, 4):
                ins = v.scalar_tensor_tensor(t, u[:, n:n + S], b.taps[:, 4 * part + n:4 * part + n + 1], t,
                                             ALU.mult, ALU.add)
                if n < 3:
                    step(ins)
                else:
                    ins.then_inc(K.sem("gdn_conv"), 1)
                yield

    def normalize(i=None):
        j = 0 if i is None else i + 1
        for part in range(2):
            e.eng.wait_ge(K.sem("gdn_rstd"), j * 2 + part + 1)
            v.scalar_tensor_tensor(b.x[:, part, :], b.x[:, part, :], P ** -0.5 if part == 0 else 1.0, b.t[:, part, :],
                                   ALU.mult, ALU.mult).then_inc(K.sem("gdn_normed"), 1)

    def select(j):
        st.step(v.tensor_copy(b.sel[0:H8, :], K.const[0:H8, bass.ds(j + n_ident, 1)].broadcast_to([H8, P])))
        st.step(v.tensor_copy(b.sel[32:40, :], K.const[32:40, bass.ds(j + n_ident + 32, 1)].broadcast_to([H8, P])))
        st.step(v.tensor_copy(b.hb[0:CH, :].unsqueeze(2), tok[:, :, bass.ds(j, 1)]))
        st.step(v.tensor_copy(b.hg[0:CH, :].unsqueeze(2), tok[:, :, bass.ds(j + 32, 1)]))
        step(v.tensor_copy(b.hf[0:CH, :].unsqueeze(2), b.f1[0:CH, :, bass.ds(j, 1)]))
        e.eng.sem_inc(K.sem("gdn_head"), 1)

    take(convolutions(), 12)
    normalize()
    select(0)

    def head(i, more):
        dt = by_chunk(b.dt[0:CH, :])
        ring.wait("grow", i)
        e.eng.wait_ge(K.sem("gdn_normed"), i * 2 + 2)
        step(v.tensor_copy(b.egl[:, :].unsqueeze(2), by_chunk(ring.bank("grow")[:, :])[:, :, CH - 1:CH]))
        ring.wait("gi", i)
        ring.read("gi", v.tensor_tensor(dt, by_chunk(ring.bank("gi")[0:CH, :]), bc(b.hg[0:CH, :]), ALU.subtract))
        ring.wait_read("gi", i)
        v.tensor_tensor(dt, dt, each("upto_neg"), ALU.add).then_inc(K.sem("gdn_decay_in"), 1)
        ring.read("grow", v.tensor_tensor(b.qd, b.x[:, 0, :], ring.bank("grow")[:, :], ALU.mult))
        e.eng.wait_ge(K.sem("gdn_decay"), i + 1)
        um = by_chunk(b.umat[0:CH, :])
        ring.read("beta", v.tensor_tensor(um, dt, by_chunk(ring.bank("beta")[0:CH, :]), ALU.mult))
        ring.wait_read("beta", i)
        ring.wait("gram", i)
        ring.read("gram", v.tensor_tensor(um, um, by_chunk(ring.bank("gram")[0:CH, :]), ALU.mult))
        ring.wait_read("gram", i)
        ring.wait("qk", i)
        ring.read("qk", v.tensor_tensor(by_chunk(b.qkt[0:CH, :]), by_chunk(ring.bank("qk")[0:CH, :]), dt, ALU.mult))
        S_, T_ = by_chunk(b.s[0:CH, :]), by_chunk(b.tt[0:CH, :])
        U_ = [by_chunk(u[0:CH, :]) for u in b.um]
        step(v.tensor_tensor(U_[0], um, each("level0"), ALU.mult))
        v.tensor_tensor(S_, each("ident"), U_[0], ALU.subtract).then_inc(K.sem("gdn_s"), 1)
        e.eng.wait_ge(K.sem("gdn_s"), i + 1)
        v.tensor_tensor(U_[1], um, each("level1"), ALU.mult).then_inc(K.sem("gdn_um"), 1)
        for half in range(2):
            cs = slice(4 * half, 4 * half + 4)
            use = f"kt{half}"
            ring.wait(use, i)
            src = ring.bank(use)[0:CH, :].rearrange("p (c d) -> p c d", d=P)
            step(v.tensor_tensor(b.kbe[:, cs, :], src, bc(b.hf[0:CH, cs], P), ALU.mult))
            last = dt[:, cs, CH - 1:CH].broadcast_to([CH, 4, P])
            ring.read(use, v.tensor_tensor(b.kd[:, cs, :], src, last, ALU.mult))
            ring.wait_read(use, i)
        for half in range(2):
            cs = slice(4 * half, 4 * half + 4)
            use = f"vt{half}"
            ring.wait(use, i)
            src = ring.bank(use)[0:CH, :].rearrange("p (c d) -> p c d", d=P)
            ring.read(use, v.tensor_tensor(b.vb[:, cs, :], src, bc(b.hb[0:CH, cs], P), ALU.mult))
            ring.wait_read(use, i)
        ring.wait_read("grow", i)
        ring.wait_read("qk", i)
        e.eng.sem_inc(K.sem("gdn_tok"), 1)
        for l in GDN_LEVELS:
            if l < 5:
                if l >= 2:
                    ring.wait(f"w{l - 1}", i)
                v.tensor_tensor(U_[(l + 1) % 2], um, each(f"level{l + 1}"), ALU.mult).then_inc(K.sem("gdn_um"), 1)
                ring.wait(f"dt{l}", i)
                ring.wait_read(f"w{l}", i)
                ring.read(f"dt{l}", v.tensor_tensor(b.tt[0:CH, :], b.tt[0:CH, :], ring.bank(f"dt{l}")[0:CH, :],
                                                    ALU.subtract))
                ring.wait(f"ds{l}", i)
                ring.read(f"ds{l}", v.tensor_tensor(b.s[0:CH, :], b.s[0:CH, :], ring.bank(f"ds{l}")[0:CH, :], ALU.subtract))
                ring.wait_read(f"ds{l}", i)
                ring.wait_read(f"dt{l}", i)
            else:
                ring.wait(f"ds{l}", i)
                ring.read(f"ds{l}", v.tensor_tensor(b.s[0:CH, :], b.s[0:CH, :], ring.bank(f"ds{l}")[0:CH, :], ALU.subtract))
                ring.wait_read(f"ds{l}", i)
        conv = convolutions(i) if more else iter(())
        for c in range(NCH):
            ring.wait(f"v{c}", i)
            ring.read(f"v{c}", v.tensor_copy(b.vn[0:CH, c % 2, :], ring.bank(f"v{c}")[0:CH, 0:P]))
            take(conv, 1)
            if c < NCH - 1:
                ring.wait(f"k{c}", i)
                src, new = ring.bank(f"k{c}")[:, 0:P], b.st[:, (c + 1) % 2, :]
                if c == 0:
                    ins = v.tensor_copy(new, src)
                else:
                    ring.wait_read(f"k{c - 1}", i)
                    ins = v.scalar_tensor_tensor(new, b.st[:, c % 2, :], b.egl[:, c:c + 1], src, ALU.mult, ALU.add)
                ring.read(f"k{c}", ins)
                take(conv, 1)
        if more:
            normalize(i)
            select(i + 1)
        e.eng.wait_ge(K.sem("gdn_o_rstd"), i + 1)
        step(v.scalar_tensor_tensor(b.o, K.ps[7][:, :], K.col("gdn_norm_w", 0), b.o, ALU.mult, ALU.mult))
        e.eng.sem_inc(K.sem("gdn_o_free"), 1)
        e.eng.wait_ge(K.sem("gdn_z"), i + 1)
        e.eng.wait_ge(K.sem("split_done"), i + FIRST_SPLIT["gdn_y"])
        v.tensor_tensor(K.y[:, 0, :], b.o, b.z, ALU.mult).then_inc(K.sem("y_done"), 1)
        y_pair_vector(e, "gdn_y", i)

    with e.eng.Fori(0, H8 - 1) as i:
        st.enter(i, GDN_STEPS)
        head(i, True)
        st.leave(H8 - 1)
    head(H8 - 1, False)
    out_residual_dve(e, "gdn_out")


GDN_STEPS = 20


TWO_PI_HI = 6.28125
TWO_PI_LO = 2.0 * math.pi - TWO_PI_HI
PI_BELOW = 3.1415925


def rope_angles(e, freq, cos, sin, n_before):
    K, v = e.K, e.K.nc.vector
    e.eng.wait_ge(K.sem("position"), 16 * (n_before + 1))
    ints = K.root[:, :].bitcast(I32)

    def step(ins):
        e.steps.step(ins)
        e.steps.wait()

    ang, turns = K.sq[:, 0, :], K.sq[:, 1, :]
    step(v.tensor_copy(ang, ints))
    step(v.tensor_scalar(ang, ang, K.c(freq), None, ALU.mult))
    for out, quarter in ((sin, 0.0), (cos, 0.25)):
        step(v.tensor_scalar(turns, ang, 1.0 / (2.0 * math.pi), quarter, ALU.mult, ALU.add))
        step(v.tensor_copy(ints, turns))
        step(v.tensor_copy(turns, ints))
        step(v.scalar_tensor_tensor(out, turns, -TWO_PI_HI, ang, ALU.mult, ALU.add))
        step(v.scalar_tensor_tensor(out, turns, -TWO_PI_LO, out, ALU.mult, ALU.add))
        if quarter:
            step(v.tensor_scalar(out, out, math.pi / 2, None, ALU.add))
        step(v.tensor_scalar(out, out, PI_BELOW, -PI_BELOW, ALU.min, ALU.max))
    e.eng.sem_inc(K.sem("angles"), 1)


def fetch_positions(e, source, n_before):
    e.eng.wait_ge(e.K.sem("position_room"), n_before + 1)
    e.eng.dma_start(e.K.root[:, :].bitcast(I32), source.broadcast_to([P, S])).then_inc(e.K.sem("position"), 16)


def rope_sines(e, cos, sin, n_before):
    e.eng.wait_ge(e.K.sem("angles"), n_before + 1)
    e.K.nc.scalar.activation(sin, sin, ACT.Sin).then_inc(e.K.sem("tables"), 1)
    e.K.nc.scalar.activation(cos, cos, ACT.Sin).then_inc(e.K.sem("tables"), 1)


SWA_G = [f"{w}_{s}" for s in range(2) for w in ("rot", "s00", "s01", "s10", "s11", "t00", "t01", "t10", "t11", "o")]
BLOCKS = [(0, 1), (1, 0), (1, 1), (2, 0), (2, 1), (3, 0), (3, 1)]


def swa_buffers(K):
    b = Names()
    (b.cos, b.sin, b.k, b.kr, b.v, b.q, b.qr, b.rot, b.z, b.v_tok, b.p0, b.p1, b.pt0, b.pt1, b.mx, b.es, b.sum, b.rec) = carve(
        K, (S,), (S,), (S,), (S,), (S,), (S,), (S,), (S,), (S,), (QT, P), (QT, 256), (QT, 256), (7, P), (7, P), (8,),
        (8,), (8,), (8,))
    return b


def swa_pe(e):
    K, b, nc, mm = e.K, swa_buffers(e.K), e.K.nc, e.K.nc.tensor.matmul
    ring, kv = Ring(e, "swa_aux", (4, 5, 6, 7), SWA_G), Ring(e, "swa_kv", (4, 5), ["rot", "v"])
    ident = K.c("ident")
    prenorm_pe(e, "swa", FIRST_JOB["swa0"])
    for p in range(2):
        c0 = FIRST_JOB[f"swa{p}"]
        if p:
            job(e, c0)
        job(e, c0 + 1)
        if p:
            for use in SWA_G[-4:]:
                ring.wait_read(use, 2 * p - 1)
        evacuated(e, c0)
        kv.claim("rot", p)
        kv.written(mm(kv.bank("rot")[:, :], K.c("rotate"), b.k, start=True, stop=True))
        evacuated(e, c0 + 1)
        kv.claim("v", p)
        for t in range(QT):
            ins = nc.tensor.transpose(kv.bank("v")[:, t * P:(t + 1) * P], b.v[:, t * P:(t + 1) * P], ident)
        kv.written(ins)
        kv.wait_read("rot", p)
        kv.wait_read("v", p)
        with e.eng.Fori(0, 2) as i:
            for s in range(2):
                trip, c, use = i + 2 * p, c0 + 2 + 2 * s, lambda name: f"{name}_{s}"
                job(e, c, i)
                evacuated(e, c, i)
                ring.claim(use("rot"), trip)
                ring.written(mm(ring.bank(use("rot"))[:, :], K.c("rotate"), b.q, start=True, stop=True))
                z = job_parts(e, c + 1, i)
                take(z, 4)
                e.eng.wait_ge(K.sem("swa_q"), trip * 2 + s + 1)
                settle(e)
                for half in range(2):
                    rows = slice(64 * half, 64 * half + 64)
                    for pair in range(2):
                        u = use(f"s{half}{pair}")
                        ring.claim(u, trip)
                        settle(e)
                        for q in (2 * pair, 2 * pair + 1):
                            first = P if q == 0 else 0
                            dst = ring.bank(u)[:, (q % 2) * 256 + first:(q % 2) * 256 + 256]
                            mm(dst, b.qr[rows, q * P:(q + 1) * P], b.kr[rows, (q - 1) * P + first:(q + 1) * P],
                               start=True, stop=False)
                            ins = mm(dst, K.ident_r[:, :], K.mask_r[:, first:2 * P], start=False, stop=True)
                        ring.written(ins)
                take(z, 4)
                for half in range(2):
                    e.eng.wait_ge(K.sem("swa_p"), trip * 4 + 2 * s + half + 1)
                    for n, (q, own) in enumerate(BLOCKS):
                        u = use(f"t{half}{n // 4}")
                        if n % 4 == 0:
                            ring.claim(u, trip)
                        ins = nc.tensor.transpose(ring.bank(u)[:, (n % 4) * P:(n % 4 + 1) * P],
                                                  (b.p0, b.p1)[half][:, q, own * P:(own + 1) * P], ident)
                        if n in (3, 6):
                            ring.written(ins)
                ring.claim(use("o"), trip)
                for half in range(2):
                    ring.wait_read(use(f"t{half}0"), trip)
                    ring.wait_read(use(f"t{half}1"), trip)
                    rows = slice(64 * half, 64 * half + 64)
                    settle(e)
                    for n, (q, own) in enumerate(BLOCKS):
                        ins = mm(ring.bank(use("o"))[rows, q * P:(q + 1) * P], b.v_tok[:, q - 1 + own, rows],
                                 (b.pt0, b.pt1)[half][:, n, :], start=own == 0 or q == 0, stop=own == 1)
                ring.written(ins)
    out_pe(e, "swa_out", "swa_y")


def swa_act(e):
    K, b, act = e.K, swa_buffers(e.K), e.K.nc.scalar.activation
    ring = Ring(e, "swa_aux", (4, 5, 6, 7), SWA_G)
    prenorm_act(e, "swa")
    fetch_positions(e, K.positions, 0)
    rope_sines(e, b.cos, b.sin, 0)

    def evacuate(c, dst, i=None, func=ACT.Copy, scale=1.0):
        job_wait(e, c, i)
        act(dst, bank_of(e, c)[:, :], func, scale=scale).then_inc(K.job_sems["bank"][c % SLOTS], 1)

    for p in range(2):
        c0 = FIRST_JOB[f"swa{p}"]
        weight_high(e, c0 + AHEAD)
        weight_high(e, c0 + 1 + AHEAD)
        evacuate(c0, b.k)
        evacuate(c0 + 1, b.v)
        with e.eng.Fori(0, 2) as i:
            for s in range(2):
                trip, c, use = i + 2 * p, c0 + 2 + 2 * s, lambda name: f"{name}_{s}"
                weight_high(e, c + AHEAD, i)
                evacuate(c, b.q, i, scale=64 ** -0.5)
                weight_high(e, c + 1 + AHEAD, i)
                for half in range(2):
                    ph = (b.p0, b.p1)[half]
                    e.eng.wait_ge(K.sem("swa_max"), trip * 4 + 2 * s + half + 1)
                    for q in range(QT):
                        first = P if q == 0 else 0
                        j = 4 * half + q
                        act(ph[:, q, first:256], ring.bank(use(f"s{half}{q // 2}"))[:, (q % 2) * 256 + first:(q % 2) * 256 + 256],
                            ACT.Exp, bias=b.mx[:, j:j + 1], accum_out=b.sum[:, j:j + 1]).then_inc(K.sem("swa_e"), 1)
                    act(b.es[:, 4 * half:4 * half + 4], b.es[:, 4 * half:4 * half + 4], ACT.Exp).then_inc(K.sem("swa_e"), 1)
                evacuate(c + 1, b.z, i, ACT.Silu)
                t = i * 2 + s + 4 * p
                y_pair_scalar(e, "swa_y", t)
    ahead_act(e, "swa_out")


def swa_dve(e):
    K, b, nc, st, v = e.K, swa_buffers(e.K), e.K.nc, e.steps, e.K.nc.vector
    ring, kv = Ring(e, "swa_aux", (4, 5, 6, 7), SWA_G), Ring(e, "swa_kv", (4, 5), ["rot", "v"])
    prenorm_dve(e, "swa", "norm_w", 3 * DT, FIRST_JOB["swa0"])
    e.eng.sem_inc(K.sem("position_room"), 1)
    rope_angles(e, "swa_freq", b.cos, b.sin, 0)
    ring.begin()
    kv.begin()
    e.eng.wait_ge(K.sem("tables"), 2)

    def step(ins):
        st.step(ins)
        st.wait()

    for p in range(2):
        c0 = FIRST_JOB[f"swa{p}"]
        evacuated(e, c0)
        step(v.tensor_tensor(b.kr, b.k, b.cos, ALU.mult))
        kv.wait("rot", p)
        kv.read("rot", v.tensor_tensor(b.rot, kv.bank("rot")[:, :], b.sin, ALU.mult))
        kv.wait_read("rot", p)
        step(v.tensor_tensor(b.kr, b.kr, b.rot, ALU.add))
        kv.wait("v", p)
        kv.read("v", v.tensor_copy(b.v_tok, kv.bank("v")[:, :].rearrange("p (a d) -> p a d", d=P)))
        with e.eng.Fori(0, 2) as i:
            st.enter(i, 2 * 22)
            for s in range(2):
                trip, c, use = i + 2 * p, c0 + 2 + 2 * s, lambda name: f"{name}_{s}"
                evacuated(e, c, i)
                step(v.tensor_tensor(b.qr, b.q, b.cos, ALU.mult))
                ring.wait(use("rot"), trip)
                ring.read(use("rot"), v.tensor_tensor(b.rot, ring.bank(use("rot"))[:, :], b.sin, ALU.mult))
                ring.wait_read(use("rot"), trip)
                step(v.tensor_tensor(b.qr, b.qr, b.rot, ALU.add))
                e.eng.sem_inc(K.sem("swa_q"), 1)

                def top(half):
                    j = 4 * half
                    for q in range(QT):
                        first = P if q == 0 else 0
                        u = use(f"s{half}{q // 2}")
                        ring.wait(u, trip)
                        st.step(v.tensor_reduce(b.mx[:, j + q:j + q + 1],
                                                ring.bank(u)[:, (q % 2) * 256 + first:(q % 2) * 256 + 256], AX.X, ALU.max))
                    st.wait()
                    sink = K.sinks[:, bass.ds(i * 2 + s + 4 * (2 * p + half), 1)].broadcast_to([P, QT])
                    mx, es = b.mx[:, j:j + 4], b.es[:, j:j + 4]
                    step(v.tensor_tensor(mx, mx, sink, ALU.max))
                    step(v.tensor_tensor(es, sink, mx, ALU.subtract))
                    step(v.tensor_scalar(mx, mx, -1.0, None, ALU.mult))
                    e.eng.sem_inc(K.sem("swa_max"), 1)

                def share(half):
                    j = 4 * half
                    ph, su, es, rec = (b.p0, b.p1)[half], b.sum[:, j:j + 4], b.es[:, j:j + 4], b.rec[:, j:j + 4]
                    e.eng.wait_ge(K.sem("swa_e"), trip * 20 + 10 * s + 5 * half + 5)
                    for pair in range(2):
                        e.eng.sem_inc(ring.free[ring.find(use(f"s{half}{pair}"))[1]], 1)
                    step(v.tensor_tensor(su, su, es, ALU.add))
                    step(v.reciprocal(rec, su))
                    st.step(v.tensor_scalar(ph[:, 0, P:256], ph[:, 0, P:256], rec[:, 0:1], None, ALU.mult))
                    v.tensor_tensor(ph[:, 1:4, :], ph[:, 1:4, :], rec[:, 1:4].unsqueeze(2).broadcast_to([P, 3, 256]),
                                    ALU.mult).then_inc(K.sem("swa_scaled"), 1)
                    st.wait()
                    e.eng.wait_ge(K.sem("swa_scaled"), trip * 4 + 2 * s + half + 1)
                    e.eng.sem_inc(K.sem("swa_p"), 1)

                def moved(half):
                    for n in range(2):
                        u, w = use(f"t{half}{n}"), (4, 3)[n]
                        ring.wait(u, trip)
                        ring.read(u, v.tensor_copy((b.pt0, b.pt1)[half][:, 4 * n:4 * n + w, :],
                                                   ring.bank(u)[:, 0:w * P].rearrange("p (a d) -> p a d", d=P)))

                top(0)
                top(1)
                share(0)
                share(1)
                moved(0)
                moved(1)
                ring.wait(use("o"), trip)
                evacuated(e, c + 1, i)
                t = i * 2 + s + 4 * p
                e.eng.wait_ge(K.sem("split_done"), t + FIRST_SPLIT["swa_y"])
                ring.read(use("o"), v.tensor_tensor(b.rot, ring.bank(use("o"))[:, :], b.z, ALU.mult))
                ring.wait_read(use("o"), trip)
                v.tensor_copy(K.y[:, 0, :], b.rot).then_inc(K.sem("y_done"), 1)
                y_pair_vector(e, "swa_y", t)
            st.leave(2)
    out_residual_dve(e, "swa_out")


def final_pe(e):
    stat_tensor(e, "final")


def final_act(e):
    stat_scalar(e, "final", e.K.X, lambda k: x_wait(e, "final", k))


def final_dve(e):
    K = e.K
    stat_vector(e, "final")
    for k in range(DT):
        K.nc.vector.scalar_tensor_tensor(K.X[:, k, :], K.X[:, k, :], K.col("final_norm_w", k), K.rstd[:, :],
                                         ALU.mult, ALU.mult).then_inc(K.sem("x_ready"), 1)
    e.eng.wait_ge(K.sem("x_ready"), X_DONE["final"])


def out_m_dve(e, phase, step, add=False, before_end=DT):
    K, c0 = e.K, FIRST_JOB[phase]
    count, base = K.sem("m_ready"), M_DONE[step] - before_end
    if phase in SUMMED_BY:
        e.steps.step(K.nc.vector.memset(K.root[:, :], 0.0))
        e.steps.wait()
    with e.eng.Fori(0, DT // SLOTS) as i:
        for r in range(SLOTS):
            job_wait(e, c0 + r, i)
            m = at(K.M, i * SLOTS + r)
            src = bank_of(e, c0 + r)[:, :]
            ins = K.nc.vector.tensor_tensor(m, src, m, ALU.add) if add else K.nc.vector.tensor_copy(m, src)
            ins.then_inc(count, 1)
            e.eng.wait_ge(count, i * SLOTS + r + base + 1)
            release(e, c0 + r)
            if phase in SUMMED_BY:
                add_square(e, SUMMED_BY[phase], i, r)


def post_pe(e, step):
    stat_tensor(e, step + "_post")


def post_act(e, step):
    K = e.K
    stat_scalar(e, step + "_post", K.M, lambda k: e.eng.wait_ge(K.sem("m_ready"), M_DONE[step] - DT + k + 1))


def post_dve(e, step, weight, col0, split=None):
    K, v = e.K, e.K.nc.vector
    stat_vector(e, step + "_post")
    for k in range(DT + 1):
        if k < DT:
            e.steps.step(v.scalar_tensor_tensor(K.M[:, k, :], K.M[:, k, :], K.col(weight, col0 + k), K.rstd[:, :],
                                                ALU.mult, ALU.mult))
        if k:
            e.eng.wait_ge(e.steps.sem, e.steps.base + e.steps.k - (1 if k < DT else 0))
            v.tensor_tensor(K.X[:, k - 1, :], K.X[:, k - 1, :], K.M[:, k - 1, :], ALU.add).then_inc(K.sem("x_ready"), 1)
        if split and k > 1:
            split_low(e, split, k - 2, k - 2, K.X[:, k - 2, :])
    if split:
        split_low(e, split, DT - 1, DT - 1, K.X[:, DT - 1, :])
    e.eng.wait_ge(K.sem("x_ready"), X_DONE[step])


HG_USES = ["vt0", "vt1", "at0", "at1", "ke0a", "ke0b", "ke1a", "ke1b", "ks0a", "ks0b", "ks1a", "ks1b", "o_norm"]
HG_ORDER = [list(range(NCH)), list(range(NCH))[::-1]]


def hg_buffers(K):
    b = Names()
    (b.f, b.g, b.k, b.eg, b.v_tok, b.ke0, b.ke1, b.st0, b.st1, b.gl, b.hp, b.mx, b.lb, b.one_lb, b.e3, b.t8) = carve(
        K, (2, S), (2, S), (2, S), (2, S), (NCH, P), (NCH, P), (NCH, P), (NCH, P), (NCH, P), (2, NCH), (4,), (DT,),
        (DT,), (DT,), (3, DT), (DT,))
    b.q, b.v, b.ki = K.root[:, :], K.rstd[:, :], K.sq
    return b


def hg_pe(e):
    K, b, nc, c0, mm = e.K, hg_buffers(e.K), e.K.nc, FIRST_JOB["hg"], e.K.nc.tensor.matmul
    ring = Ring(e, "hg_aux", (4, 5, 6), HG_USES)
    ident = K.c("ident")
    prenorm_pe(e, "hg", c0)
    for r in range(1, 4):
        job(e, c0 + r)
    e.eng.wait_ge(K.sem("hg_begin"), 1)

    def head(i, more):
        nxt = all_parts(*[job_parts(e, c0 + 4 + r, i) for r in range(4)]) if more else iter(())
        evacuated(e, c0 + 3, i)
        for n in range(2):
            use = f"vt{n}"
            ring.claim(use, i)
            settle(e)
            for c in range(4):
                ins = nc.tensor.transpose(ring.bank(use)[0:CH, c * P:(c + 1) * P], chunk(b.v, 4 * n + c), ident)
            ring.written(ins)
        take(nxt, 14)
        for d in range(2):
            e.eng.wait_ge(K.sem("hg_decayed"), i * 2 + d + 1)
            use = f"at{d}"
            ring.claim(use, i)
            settle(e)
            for c in range(NCH):
                ins = mm(chunk(ring.bank(use)[0:CH, :], c), chunk(b.ki[:, d, :], c), chunk(b.f[:, d, :], c),
                         start=True, stop=True)
            ring.written(ins)
            take(nxt, 1)
        for d in range(2):
            e.eng.wait_ge(K.sem("hg_k_end"), i * 2 + d + 1)
            for n in range(2):
                use = f"ke{d}{'ab'[n]}"
                ring.claim(use, i)
                settle(e)
                for c in range(4):
                    ins = nc.tensor.transpose(ring.bank(use)[0:CH, c * P:(c + 1) * P], chunk(b.k[:, d, :], 4 * n + c), ident)
                ring.written(ins)
            take(nxt, 1)
        for d in range(2):
            ke = (b.ke0, b.ke1)[d]
            ring.wait_read(f"ke{d}a", i)
            ring.wait_read(f"ke{d}b", i)
            for n in range(2):
                use = f"ks{d}{'ab'[n]}"
                ring.claim(use, i)
                settle(e)
                for m, c in enumerate(HG_ORDER[d][4 * n:4 * n + 4 - n]):
                    ins = mm(ring.bank(use)[:, m * P:(m + 1) * P], ke[0:CH, c, :], b.v_tok[0:CH, c, :], start=True, stop=True)
                ring.written(ins)
            take(nxt, 3)
        e.eng.wait_ge(K.sem("hg_states"), i + 1)
        O = K.ps[7]
        settle(e)
        for c in range(NCH):
            dst = chunk(O, c)
            mm(dst, b.v_tok[0:CH, c, :], chunk(b.g[0:CH, 0, :], c), start=True, stop=False)
            ins = mm(dst, b.v_tok[0:CH, c, :], chunk(b.g[0:CH, 1, :], c), start=False, stop=False)
            for d in range(2):
                first = c == HG_ORDER[d][0]
                if not first:
                    last = d == 1 or c == HG_ORDER[1][0]
                    ins = mm(dst, (b.st0, b.st1)[d][:, c, :], chunk(b.f[:, d, :], c), start=False, stop=last)
        ins.then_inc(K.sem("hg_o"), 1)
        take(nxt, 3)
        e.eng.wait_ge(K.sem("hg_o_square"), i + 1)
        ring.claim("o_norm", i)
        ring.written(mm(ring.bank("o_norm")[:, :], K.c("ones")[:, 0:P], b.g[:, 0, :], start=True, stop=True))
        take(nxt, 5)

    with e.eng.Fori(0, H8 - 1) as i:
        head(i, True)
    head(H8 - 1, False)
    c0 = FIRST_JOB["hg_gate"]
    with e.eng.Fori(0, DT // SLOTS) as i:
        for r in range(SLOTS):
            job(e, c0 + r, i)
    out_pe(e, "hg_out", "hg_y")
    post_pe(e, "hg")


def hg_act(e):
    K, b, nc, c0, act, st = e.K, hg_buffers(e.K), e.K.nc, FIRST_JOB["hg"], e.K.nc.scalar.activation, e.steps
    ring = Ring(e, "hg_aux", (4, 5, 6), HG_USES)
    e.eng.wait_ge(K.sem("hg_lb_in"), 1)
    act(b.e3, b.e3, ACT.Exp).then_inc(K.sem("hg_lb_e"), 1)
    prenorm_act(e, "hg")
    for r in range(4):
        weight_high(e, c0 + r + AHEAD)

    def gates(i=None):
        for d in range(2):
            c = c0 + 1 + d if i is None else c0 + 5 + d
            job_wait(e, c, i)
            act(b.f[:, d, :], bank_of(e, c)[:, :], ACT.Sigmoid).then_inc(K.job_sems["bank"][c % SLOTS], 1)

    def head(i, more):
        for r, dst, func, scale in ((0, b.q, ACT.Copy, P ** -0.5), (3, b.v, ACT.Copy, 1.0)):
            job_wait(e, c0 + r, i)
            act(dst, bank_of(e, c0 + r)[:, :], func, scale=scale).then_inc(K.job_sems["bank"][(c0 + r) % SLOTS], 1)
        if more:
            weight_high(e, c0 + 4 + AHEAD, i)
        for d in range(2):
            e.eng.wait_ge(K.sem("hg_f"), i * 2 + d + 1)
            act(b.eg[:, d, :], b.f[:, d, :], ACT.Ln).then_inc(K.sem("hg_log"), 1)
        for d in range(2):
            e.eng.wait_ge(K.sem("hg_cum"), i * 2 + d + 1)
            act(b.ki[:, d, :], b.g[:, d, :], ACT.Exp, scale=-1.0).then_inc(K.sem("hg_exp"), 1)
            act(b.eg[:, d, :], b.g[:, d, :], ACT.Exp).then_inc(K.sem("hg_exp"), 1)
        for d in range(2):
            e.eng.wait_ge(K.sem("hg_to_end"), i * 2 + d + 1)
            act(b.g[:, d, :], b.g[:, d, :], ACT.Exp).then_inc(K.sem("hg_end_e"), 1)
        if more:
            weight_high(e, c0 + 5 + AHEAD, i)
        for d in range(2):
            for n in range(2):
                use = f"ke{d}{'ab'[n]}"
                ring.wait(use, i)
                ring.read(use, act((b.ke0, b.ke1)[d][0:CH, 4 * n:4 * n + 4, :],
                                   ring.bank(use)[0:CH, :].rearrange("p (c d) -> p c d", d=P), ACT.Copy))
        if more:
            weight_high(e, c0 + 6 + AHEAD, i)
            weight_high(e, c0 + 7 + AHEAD, i)
        e.eng.wait_ge(K.sem("hg_o"), i + 1)
        act(b.g[:, 0, :], K.ps[7][:, :], ACT.Square, scale=P ** -0.5).then_inc(K.sem("hg_o_square"), 1)
        if more:
            gates(i)
        ring.wait("o_norm", i)
        ring.read("o_norm", act(b.g[:, 0, :], ring.bank("o_norm")[:, :], ACT.Ln, bias=K.c("eps")))
        ring.wait_read("o_norm", i)
        act(b.g[:, 0, :], b.g[:, 0, :], ACT.Exp, scale=-0.5).then_inc(K.sem("hg_o_rstd"), 1)

    gates()
    with e.eng.Fori(0, H8 - 1) as i:
        head(i, True)
    head(H8 - 1, False)
    c0 = FIRST_JOB["hg_gate"]
    split = FIRST_SPLIT["hg_y"]
    with e.eng.Fori(0, DT // SLOTS) as i:
        for r in range(SLOTS):
            weight_high(e, c0 + r + AHEAD, i)
            job_wait(e, c0 + r, i)
            e.eng.wait_ge(K.sem("y_done"), i * SLOTS + r + split)
            act(b.q, bank_of(e, c0 + r)[:, :], ACT.Silu).then_inc(K.job_sems["bank"][(c0 + r) % SLOTS], 1)
            y_pair_scalar(e, "hg_y", i * SLOTS + r)
    ahead_act(e, "hg_out")
    post_act(e, "hg")


def hg_dve(e):
    K, b, nc, c0, st, v = e.K, hg_buffers(e.K), e.K.nc, FIRST_JOB["hg"], e.steps, e.K.nc.vector
    ring = Ring(e, "hg_aux", (4, 5, 6), HG_USES)

    def step(ins):
        st.step(ins)
        st.wait()

    rows = K.param[:, K.cols["hg_lb_logits_2"]:K.cols["hg_lb_logits_2"] + 3 * DT].rearrange("p (a t) -> p a t", a=3)
    step(v.tensor_tensor(b.mx, rows[:, 0, :], rows[:, 1, :], ALU.max))
    step(v.tensor_tensor(b.mx, b.mx, rows[:, 2, :], ALU.max))
    v.tensor_tensor(b.e3, rows, b.mx.unsqueeze(1).broadcast_to([P, 3, DT]), ALU.subtract).then_inc(K.sem("hg_lb_in"), 1)
    prenorm_dve(e, "hg", "pre_mix_norm_2", 0, FIRST_JOB["hg"])
    e.eng.wait_ge(K.sem("hg_lb_e"), 1)
    step(v.tensor_tensor(b.t8, b.e3[:, 0, :], b.e3[:, 1, :], ALU.add))
    step(v.tensor_tensor(b.t8, b.t8, b.e3[:, 2, :], ALU.add))
    step(v.reciprocal(b.t8, b.t8))
    step(v.tensor_tensor(b.lb, b.e3[:, 0, :], b.t8, ALU.mult))
    step(v.tensor_scalar(b.one_lb, b.lb, -1.0, 1.0, ALU.mult, ALU.add))
    ring.begin()
    e.eng.sem_inc(K.sem("hg_begin"), 1)

    def head(i, more):
        step(v.tensor_copy(b.hp[:, 0:1], b.lb[:, bass.ds(i, 1)]))
        step(v.tensor_copy(b.hp[:, 1:2], b.one_lb[:, bass.ds(i, 1)]))
        step(v.tensor_copy(b.hp[:, 2:3], K.param[:, bass.ds(i + K.cols["hg_o_norm_2"], 1)]))
        for d in range(2):
            f = b.f[:, d, :]
            evacuated(e, c0 + 1 + d, i)
            st.step(v.tensor_scalar(f, f, b.hp[:, 1:2], b.hp[:, 0:1], ALU.mult, ALU.add))
            st.wait()
            e.eng.sem_inc(K.sem("hg_f"), 1)
        for d in range(2):
            step(v.tensor_scalar(b.k[:, d, :], b.f[:, d, :], -1.0, 1.0, ALU.mult, ALU.add))
        for n in range(2):
            use = f"vt{n}"
            ring.wait(use, i)
            ring.read(use, v.tensor_copy(b.v_tok[0:CH, 4 * n:4 * n + 4, :],
                                         ring.bank(use)[0:CH, :].rearrange("p (c d) -> p c d", d=P)))
        for d in range(2):
            e.eng.wait_ge(K.sem("hg_log"), i * 2 + d + 1)
            g, lg = b.g[:, d, :], b.eg[:, d, :]
            if d:
                g, lg = g[:, ::-1], lg[:, ::-1]
            step(v.tensor_tensor_scan(g, K.c("restart"), lg, 0.0, ALU.mult, ALU.add))
            e.eng.sem_inc(K.sem("hg_cum"), 1)
        for d in range(2):
            end = CH - 1 if d == 0 else 0
            g = b.g[:, d, :]
            step(v.tensor_copy(b.gl[:, d, :].unsqueeze(2), by_chunk(g)[:, :, end:end + 1]))
            e.eng.wait_ge(K.sem("hg_exp"), i * 4 + 2 * d + 2)
            st.step(v.tensor_tensor(b.ki[:, d, :], b.ki[:, d, :], b.k[:, d, :], ALU.mult))
            st.step(v.tensor_tensor(b.f[:, d, :], b.q, b.eg[:, d, :], ALU.mult))
            step(v.tensor_tensor(by_chunk(g), b.gl[:, d, :].unsqueeze(2).broadcast_to([P, NCH, CH]), by_chunk(g), ALU.subtract))
            e.eng.sem_inc(K.sem("hg_decayed"), 1)
            e.eng.sem_inc(K.sem("hg_to_end"), 1)
        for d in range(2):
            e.eng.wait_ge(K.sem("hg_end_e"), i * 2 + d + 1)
            step(v.tensor_tensor(b.k[:, d, :], b.k[:, d, :], b.g[:, d, :], ALU.mult))
            e.eng.sem_inc(K.sem("hg_k_end"), 1)
        for d in range(2):
            use = f"at{d}"
            ring.wait(use, i)
            mask = K.c("upto" if d == 0 else "from")[0:CH, 0:CH].unsqueeze(1).broadcast_to([CH, NCH, CH])
            ring.read(use, v.tensor_tensor(by_chunk(b.g[0:CH, d, :]), by_chunk(ring.bank(use)[0:CH, :]), mask, ALU.mult))
        for d in range(2):
            order, S_ = HG_ORDER[d], (b.st0, b.st1)[d]
            end = CH - 1 if d == 0 else 0
            for n in range(7):
                c, nxt = order[n], order[n + 1]
                use = f"ks{d}{'ab'[n // 4]}"
                if n % 4 == 0:
                    ring.wait(use, i)
                src = ring.bank(use)[:, (n % 4) * P:(n % 4 + 1) * P]
                if n == 0:
                    ins = v.tensor_copy(S_[:, nxt, :], src)
                else:
                    ins = v.scalar_tensor_tensor(S_[:, nxt, :], S_[:, c, :], b.eg[:, d, c * CH + end:c * CH + end + 1], src,
                                                 ALU.mult, ALU.add)
                step(ins)
                if n in (3, 6):
                    e.eng.sem_inc(ring.free[ring.find(use)[1]], 1)
        e.eng.sem_inc(K.sem("hg_states"), 1)
        e.eng.wait_ge(K.sem("hg_o_rstd"), i + 1)
        step(v.scalar_tensor_tensor(at(K.M, i), K.ps[7][:, :], b.hp[:, 2:3], b.g[:, 0, :], ALU.mult, ALU.mult))

    with e.eng.Fori(0, H8 - 1) as i:
        st.enter(i, HG_STEPS)
        head(i, True)
        st.leave(H8 - 1)
    head(H8 - 1, False)
    c0 = FIRST_JOB["hg_gate"]
    with e.eng.Fori(0, DT // SLOTS) as i:
        for r in range(SLOTS):
            t = i * SLOTS + r
            evacuated(e, c0 + r, i)
            e.eng.wait_ge(K.sem("split_done"), t + FIRST_SPLIT["hg_y"])
            v.tensor_tensor(K.y[:, 0, :], at(K.M, t), b.q, ALU.mult).then_inc(K.sem("y_done"), 1)
            y_pair_vector(e, "hg_y", t)
    out_m_dve(e, "hg_out", "hg")
    post_dve(e, "hg", "post_mix_norm_2", 0)


HG_STEPS = 34


TRIP = DT // SLOTS


def mlp_pe(e, name):
    stat_tensor(e, name)
    c0 = FIRST_JOB[name]
    with e.eng.Fori(0, 4) as q:
        with e.eng.Fori(0, TRIP) as i:
            for r in range(SLOTS):
                if r == 0:
                    job_with_waits(e, c0, q * 2 * TRIP + i, A_TILES, name + "_h")
                else:
                    job(e, c0 + r, q * 2 * TRIP + i)
        with e.eng.Fori(0, TRIP) as i:
            for r in range(SLOTS):
                if r == 0:
                    job_with_waits(e, c0 + DT, q * 2 * TRIP + i, B_TILES, name + "_y", q * DT)
                else:
                    job(e, c0 + DT + r, q * 2 * TRIP + i, B_TILES)
    post_pe(e, name)


def mlp_buffers(K):
    return K.work[:, 0:S]


def mlp_act(e, name):
    K, relu, c0 = e.K, mlp_buffers(e.K), FIRST_JOB[name]
    prenorm_act(e, name)
    with e.eng.Fori(0, 4) as q:
        with e.eng.Fori(0, TRIP) as i:
            for r in range(SLOTS):
                trip, n = q * 2 * TRIP + i, i * SLOTS + r
                weight_high(e, c0 + r + AHEAD, trip)
                job_wait(e, c0 + r, trip)
                e.eng.wait_ge(K.sem("y_done"), q * DT + n + FIRST_SPLIT[name + "_y"])
                K.nc.scalar.activation(relu, bank_of(e, c0 + r)[:, :], ACT.Relu).then_inc(K.sem("relu_done"), 1)
                e.eng.wait_ge(K.sem("y_done"), q * DT + n + FIRST_SPLIT[name + "_y"] + 1)
                K.nc.scalar.activation(at(K.act_hi, n + DT), K.y[:, 0, :], ACT.Copy).then_inc(K.sem("split_high_done"), 1)
        with e.eng.Fori(0, TRIP) as i:
            for r in range(SLOTS):
                weight_high(e, c0 + DT + r + AHEAD, q * 2 * TRIP + i)
    post_act(e, name)


def mlp_dve(e, name, layer):
    K, relu, c0, v = e.K, mlp_buffers(e.K), FIRST_JOB[name], e.K.nc.vector
    relus = 4 * DT * (XSTEPS[:XSTEPS.index(name)].count("mlp0"))
    for k in range(DT):
        e.steps.step(v.memset(K.M[:, k, :], 0.0))
    prenorm_dve(e, name, "pre_mlp_norm_2", layer * DT, c0)
    e.steps.wait()
    with e.eng.Fori(0, 4) as q:
        with e.eng.Fori(0, TRIP) as i:
            for r in range(SLOTS):
                trip, n = q * 2 * TRIP + i, i * SLOTS + r
                first = q * DT + n + FIRST_SPLIT[name + "_y"]
                e.eng.wait_ge(K.sem("relu_done"), q * DT + n + relus + 1)
                e.eng.wait_ge(K.sem("split_done"), first)
                v.scalar_tensor_tensor(K.y[:, 0, :], bank_of(e, c0 + r)[:, :], 0.0, relu, ALU.max, ALU.mult) \
                    .then_inc(K.sem("y_done"), 1)
                e.eng.wait_ge(K.sem("y_done"), first + 1)
                release(e, c0 + r)
                e.eng.wait_ge(K.sem("split_high_done"), first + 1)
                v.tensor_tensor(at(K.act_lo, n + DT), K.y[:, 0, :], at(K.act_hi, n + DT).bitcast(F32),
                                ALU.subtract).then_inc(K.sem("split_done"), 1)
        with e.eng.Fori(0, TRIP) as i:
            for r in range(SLOTS):
                trip, n = q * 2 * TRIP + i, i * SLOTS + r
                m_before = q * DT + n + M_DONE[name] - 4 * DT
                if r == 0:
                    e.eng.wait_ge(K.sem("m_ready"), m_before)
                job_wait(e, c0 + DT + r, trip)
                m = at(K.M, n)
                v.tensor_tensor(m, bank_of(e, c0 + r)[:, :], m, ALU.add).then_inc(K.sem("m_ready"), 1)
                e.eng.wait_ge(K.sem("m_ready"), m_before + 1)
                release(e, c0 + DT + r)
    post_dve(e, name, "post_mlp_norm_2", layer * DT, f"ple{layer}_h")


PLE_USES = ["e0", "e1", "e2", "e3"]


def ple_embedding(K):
    return K.work[:, S:3 * S].rearrange("p (a s) -> p a s", a=2)


def ple_pe(e, name):
    ring = Ring(e, "ple_aux", (4, 5, 6, 7), PLE_USES)
    c0 = FIRST_JOB[name + "_gate"]
    with e.eng.Fori(0, TRIP) as i:
        for r in range(SLOTS):
            if r == 0:
                job_with_waits(e, c0, i, A_TILES, name + "_h")
            else:
                job(e, c0 + r, i)
    c0 = FIRST_JOB[name + "_proj"]
    split_wait(e, name + "_p", 2)
    for k in range(2):
        job_start(e, c0 + k)
        for t, use in enumerate(PLE_USES):
            ring.claim(use, NTH_PLE[name] * 2 + k)
            ring.written(product(e, c0 + k, ring.bank(use)[:, :], B_TILES[:2], 2 * t))
        e.eng.wait_ge(ring.ready, (NTH_PLE[name] * 2 + k + 1) * len(PLE_USES))
        e.eng.sem_inc(e.K.job_sems["done"], 1)
    ring.wait_read("e3", NTH_PLE[name] * 2 + 1)
    post_pe(e, name)


def ple_act(e, name, layer):
    K, act, emb = e.K, e.K.nc.scalar.activation, ple_embedding(e.K)
    x_wait(e, name, 0)
    e.eng.dma_start(emb, K.p_t[layer].rearrange("(t p) s -> p t s", p=P)).then_inc(K.sem("embedding"), 16)
    for k in range(DT):
        x_wait(e, name, k)
        act(K.act_hi[:, k, :], K.X[:, k, :], ACT.Copy).then_inc(K.sem("split_high_done"), 1)
    e.eng.wait_ge(K.sem("embedding"), 16 * (NTH_PLE[name] + 1))
    for k in range(2):
        act(K.act_hi[:, DT + k, :], emb[:, k, :], ACT.Copy).then_inc(K.sem("split_high_done"), 1)
    c0 = FIRST_JOB[name + "_gate"]
    with e.eng.Fori(0, TRIP) as i:
        for r in range(SLOTS):
            weight_high(e, c0 + r + AHEAD, i)
            job_wait(e, c0 + r, i)
            act(at(K.M, i * SLOTS + r), bank_of(e, c0 + r)[:, :], ACT.Sigmoid).then_inc(K.job_sems["bank"][(c0 + r) % SLOTS], 1)
    for k in range(2):
        weight_high(e, FIRST_JOB[name + "_proj"] + k + AHEAD)
    post_act(e, name)


def ple_dve(e, name, layer):
    K, v, emb = e.K, e.K.nc.vector, ple_embedding(e.K)
    ring = Ring(e, "ple_aux", (4, 5, 6, 7), PLE_USES)
    if NTH_PLE[name] == 0:
        ring.begin()
    e.eng.sem_inc(K.sem("y_done"), DT + 2)
    for k in range(2):
        split_low(e, name + "_p", k, DT + k, emb[:, k, :])
    gate, proj = FIRST_JOB[name + "_gate"], FIRST_JOB[name + "_proj"]
    for n in range(DT):
        use = PLE_USES[n % 4]
        if n % 4 == 0:
            job_wait(e, proj + n // 4)
            release(e, proj + n // 4)
        ring.wait(use, NTH_PLE[name] * 2 + n // 4)
        evacuated(e, gate + n)
        v.tensor_tensor(K.M[:, n, :], ring.bank(use)[:, :], K.M[:, n, :], ALU.mult).then_inc(K.sem("m_ready"), 1)
        e.eng.wait_ge(K.sem("m_ready"), M_DONE[name] - DT + n + 1)
        e.eng.sem_inc(ring.free[ring.find(use)[1]], 1)
    post_dve(e, name, "ple_norm_2", layer * DT)


ROPE_TURN = ["second", "rot0", "rot1"]


def mla_uses():
    return [f"{u}_{s}" for s in range(2) for u in MLA_ORDER]


MLA_ORDER = ["n1", "k0", "k1", "v1", "s00", "s10", "s01", "vt0", "s11", "vt1", "t00", "t10", "s02", "s12",
             "t01", "t11", "s03", "s13", "t02", "t12", "t03", "t13", "o0", "o1"]
MLA_VECTOR_ORDER = ["k0", "k1", "s00", "s10", "t00", "s01", "t10", "vt0", "s11", "t01", "vt1", "t11", "s02", "s12",
                    "t02", "s03", "t12", "s13", "t03", "t13", "o0", "o1"]


def mla_buffers(K):
    b = Names()
    (qr, v_tok0, v_tok1, p, pt0, pt1, mx, sums, rec) = carve(
        K, (DT, S), (QT, P), (QT, P), (2, S), (QT, S), (QT, S), (4,), (4,), (4,))
    b.qr = [[qr[:, 2 * k:2 * k + 2, :] for k in range(2 * part, 2 * part + 2)] for part in range(2)]
    masks = const_at("upto")
    b.kn = K.const[:, masks:masks + 2 * S].rearrange("p (a s) -> p a s", a=2)
    b.kr, b.v = K.rstd[:, :], pt1[:, 0:2, :]
    b.p = [[p[:, 0, :], p[:, 1, :]], [K.sq[:, 0, :], K.sq[:, 1, :]]]
    b.v_tok, b.pt = [v_tok0, v_tok1], [pt0, pt1]
    b.stat = lambda a, h, q: a[:, 2 * h + q % 2:2 * h + q % 2 + 1]
    b.mx, b.sum, b.rec = mx, sums, rec
    b.qn, b.qs = K.y, K.root[:, :]
    b.cos, b.sin, b.rot, b.k_raw = pt0[:, 0, :], pt0[:, 1, :], pt0[:, 2, :], pt0[:, 3, :]
    return b


def mla_turned(b, t):
    return b.qr[t // 4][t % 2][:, t // 2 % 2, :]


def mla_pe(e):
    K, b, nc, mm, c0 = e.K, mla_buffers(e.K), e.K.nc, e.K.nc.tensor.matmul, FIRST_JOB["mla_in"]
    ident = K.c("ident")
    turn, key = Ring(e, "mla_rope", (4, 5, 6), ROPE_TURN), Ring(e, "mla_key", (4,), ["rot"])
    ring = Ring(e, "mla_aux", (4, 5, 6, 7), mla_uses())
    prenorm_pe(e, "mla", c0)
    for r in range(1, 6):
        job(e, c0 + r)
    stat_tensor(e, "mla_q")
    evacuated(e, c0 + 5)
    key.claim("rot", 0)
    key.written(mm(key.bank("rot")[:, :], K.c("rotate"), b.k_raw, start=True, stop=True))
    stat_tensor(e, "mla_kv")
    split_wait(e, "mla_cq", 3)
    key.wait_read("rot", 0)
    c0 = FIRST_JOB["mla_rope"]
    for k in range(4):
        job_start(e, c0 + k)
        product(e, c0 + k, bank_of(e, c0 + k)[:, :], [8, 9, 10])
        turn.claim("second", k)
        ins = product(e, c0 + k, turn.bank("second")[:, :], [8, 9, 10], 3)
        turn.written(ins)
        e.eng.wait_ge(turn.ready, k * len(ROPE_TURN) + 1)
        e.eng.sem_inc(K.job_sems["done"], 1)
        evacuated(e, c0 + k)
        turn.wait_read("second", k)
        for s in range(2):
            turn.claim(f"rot{s}", k)
            turn.written(mm(turn.bank(f"rot{s}")[:, :], K.c("rotate"), mla_turned(b, 2 * k + s), start=True, stop=True))
    turn.wait_read("rot0", 3)
    turn.wait_read("rot1", 3)
    split_wait(e, "mla_ckv", 2)
    e.eng.wait_ge(K.sem("mla_begin"), 1)
    for part, out in ((0, "mla_outa"), (1, "mla_outb")):
        c0 = FIRST_JOB[("mla_a", "mla_b")[part]]
        with e.eng.Fori(0, 2) as i:
            for s in range(2):
                trip, c = i + 2 * part, c0 + 2 * s
                mla_pair_pe(e, b, ring, ident, trip, c, i, s)
        out_pe(e, out, "mla_y", A_TILES, part * DT)
    post_pe(e, "mla")


def mla_pair_pe(e, b, ring, ident, trip, c, i, s):
    K, nc, mm = e.K, e.K.nc, e.K.nc.tensor.matmul
    job_start(e, c, i)
    product(e, c, bank_of(e, c)[:, :], [8, 9, 10])
    ring.claim(f"n1_{s}", trip)
    ring.written(product(e, c, ring.bank(f"n1_{s}")[:, :], [8, 9, 10], 3))
    ring.wait(f"n1_{s}", trip)
    e.eng.sem_inc(K.job_sems["done"], 1)
    job_start(e, c + 1, i)
    for use, chunk0 in (("k0", 0), ("k1", 2), ("v1", 6)):
        ring.claim(f"{use}_{s}", trip)
        ring.written(product(e, c + 1, ring.bank(f"{use}_{s}")[:, :], [11, 12], chunk0))
    product(e, c + 1, bank_of(e, c + 1)[:, :], [11, 12], 4).then_inc(K.job_sems["done"], 1)
    e.eng.wait_ge(K.sem("mla_staged"), trip * 2 + s + 1)
    evacuated(e, c, i)
    for what in MLA_ORDER[4:]:
        use, h, q = f"{what}_{s}", int(what.strip("stov")[0]), int(what[-1])
        ring.claim(use, trip)
        dst = ring.bank(use)
        if what[0] == "s":
            if q == 0:
                ring.wait_read(f"k{h}_{s}", trip)
                ring.wait_read(f"n1_{s}", trip)
            settle(e)
            rows = slice(64 * h, 64 * h + 64)
            mm(dst[:, :], b.qn[:, h, q * P:(q + 1) * P], b.kn[:, h, :], start=True, stop=False)
            ins = mm(dst[:, :], b.qs[rows, q * P:(q + 1) * P], b.kr[rows, :], start=False, stop=True)
        elif what[0] == "v":
            if h:
                ring.wait_read(f"v1_{s}", trip)
            else:
                evacuated(e, c + 1, i)
            settle(e)
            for t in range(QT):
                ins = nc.tensor.transpose(dst[:, t * P:(t + 1) * P], b.v[:, h, t * P:(t + 1) * P], ident)
        elif what[0] == "t":
            e.eng.wait_ge(K.sem(f"mla_p{h}"), trip * 8 + s * 4 + q + 1)
            settle(e)
            for t in range(QT):
                ins = nc.tensor.transpose(dst[:, t * P:(t + 1) * P], b.p[h][q % 2][:, t * P:(t + 1) * P], ident)
        else:
            ring.wait_read(f"t{h}3_{s}", trip)
            if h == 0:
                ring.wait_read(f"vt0_{s}", trip)
            settle(e)
            for t in range(QT):
                ins = mm(dst[:, :], b.v_tok[h][:, t, :], b.pt[h][:, t, :], start=t == 0, stop=t == QT - 1)
        ring.written(ins)


def mla_act(e):
    K, b, act, c0 = e.K, mla_buffers(e.K), e.K.nc.scalar.activation, FIRST_JOB["mla_in"]
    turn = Ring(e, "mla_rope", (4, 5, 6), ROPE_TURN)
    ring = Ring(e, "mla_aux", (4, 5, 6, 7), mla_uses())
    scale = (128 + 64) ** -0.5
    prenorm_act(e, "mla")
    fetch_positions(e, K.positions_2, ROPES_BEFORE)
    for r in range(6):
        weight_high(e, c0 + r + AHEAD)
        job_wait(e, c0 + r)
        bank = K.job_sems["bank"][(c0 + r) % SLOTS]
        act(K.M[:, r, :] if r < 5 else b.k_raw, bank_of(e, c0 + r)[:, :], ACT.Copy).then_inc(bank, 1)
    rope_sines(e, b.cos, b.sin, ROPES_BEFORE)
    stat_scalar(e, "mla_q", K.M, lambda k: evacuated(e, c0 + k))
    norm_split_scalar(e, "mla_cq", 3, DT)
    stat_scalar(e, "mla_kv", K.M[:, 3:5, :], lambda k: evacuated(e, c0 + 3 + k))
    norm_split_scalar(e, "mla_ckv", 2, DT + 3)
    c0 = FIRST_JOB["mla_rope"]
    for k in range(4):
        weight_high(e, c0 + k + AHEAD)
        job_wait(e, c0 + k)
        act(mla_turned(b, 2 * k), bank_of(e, c0 + k)[:, :], ACT.Copy, scale=scale).then_inc(K.job_sems["bank"][(c0 + k) % SLOTS], 1)
        turn.wait("second", k)
        turn.read("second", act(mla_turned(b, 2 * k + 1), turn.bank("second")[:, :], ACT.Copy, scale=scale))
    for part, out in ((0, "mla_outa"), (1, "mla_outb")):
        c0 = FIRST_JOB[("mla_a", "mla_b")[part]]
        with e.eng.Fori(0, 2) as i:
            for s in range(2):
                trip, c, per = i + 2 * part, c0 + 2 * s, len(mla_uses())
                weight_high(e, c + AHEAD, i)
                job_wait(e, c, i)
                act(b.qn[:, 0, :], bank_of(e, c)[:, :], ACT.Copy, scale=scale).then_inc(K.job_sems["bank"][c % SLOTS], 1)
                ring.wait(f"n1_{s}", trip)
                ring.read(f"n1_{s}", act(b.qn[:, 1, :], ring.bank(f"n1_{s}")[:, :], ACT.Copy, scale=scale))
                weight_high(e, c + 1 + AHEAD, i)
                use = f"v1_{s}"
                ring.wait(use, trip)
                ring.read(use, act(b.v[:, 1, :], ring.bank(use)[:, :], ACT.Copy))
                job_wait(e, c + 1, i)
                act(b.v[:, 0, :], bank_of(e, c + 1)[:, :], ACT.Copy).then_inc(K.job_sems["bank"][(c + 1) % SLOTS], 1)
                for what in MLA_ORDER[4:]:
                    if what[0] == "v":
                        continue
                    use, h, q = f"{what}_{s}", int(what[1]), int(what[-1])
                    if what[0] == "s":
                        e.eng.wait_ge(K.sem(f"mla_max{h}"), trip * 8 + s * 4 + q + 1)
                        if q >= 2:
                            ring.wait(f"t{h}{q - 2}_{s}", trip)
                        ring.read(use, act(b.p[h][q % 2], ring.bank(use)[:, :], ACT.Exp, bias=b.stat(b.mx, h, q),
                                           accum_out=b.stat(b.sum, h, q)))
                    elif what[0] == "t":
                        ring.wait(use, trip)
                        ring.read(use, act(b.pt[h][:, :, q * P:(q + 1) * P],
                                           ring.bank(use)[:, :].rearrange("p (a d) -> p a d", d=P), ACT.Copy))
                    else:
                        ring.wait(use, trip)
                        act(at(K.act_hi, i * 4 + 2 * s + h), ring.bank(use)[:, :], ACT.Copy) \
                            .then_inc(K.sem("split_high_done"), 1)
        ahead_act(e, out)
    post_act(e, "mla")


def mla_dve(e):
    K, b, v, st, c0 = e.K, mla_buffers(e.K), e.K.nc.vector, e.steps, FIRST_JOB["mla_in"]
    turn, key = Ring(e, "mla_rope", (4, 5, 6), ROPE_TURN), Ring(e, "mla_key", (4,), ["rot"])
    ring = Ring(e, "mla_aux", (4, 5, 6, 7), mla_uses())

    def step(ins):
        st.step(ins)
        st.wait()

    prenorm_dve(e, "mla", "pre_mix_norm_2", DT, c0)
    e.eng.sem_inc(K.sem("position_room"), 1)
    rope_angles(e, "mla_freq", b.cos, b.sin, ROPES_BEFORE)
    for r in (turn, key):
        r.begin()
    e.eng.wait_ge(K.sem("tables"), 2 * ROPES_BEFORE + 2)
    stat_vector(e, "mla_q")
    norm_split_vector(e, "mla_q", "mla_cq", K.M, "mla_q_norm_2", 0, 3, DT)
    stat_vector(e, "mla_kv")
    norm_split_vector(e, "mla_kv", "mla_ckv", K.M[:, 3:5, :], "mla_kv_norm_2", 0, 2, DT + 3)
    evacuated(e, c0 + 5)
    step(v.tensor_tensor(b.kr, b.k_raw, b.cos, ALU.mult))
    key.wait("rot", 0)
    key.read("rot", v.tensor_tensor(b.rot, key.bank("rot")[:, :], b.sin, ALU.mult))
    key.wait_read("rot", 0)
    step(v.tensor_tensor(b.kr, b.kr, b.rot, ALU.add))
    for k in range(4):
        for s in range(2):
            q, use = mla_turned(b, 2 * k + s), f"rot{s}"
            turn.wait(use, k)
            step(v.tensor_tensor(q, q, b.cos, ALU.mult))
            turn.read(use, v.tensor_tensor(b.rot, turn.bank(use)[:, :], b.sin, ALU.mult))
            turn.wait_read(use, k)
            step(v.tensor_tensor(q, q, b.rot, ALU.add))
    ring.begin()
    e.eng.sem_inc(K.sem("mla_begin"), 1)
    e.eng.sem_inc(K.sem("y_done"), 2 * DT)
    for part, out in ((0, "mla_outa"), (1, "mla_outb")):
        c0 = FIRST_JOB[("mla_a", "mla_b")[part]]
        with e.eng.Fori(0, 2) as i:
            st.enter(i, 2 * MLA_STEPS)
            for s in range(2):
                trip, c = i + 2 * part, c0 + 2 * s
                step(v.tensor_copy(b.qs, at(b.qr[part][s], i)))
                e.eng.sem_inc(K.sem("mla_staged"), 1)
                for what in MLA_VECTOR_ORDER:
                    use, h, q = f"{what}_{s}", int(what.strip("stovk")[0]), int(what[-1])
                    if what[0] == "k":
                        ring.wait(use, trip)
                        ring.read(use, v.tensor_copy(b.kn[:, h, :], ring.bank(use)[:, :]))
                    elif what[0] == "v":
                        ring.wait(use, trip)
                        ring.read(use, v.tensor_copy(b.v_tok[h], ring.bank(use)[:, :].rearrange("p (a d) -> p a d", d=P)))
                    elif what[0] == "s":
                        mx = b.stat(b.mx, h, q)
                        ring.wait(use, trip)
                        step(v.tensor_reduce(mx, ring.bank(use)[:, :], AX.X, ALU.max))
                        v.tensor_scalar(mx, mx, -1.0, None, ALU.mult).then_inc(K.sem(f"mla_max{h}"), 1)
                    elif what[0] == "t":
                        rec, p = b.stat(b.rec, h, q), b.p[h][q % 2]
                        ring.wait_read(f"s{h}{q}_{s}", trip)
                        step(v.reciprocal(rec, b.stat(b.sum, h, q)))
                        v.tensor_scalar(p, p, rec, None, ALU.mult).then_inc(K.sem(f"mla_p{h}"), 1)
                    else:
                        t = i * 4 + 2 * s + h
                        ring.wait(use, trip)
                        e.eng.wait_ge(K.sem("split_high_done"), t + part * DT + FIRST_SPLIT["mla_y"] + 1)
                        v.tensor_tensor(at(K.act_lo, t), ring.bank(use)[:, :], at(K.act_hi, t).bitcast(F32),
                                        ALU.subtract).then_inc(K.sem("split_done"), 1)
                        e.eng.wait_ge(K.sem("split_done"), t + part * DT + FIRST_SPLIT["mla_y"] + 1)
                        e.eng.sem_inc(ring.free[ring.find(use)[1]], 1)
            st.leave(2)
        out_m_dve(e, out, "mla", add=part == 1, before_end=(2 - part) * DT)
    post_dve(e, "mla", "post_mix_norm_2", DT)


MLA_STEPS = 17
ROPES_BEFORE = int("swa" in XSTEPS)


PROGRAM = {
    "conv": (conv_pe, conv_act, conv_dve),
    "fox": (fox_pe, fox_act, fox_dve),
    "gdn": (gdn_pe, gdn_act, gdn_dve),
    "swa": (swa_pe, swa_act, swa_dve),
    "final": (final_pe, final_act, final_dve),
    "hg": (hg_pe, hg_act, hg_dve),
    "mlp0": (lambda e: mlp_pe(e, "mlp0"), lambda e: mlp_act(e, "mlp0"), lambda e: mlp_dve(e, "mlp0", 0)),
    "ple0": (lambda e: ple_pe(e, "ple0"), lambda e: ple_act(e, "ple0", 0), lambda e: ple_dve(e, "ple0", 0)),
    "mla": (mla_pe, mla_act, mla_dve),
    "mlp1": (lambda e: mlp_pe(e, "mlp1"), lambda e: mlp_act(e, "mlp1"), lambda e: mlp_dve(e, "mlp1", 1)),
    "ple1": (lambda e: ple_pe(e, "ple1"), lambda e: ple_act(e, "ple1", 1), lambda e: ple_dve(e, "ple1", 1)),
}
STAGES = list(PROGRAM)


def chunked(w):
    n = w.shape[0] // P
    a = np.zeros((P, D), w.dtype)
    a[:, :n * P] = w.reshape(n, P, P).transpose(1, 0, 2).reshape(P, n * P)
    return a


def tiles_of(w, first, n=DT):
    return [chunked(w[:, first + k * P:first + (k + 1) * P]) for k in range(n)]


def wide(parts):
    a = np.zeros((parts[0][1].shape[0], P), parts[0][1].dtype)
    for place, w in parts:
        a[:, place:place + w.shape[1]] = w
    return a


def weight_jobs(w):
    jobs = []

    def per_head(m, parts, n=H8):
        return [chunked(m[:, q * D + h * P:q * D + (h + 1) * P]) for h in range(n) for q in parts]

    jobs += per_head(w["conv_w_in"][0], range(4)) + tiles_of(w["conv_w_out"][0], 0)
    fox = w["fox_w_in"][0]
    jobs += [chunked(wide([(0, fox[:, 4 * D:])]))] + per_head(fox, range(4)) + tiles_of(w["fox_w_out"][0], 0)
    gdn = w["gdn_w_in"][0]
    jobs += [chunked(wide([(0, gdn[:, 4 * D:4 * D + H8]), (32, gdn[:, 4 * D + H8:])]))]
    jobs += per_head(gdn, range(4)) + tiles_of(w["gdn_w_out"][0], 0)
    swa, swa_out, rows = w["swa_w_in"][0], w["swa_w_out"][0], []
    for p in range(2):
        jobs += [chunked(swa[:, D + p * P:D + (p + 1) * P]), chunked(swa[:, D + 256 + p * P:D + 256 + (p + 1) * P])]
        for g in range(4):
            two = np.concatenate([np.arange(64) + 64 * (4 * kv + g) for kv in (2 * p, 2 * p + 1)])
            jobs += [chunked(swa[:, two]), chunked(swa[:, D + 512 + two])]
            rows.append(two)
    jobs += tiles_of(swa_out[np.concatenate(rows)], 0)
    hg = w["hg_w_in_2"][0]
    jobs += per_head(hg, range(4)) + tiles_of(hg, 4 * D) + tiles_of(w["hg_w_out_2"][0], 0)

    def mlp(l):
        out = []
        for q in range(4):
            out += tiles_of(w["w_mlp_in_2"][l], q * D) + tiles_of(w["w_mlp_out_2"][l][q * D:(q + 1) * D], 0)
        return out

    def ple(l):
        proj = w["w_ple_proj_2"][l]
        return tiles_of(w["w_ple_gate_2"][l], 0) + [
            chunked(np.concatenate([proj[:, (4 * k + t) * P:(4 * k + t + 1) * P] for t in range(4)])) for k in range(2)]

    jobs += mlp(0) + ple(0)
    win, uq, ukv, wo = w["mla_w_in_2"][0], w["mla_w_uq_2"][0], w["mla_w_ukv_2"][0], w["mla_w_o_2"][0]
    jobs += tiles_of(win, 0, 5) + [chunked(wide([(0, win[:, 640:]), (64, win[:, 640:])]))]
    for k in range(4):
        jobs.append(chunked(np.concatenate(
            [np.concatenate([uq[:, (2 * t + s) * 192 + 128:(2 * t + s + 1) * 192] for s in range(2)], 1)
             for t in (2 * k, 2 * k + 1)])))
    for part in range(2):
        for t in range(4 * part, 4 * part + 4):
            jobs.append(chunked(np.concatenate([uq[:, h * 192:h * 192 + 128] for h in (2 * t, 2 * t + 1)])))
            jobs.append(chunked(np.concatenate([ukv[:, h * 256 + o:h * 256 + o + P]
                                                for o in (0, P) for h in (2 * t, 2 * t + 1)])))
        jobs += tiles_of(wo[part * D:(part + 1) * D], 0)
    jobs += mlp(1) + ple(1)
    assert len(jobs) == N_JOBS, (len(jobs), N_JOBS)
    jobs += [jobs[0]] * (PADDED_JOBS - N_JOBS)
    return np.stack(jobs)


def feature_columns(a):
    return np.ascontiguousarray(a.reshape(-1, P).T)


def parameter_block(w):
    parts = []
    for name, n in PARAMS:
        a = w[name]
        if name == "conv_w_conv":
            a = a[0].reshape(3, DT, P).transpose(1, 0, 2)
        if name == "gdn_w_conv":
            a = a[0].reshape(4, 3, H8, P).transpose(2, 1, 0, 3)
        a = feature_columns(a)
        assert a.shape[1] == n, (name, a.shape)
        parts.append(a)
    for name in HEAD_COLS:
        a = np.zeros((P, 1), np.float32)
        at_row = 0 if name == "fox_b_f" else 32
        a[at_row:at_row + H8, 0] = w[name][0]
        parts.append(a)
    return np.concatenate(parts, 1)


def kernel(**inputs):
    from concourse import bacc
    from concourse.bass_utils import run_bass_kernel_spmd

    w = {k: np.asarray(v) for k, v in inputs.items()}
    nc = bacc.Bacc("TRN2", target_bir_lowering=False, num_devices=1)
    arrays = {
        "weights": weight_jobs(w),
        "x_t": np.ascontiguousarray(w["x"][0].T),
        "p_t": np.ascontiguousarray(w["p_2"][:, 0].transpose(0, 2, 1)),
        "consts": np.concatenate(list(const_layout().values()), 1),
        "params": parameter_block(w),
        "positions": w["positions"], "positions_2": w["positions_2"], "sinks": w["swa_sinks"][0],
    }
    args = [nc.dram_tensor(k, a.shape, mybir.dt.from_np(a.dtype), kind="ExternalInput").ap() for k, a in arrays.items()]
    out = nc.dram_tensor("out_t", (D, S), F32, kind="ExternalOutput").ap()
    hybrid_stack(nc, *args, out)
    r = run_bass_kernel_spmd(nc, [arrays], core_ids=[0])
    return np.ascontiguousarray(np.asarray(r.results[0]["out_t"]).T)[None]
```
